# Optimizing a Trainium2 kernel written in Bass

```python
import math
import jax, jax.numpy as jnp
from jax import lax
import numpy as np

D_MODEL = 1024
BATCH = 1
SEQ = 256
DEPTH = 1

GRID_W = 64
CTX_LEN = 256
N_BRANCH = 3
D_BR = D_MODEL // 2
HY_ORDER = 2
HY_BANDS = 16
HY_POS_DIM = 1 + 2 * HY_BANDS
HY_FILTER_HID = 64
HY_DECAY_SLOW = 3.07
HY_DECAY_FAST = 15.35
FN_GROUPS = 4
FN_GROUP_W = D_BR // FN_GROUPS
ML_HEADS = 4
ML_HD = D_BR // ML_HEADS
ML_CHUNK = 128
ML_FGATE_LO = 3.0
ML_FGATE_HI = 6.0
P_HY = 3 * D_BR
P_FN = D_BR
P_ML = 4 * D_BR
P_MLG = 4 * ML_HEADS
P_GATE = N_BRANCH * D_MODEL
OFF_FN = P_HY
OFF_ML = OFF_FN + P_FN
OFF_MLG = OFF_ML + P_ML
OFF_GATE = OFF_MLG + P_MLG
P_TOT = OFF_GATE + P_GATE
MOE_GROUPS = 4
MOE_PER_GROUP = 4
MOE_EXPERTS = MOE_GROUPS * MOE_PER_GROUP
MOE_TOPK = 2
EXPERT_HID = D_MODEL // 4
EPS = 1e-6


def rmsnorm(x, w):
    xf = x.astype(jnp.float32)
    y = xf * lax.rsqrt(jnp.mean(xf * xf, axis=-1, keepdims=True) + EPS)
    return (y * w.astype(jnp.float32)).astype(x.dtype)

def modulate(h, shift, scale):
    return h * (1 + scale) + shift

def dwconv_grid(u, w, b, grid):
    B, L, C = u.shape
    rows, width = grid
    img = u.reshape(B, rows, width, C)
    out = lax.conv_general_dilated(img, w[:, :, None, :].astype(u.dtype), (1, 1), "SAME",
                                   dimension_numbers=("NHWC", "HWIO", "NHWC"),
                                   feature_group_count=C)
    return out.reshape(B, L, C) + b.astype(u.dtype)

def hyena_filter(L, lp):
    f32 = jnp.float32
    t = jnp.arange(L, dtype=f32) / L
    bands = jnp.linspace(1e-4, HY_BANDS - 1, HY_BANDS, dtype=f32)
    ang = (2 * math.pi) * t[:, None] * bands[None, :]
    feats = jnp.concatenate([t[:, None], jnp.cos(ang), jnp.sin(ang)], axis=-1)
    freq = lp["hy_f_freq"].astype(f32)
    h = jnp.sin(freq * (feats @ lp["hy_f_w1"].astype(f32) + lp["hy_f_b1"].astype(f32)))
    h = jnp.sin(freq * (h @ lp["hy_f_w2"].astype(f32) + lp["hy_f_b2"].astype(f32)))
    h = (h @ lp["hy_f_w3"].astype(f32)).reshape(L, HY_ORDER, 2, D_BR)
    h = h * jnp.exp(-t[:, None, None, None] * jnp.abs(lp["hy_decay"].astype(f32)))
    fwd, bwd = h[:, :, 0], h[:, :, 1]
    k = jnp.concatenate([fwd, jnp.zeros_like(fwd[:1]), jnp.flip(bwd[1:], axis=0)], axis=0)
    k = k * lax.rsqrt(jnp.sum(k * k, axis=0, keepdims=True) + EPS)
    return jnp.fft.rfft(k, axis=0)

def fft_longconv(u, kf, skip):
    L = u.shape[1]
    uf = jnp.fft.rfft(u, n=2 * L, axis=1)
    y = jnp.fft.irfft(uf * kf[None], n=2 * L, axis=1)[:, :L]
    return y + u * skip

def hyena_branch(zh, grid, lp):
    L = zh.shape[1]
    u = dwconv_grid(zh, lp["hy_conv_w"], lp["hy_conv_b"], grid).astype(jnp.float32)
    v, x1, x2 = jnp.split(u, 3, axis=-1)
    kf = hyena_filter(L, lp)
    skip = lp["hy_skip"].astype(jnp.float32)
    z = x1 * fft_longconv(v, kf[:, 0], skip[0])
    return x2 * fft_longconv(z, kf[:, 1], skip[1])

def fnet_branch(zf):
    B, L, _ = zf.shape
    u = zf.astype(jnp.float32).reshape(B, L, FN_GROUPS, FN_GROUP_W)
    y = jnp.fft.fft2(u, axes=(1, 3), norm="ortho").real
    return y.reshape(B, L, D_BR)

def zero_state(batch):
    f32 = jnp.float32
    return (jnp.zeros((batch, ML_HEADS, ML_HD, ML_HD), f32),
            jnp.zeros((batch, ML_HEADS, ML_HD), f32),
            jnp.zeros((batch, ML_HEADS), f32))

def mlstm_scan(q, k, v, i_pre, f_pre, state):
    B, H, L, d = q.shape
    T = ML_CHUNK
    nc = L // T

    def chunks(a):
        return jnp.moveaxis(a.reshape((B, H, nc, T) + a.shape[3:]), 2, 0)

    q = q * (d ** -0.5)
    logf = jax.nn.log_sigmoid(f_pre)
    mask = jnp.tril(jnp.ones((T, T), dtype=bool))

    def step(carry, inp):
        C, n, m = carry
        qc, kc, vc, ic, lfc = inp
        b = jnp.cumsum(lfc, axis=-1)
        Dm = jnp.where(mask, b[..., :, None] - b[..., None, :] + ic[..., None, :], -jnp.inf)
        inter = b + m[..., None]
        m_row = jnp.maximum(inter, jnp.max(Dm, axis=-1))
        w_intra = jnp.exp(Dm - m_row[..., None])
        w_inter = jnp.exp(inter - m_row)
        s = jnp.einsum("bhtk,bhsk->bhts", qc, kc) * w_intra
        num = jnp.einsum("bhts,bhsv->bhtv", s, vc) + w_inter[..., None] * jnp.einsum("bhvk,bhtk->bhtv", C, qc)
        den = jnp.sum(s, axis=-1) + w_inter * jnp.einsum("bhk,bhtk->bht", n, qc)
        den = jnp.maximum(jnp.abs(den), jnp.exp(-m_row))
        h = num / den[..., None]
        bT = b[..., -1]
        a = bT[..., None] - b + ic
        m_new = jnp.maximum(bT + m, jnp.max(a, axis=-1))
        sc = jnp.exp(a - m_new[..., None])
        decay = jnp.exp(bT + m - m_new)
        C_new = decay[..., None, None] * C + jnp.einsum("bhs,bhsv,bhsk->bhvk", sc, vc, kc)
        n_new = decay[..., None] * n + jnp.einsum("bhs,bhsk->bhk", sc, kc)
        return (C_new, n_new, m_new), h

    state, h = lax.scan(step, state, (chunks(q), chunks(k), chunks(v), chunks(i_pre), chunks(logf)))
    return jnp.moveaxis(h, 0, 2).reshape(B, H, L, d), state

def mlstm_branch(zm, zg, grid, lp, state_f, state_b):
    B, L, _ = zm.shape
    qk = jax.nn.silu(dwconv_grid(zm[..., :2 * D_BR], lp["ml_conv_w"], lp["ml_conv_b"], grid))
    v = zm[..., 2 * D_BR:3 * D_BR]
    o = zm[..., 3 * D_BR:]

    def heads(a):
        return a.reshape(B, L, ML_HEADS, ML_HD).transpose(0, 2, 1, 3).astype(jnp.float32)

    q, k, v = heads(qk[..., :D_BR]), heads(qk[..., D_BR:]), heads(v)
    g = zg.astype(jnp.float32).reshape(B, L, 4, ML_HEADS).transpose(2, 0, 3, 1)
    h_f, st_f = mlstm_scan(q, k, v, g[0], g[1], state_f)
    rev = lambda a: jnp.flip(a, axis=2)
    h_b, st_b = mlstm_scan(rev(q), rev(k), rev(v), rev(g[2]), rev(g[3]), state_b)
    h = h_f + rev(h_b)
    h = h * lax.rsqrt(jnp.mean(h * h, axis=-1, keepdims=True) + EPS)
    h = h.transpose(0, 2, 1, 3).reshape(B, L, D_BR) * lp["ml_norm_w"].astype(jnp.float32)
    return jax.nn.sigmoid(o.astype(jnp.float32)) * h, st_f, st_b

def merge_branches(y_hy, y_fn, y_ml, gate_pre, lp):
    B, L, _ = gate_pre.shape
    dt = gate_pre.dtype
    ys = jnp.stack([y_hy, y_fn, y_ml], axis=2).astype(dt)
    proj = jnp.einsum("blkc,kcd->blkd", ys, lp["w_branch"])
    g = jax.nn.sigmoid(gate_pre.astype(jnp.float32)).reshape(B, L, N_BRANCH, D_MODEL).astype(dt)
    return jnp.sum(g * proj, axis=2) @ lp["w_out"]

def token_mixer_out(z, grid, lp, ml_out):
    y_hy = hyena_branch(z[..., :OFF_FN], grid, lp)
    y_fn = fnet_branch(z[..., OFF_FN:OFF_ML])
    return merge_branches(y_hy, y_fn, ml_out, z[..., OFF_GATE:], lp)

def hier_moe(h, lp):
    B, L, D = h.shape
    t = h.reshape(B * L, D)
    g_logits = (t @ lp["moe_rg_w"] + lp["moe_rg_b"]).astype(jnp.float32)
    p_top, g_sel = lax.top_k(jax.nn.softmax(g_logits, axis=-1), 1)
    e_logits = (t @ lp["moe_re_w"] + lp["moe_re_b"]).astype(jnp.float32).reshape(B * L, MOE_GROUPS, MOE_PER_GROUP)
    g_onehot = jax.nn.one_hot(g_sel[:, 0], MOE_GROUPS, dtype=jnp.float32)
    e_in_group = jnp.sum(e_logits * g_onehot[:, :, None], axis=1)
    e_top, e_sel = lax.top_k(e_in_group, MOE_TOPK)
    w_sel = p_top * jax.nn.softmax(e_top, axis=-1)
    e_idx = g_sel * MOE_PER_GROUP + e_sel
    combine = jnp.sum(jax.nn.one_hot(e_idx, MOE_EXPERTS, dtype=jnp.float32) * w_sel[..., None], axis=1)
    hg = jnp.einsum("nd,edh->neh", t, lp["moe_w_gate"])
    hu = jnp.einsum("nd,edh->neh", t, lp["moe_w_up"])
    a = jax.nn.silu(hg) * hu * combine[..., None].astype(t.dtype)
    return jnp.einsum("neh,ehd->nd", a, lp["moe_w_down"]).reshape(B, L, D)

def first_inputs(seed: int = 0) -> dict:
    key = jax.random.key(seed)
    ks = iter(jax.random.split(key, 40))
    f32 = jnp.float32

    def nrm(shape, scale):
        return jax.random.normal(next(ks), shape, f32) * scale

    x = nrm((BATCH, SEQ, D_MODEL), 1.0)
    c = nrm((BATCH, D_MODEL), 1.0)
    ctx = nrm((BATCH, CTX_LEN, D_MODEL), 1.0)
    c_ctx = nrm((D_MODEL,), 1.0)
    ada_w = nrm((DEPTH, D_MODEL, 6 * D_MODEL), 0.5 * D_MODEL ** -0.5)
    ada_b = nrm((DEPTH, 6 * D_MODEL), 0.02)
    norm1_w = 1.0 + nrm((DEPTH, D_MODEL), 0.02)
    norm2_w = 1.0 + nrm((DEPTH, D_MODEL), 0.02)
    w_in = nrm((DEPTH, D_MODEL, P_TOT), D_MODEL ** -0.5)
    lin = jnp.linspace(ML_FGATE_LO, ML_FGATE_HI, ML_HEADS, dtype=f32)
    zh = jnp.zeros((ML_HEADS,), f32)
    fbias = jnp.concatenate([zh, lin, zh, lin])
    b_in = nrm((DEPTH, P_TOT), 0.02).at[:, OFF_MLG:OFF_GATE].add(fbias)
    hy_conv_w = nrm((DEPTH, 3, 3, P_HY), 1.0 / 3.0)
    hy_conv_b = nrm((DEPTH, P_HY), 0.02)
    hy_f_w1 = nrm((DEPTH, HY_POS_DIM, HY_FILTER_HID), HY_POS_DIM ** -0.5)
    hy_f_b1 = nrm((DEPTH, HY_FILTER_HID), 0.02)
    hy_f_w2 = nrm((DEPTH, HY_FILTER_HID, HY_FILTER_HID), HY_FILTER_HID ** -0.5)
    hy_f_b2 = nrm((DEPTH, HY_FILTER_HID), 0.02)
    hy_f_w3 = nrm((DEPTH, HY_FILTER_HID, HY_ORDER * 2 * D_BR), HY_FILTER_HID ** -0.5)
    hy_f_freq = 1.0 + nrm((DEPTH, HY_FILTER_HID), 0.02)
    decay_base = jnp.linspace(HY_DECAY_SLOW, HY_DECAY_FAST, D_BR, dtype=f32)
    hy_decay = decay_base[None, None, None, :] + nrm((DEPTH, HY_ORDER, 2, D_BR), 0.1)
    hy_skip = nrm((DEPTH, HY_ORDER, D_BR), 0.5)
    ml_conv_w = nrm((DEPTH, 3, 3, 2 * D_BR), 1.0 / 3.0)
    ml_conv_b = nrm((DEPTH, 2 * D_BR), 0.02)
    ml_norm_w = 1.0 + nrm((DEPTH, D_BR), 0.02)
    w_branch = nrm((DEPTH, N_BRANCH, D_BR, D_MODEL), D_BR ** -0.5)
    w_out = nrm((DEPTH, D_MODEL, D_MODEL), D_MODEL ** -0.5)
    moe_rg_w = nrm((DEPTH, D_MODEL, MOE_GROUPS), D_MODEL ** -0.5)
    moe_rg_b = nrm((DEPTH, MOE_GROUPS), 0.01)
    moe_re_w = nrm((DEPTH, D_MODEL, MOE_EXPERTS), D_MODEL ** -0.5)
    moe_re_b = nrm((DEPTH, MOE_EXPERTS), 0.01)
    moe_w_gate = nrm((DEPTH, MOE_EXPERTS, D_MODEL, EXPERT_HID), D_MODEL ** -0.5)
    moe_w_up = nrm((DEPTH, MOE_EXPERTS, D_MODEL, EXPERT_HID), D_MODEL ** -0.5)
    moe_w_down = nrm((DEPTH, MOE_EXPERTS, EXPERT_HID, D_MODEL), EXPERT_HID ** -0.5)
    norm_f_w = 1.0 + nrm((D_MODEL,), 0.02)
    return {"x": x, "c": c, "ctx": ctx, "c_ctx": c_ctx, "ada_w": ada_w, "ada_b": ada_b,
            "norm1_w": norm1_w, "norm2_w": norm2_w, "w_in": w_in, "b_in": b_in,
            "hy_conv_w": hy_conv_w, "hy_conv_b": hy_conv_b, "hy_f_w1": hy_f_w1, "hy_f_b1": hy_f_b1,
            "hy_f_w2": hy_f_w2, "hy_f_b2": hy_f_b2, "hy_f_w3": hy_f_w3, "hy_f_freq": hy_f_freq,
            "hy_decay": hy_decay, "hy_skip": hy_skip, "ml_conv_w": ml_conv_w, "ml_conv_b": ml_conv_b,
            "ml_norm_w": ml_norm_w, "w_branch": w_branch, "w_out": w_out,
            "moe_rg_w": moe_rg_w, "moe_rg_b": moe_rg_b, "moe_re_w": moe_re_w, "moe_re_b": moe_re_b,
            "moe_w_gate": moe_w_gate, "moe_w_up": moe_w_up, "moe_w_down": moe_w_down,
            "norm_f_w": norm_f_w}

def first_block(x, c, ctx, c_ctx, ada_w, ada_b, norm1_w, norm2_w, w_in, b_in,
              hy_conv_w, hy_conv_b, hy_f_w1, hy_f_b1, hy_f_w2, hy_f_b2, hy_f_w3, hy_f_freq,
              hy_decay, hy_skip, ml_conv_w, ml_conv_b, ml_norm_w, w_branch, w_out,
              moe_rg_w, moe_rg_b, moe_re_w, moe_re_b, moe_w_gate, moe_w_up, moe_w_down,
              norm_f_w):
    B = x.shape[0]
    rows = x.shape[1] // GRID_W
    lat_grid = (rows, GRID_W)
    ctx_grid = (1, ctx.shape[1])
    for l in range(DEPTH):
        lp = {"hy_conv_w": hy_conv_w[l], "hy_conv_b": hy_conv_b[l], "hy_f_w1": hy_f_w1[l],
              "hy_f_b1": hy_f_b1[l], "hy_f_w2": hy_f_w2[l], "hy_f_b2": hy_f_b2[l],
              "hy_f_w3": hy_f_w3[l], "hy_f_freq": hy_f_freq[l], "hy_decay": hy_decay[l],
              "hy_skip": hy_skip[l], "ml_conv_w": ml_conv_w[l], "ml_conv_b": ml_conv_b[l],
              "ml_norm_w": ml_norm_w[l], "w_branch": w_branch[l], "w_out": w_out[l],
              "moe_rg_w": moe_rg_w[l], "moe_rg_b": moe_rg_b[l], "moe_re_w": moe_re_w[l],
              "moe_re_b": moe_re_b[l], "moe_w_gate": moe_w_gate[l], "moe_w_up": moe_w_up[l],
              "moe_w_down": moe_w_down[l]}
        last = l == DEPTH - 1
        mod_l = jnp.split((jax.nn.silu(c) @ ada_w[l] + ada_b[l])[:, None, :], 6, axis=-1)
        mod_c = jnp.split((jax.nn.silu(c_ctx) @ ada_w[l] + ada_b[l])[None, None, :], 6, axis=-1)
        zc = modulate(rmsnorm(ctx, norm1_w[l]), mod_c[0], mod_c[1]) @ w_in[l] + b_in[l]
        zl = modulate(rmsnorm(x, norm1_w[l]), mod_l[0], mod_l[1]) @ w_in[l] + b_in[l]
        st0 = zero_state(B)
        ml_c, st_f, st_b = mlstm_branch(zc[..., OFF_ML:OFF_MLG], zc[..., OFF_MLG:OFF_GATE], ctx_grid, lp, st0, st0)
        ml_l, _, _ = mlstm_branch(zl[..., OFF_ML:OFF_MLG], zl[..., OFF_MLG:OFF_GATE], lat_grid, lp, st_f, st_b)
        x = x + mod_l[2] * token_mixer_out(zl, lat_grid, lp, ml_l)
        x = x + mod_l[5] * hier_moe(modulate(rmsnorm(x, norm2_w[l]), mod_l[3], mod_l[4]), lp)
        if not last:
            ctx = ctx + mod_c[2] * token_mixer_out(zc, ctx_grid, lp, ml_c)
            ctx = ctx + mod_c[5] * hier_moe(modulate(rmsnorm(ctx, norm2_w[l]), mod_c[3], mod_c[4]), lp)
    return rmsnorm(x, norm_f_w)


DEPTH_2 = 2

HEAD_DIM = 64
D_MIX = D_MODEL
A_HEADS = (3 * D_MIX) // (8 * HEAD_DIM)
A_WIDTH = A_HEADS * HEAD_DIM
IDX_HEADS = 4
IDX_DIM = HEAD_DIM
DSA_TOPK_MAX = 256
B_HEADS = D_MIX // (4 * HEAD_DIM)
B_QK_DIM = HEAD_DIM // 2
B_WIDTH = B_HEADS * HEAD_DIM
SUBLN_EPS = 1e-5
C_HEADS = A_HEADS
C_WIDTH = C_HEADS * HEAD_DIM
MOBA_BLOCK = 256
MOBA_TOPK = 3
ROPE_THETA = 500000.0
ROPE_FRACTION = 4
MAX_POS_OFFSET = 1024
Q_BLOCK = 128
MOBA_Q_BLOCK = 32
D_FF = 2816
N_EXPERTS = 8
TOP_K_EXPERTS = 2
D_FF_EXPERT = 2816
IN_COLS = (A_WIDTH, HEAD_DIM, HEAD_DIM, IDX_HEADS * IDX_DIM, IDX_DIM, IDX_HEADS,
           2 * B_HEADS * B_QK_DIM, 2 * B_HEADS * B_QK_DIM, B_WIDTH,
           C_WIDTH, C_WIDTH, C_WIDTH)
D_IN = sum(IN_COLS)


F32 = jnp.float32

def _split_points():
    pts, acc = [], 0
    for w in IN_COLS[:-1]:
        acc += w
        pts.append(acc)
    return pts

def rms_norm(x, g, eps=EPS):
    xf = x.astype(F32)
    y = xf * lax.rsqrt(jnp.mean(xf * xf, axis=-1, keepdims=True) + eps)
    return (y * g.astype(F32)).astype(x.dtype)

def rope_tables(positions, dim):
    rot = dim // ROPE_FRACTION
    inv = 1.0 / (ROPE_THETA ** (np.arange(0, rot, 2, dtype=np.float32) / rot))
    ang = positions.astype(F32)[..., None] * jnp.asarray(inv, F32)
    return jnp.cos(ang), jnp.sin(ang)

def partial_rope(x, cos, sin):
    half = cos.shape[-1]
    xf = x.astype(F32)
    x1, x2, xp = xf[..., :half], xf[..., half:2 * half], xf[..., 2 * half:]
    c, s = cos[:, :, None, :], sin[:, :, None, :]
    return jnp.concatenate([x1 * c - x2 * s, x2 * c + x1 * s, xp], axis=-1).astype(x.dtype)

def dsa_attention(q, k, v, q_idx, k_idx, w_idx):
    B, S, H, dh = q.shape
    k_top = min(DSA_TOPK_MAX, S // 4)
    key_pos = jnp.arange(S)
    kf_idx = k_idx.astype(F32)
    gather = jax.vmap(lambda zz, ii: zz[ii])

    def one_block(i):
        t0 = i * Q_BLOCK
        t = t0 + jnp.arange(Q_BLOCK)
        qb = lax.dynamic_slice_in_dim(q, t0, Q_BLOCK, axis=1).astype(F32)
        qib = lax.dynamic_slice_in_dim(q_idx, t0, Q_BLOCK, axis=1).astype(F32)
        wb = lax.dynamic_slice_in_dim(w_idx, t0, Q_BLOCK, axis=1).astype(F32) * IDX_HEADS ** -0.5
        rel = jax.nn.relu(jnp.einsum('bqhd,bsd->bqhs', qib, kf_idx) * IDX_DIM ** -0.5)
        score_idx = jnp.einsum('bqh,bqhs->bqs', wb, rel)
        causal = key_pos[None, :] <= t[:, None]
        score_idx = jnp.where(causal[None], score_idx, -jnp.inf)
        _, sel = lax.top_k(score_idx, k_top)
        valid = sel <= t[None, :, None]
        kg = gather(k, sel).astype(F32)
        vg = gather(v, sel).astype(F32)
        s = jnp.einsum('bqhd,bqkd->bqhk', qb, kg) * dh ** -0.5
        s = jnp.where(valid[:, :, None, :], s, -jnp.inf)
        p = jax.nn.softmax(s, axis=-1)
        return jnp.einsum('bqhk,bqkd->bqhd', p, vg).astype(q.dtype)

    out = lax.map(one_block, jnp.arange(S // Q_BLOCK))
    return jnp.moveaxis(out, 0, 1).reshape(B, S, H * dh)

def diff_attention(q, k, v, lam, g_sub, lam_init):
    B, S, H, _, dq = q.shape
    dv = v.shape[-1]
    key_pos = jnp.arange(S)
    kf = k.astype(F32)
    vf = v.astype(F32)

    def one_block(i):
        t0 = i * Q_BLOCK
        t = t0 + jnp.arange(Q_BLOCK)
        qb = lax.dynamic_slice_in_dim(q, t0, Q_BLOCK, axis=1).astype(F32)
        s = jnp.einsum('bqhcd,bshcd->bhcqs', qb, kf) * dq ** -0.5
        causal = key_pos[None, :] <= t[:, None]
        p = jax.nn.softmax(jnp.where(causal, s, -jnp.inf), axis=-1)
        a = p[:, :, 0] - lam * p[:, :, 1]
        return jnp.einsum('bhqs,bshd->bqhd', a, vf)

    o = lax.map(one_block, jnp.arange(S // Q_BLOCK))
    o = jnp.moveaxis(o, 0, 1).reshape(B, S, H, dv)
    o = rms_norm(o, g_sub, SUBLN_EPS) * (1.0 - lam_init)
    return o.reshape(B, S, H * dv).astype(v.dtype)

def moba_attention(q, k, v):
    B, S, H, dh = q.shape
    nb = -(-S // MOBA_BLOCK)
    n_sel = min(MOBA_TOPK, nb - 1)
    pad = nb * MOBA_BLOCK - S

    def to_blocks(z):
        z = jnp.pad(z, ((0, 0), (0, pad), (0, 0), (0, 0)))
        return z.reshape(B, nb, MOBA_BLOCK, H, dh).transpose(0, 3, 1, 2, 4)

    kb = to_blocks(k)
    vb = to_blocks(v)
    k_mean = jnp.mean(kb.astype(F32), axis=3)
    qh = q.transpose(0, 2, 1, 3)
    scale = dh ** -0.5
    in_block = jnp.arange(MOBA_BLOCK)
    gather = jax.vmap(jax.vmap(lambda zz, ii: zz[ii]))

    def one_block(i):
        t0 = i * MOBA_Q_BLOCK
        t = t0 + jnp.arange(MOBA_Q_BLOCK)
        own = t0 // MOBA_BLOCK
        qb = lax.dynamic_slice_in_dim(qh, t0, MOBA_Q_BLOCK, axis=2).astype(F32)
        k_own = lax.dynamic_index_in_dim(kb, own, axis=2, keepdims=False).astype(F32)
        v_own = lax.dynamic_index_in_dim(vb, own, axis=2, keepdims=False).astype(F32)
        s_own = jnp.einsum('bhqd,bhkd->bhqk', qb, k_own) * scale
        s_own = jnp.where((own * MOBA_BLOCK + in_block)[None, :] <= t[:, None], s_own, -jnp.inf)
        if n_sel == 0:
            p_own = jax.nn.softmax(s_own, axis=-1)
            return jnp.einsum('bhqk,bhkd->bhqd', p_own, v_own).astype(q.dtype)
        n_past = t // MOBA_BLOCK
        gate = jnp.einsum('bhqd,bhnd->bhqn', qb, k_mean)
        gate = jnp.where(jnp.arange(nb)[None, :] < n_past[:, None], gate, -jnp.inf)
        _, sel = lax.top_k(gate, n_sel)
        kg = gather(kb, sel).astype(F32)
        vg = gather(vb, sel).astype(F32)
        s_sel = jnp.einsum('bhqd,bhqnkd->bhqnk', qb, kg) * scale
        sel_ok = jnp.arange(n_sel)[None, :] < n_past[:, None]
        s_sel = jnp.where(sel_ok[None, None, :, :, None], s_sel, -jnp.inf)
        n_keys = n_sel * MOBA_BLOCK
        s_all = jnp.concatenate([s_sel.reshape(B, H, MOBA_Q_BLOCK, n_keys), s_own], axis=-1)
        p = jax.nn.softmax(s_all, axis=-1)
        p_sel = p[..., :n_keys].reshape(B, H, MOBA_Q_BLOCK, n_sel, MOBA_BLOCK)
        p_own = p[..., n_keys:]
        o = jnp.einsum('bhqnk,bhqnkd->bhqd', p_sel, vg) + jnp.einsum('bhqk,bhkd->bhqd', p_own, v_own)
        return o.astype(q.dtype)

    out = lax.map(one_block, jnp.arange(S // MOBA_Q_BLOCK))
    return out.transpose(1, 0, 3, 2, 4).reshape(B, S, H * dh)

def hybrid_mixer(h, cos64, sin64, cos32, sin32, w_in, w_out, lam_vec, g_sub, lam_init):
    B, S, _ = h.shape
    proj = jnp.einsum('bsd,dn->bsn', h, w_in)
    (q_a, k_a, v_a, q_i, k_i, w_i, q_b, k_b, v_b, q_c, k_c, v_c) = jnp.split(proj, _split_points(), axis=-1)
    q_a = partial_rope(q_a.reshape(B, S, A_HEADS, HEAD_DIM), cos64, sin64)
    k_a = partial_rope(k_a.reshape(B, S, 1, HEAD_DIM), cos64, sin64)[:, :, 0]
    q_i = partial_rope(q_i.reshape(B, S, IDX_HEADS, IDX_DIM), cos64, sin64)
    k_i = partial_rope(k_i.reshape(B, S, 1, IDX_DIM), cos64, sin64)[:, :, 0]
    y_a = dsa_attention(q_a, k_a, v_a, q_i, k_i, w_i)
    q_b = partial_rope(q_b.reshape(B, S, 2 * B_HEADS, B_QK_DIM), cos32, sin32).reshape(B, S, B_HEADS, 2, B_QK_DIM)
    k_b = partial_rope(k_b.reshape(B, S, 2 * B_HEADS, B_QK_DIM), cos32, sin32).reshape(B, S, B_HEADS, 2, B_QK_DIM)
    v_b = v_b.reshape(B, S, B_HEADS, HEAD_DIM)
    lf = lam_vec.astype(F32)
    lam = jnp.exp(jnp.sum(lf[0] * lf[1])) - jnp.exp(jnp.sum(lf[2] * lf[3])) + lam_init
    y_b = diff_attention(q_b, k_b, v_b, lam, g_sub, lam_init)
    q_c = partial_rope(q_c.reshape(B, S, C_HEADS, HEAD_DIM), cos64, sin64)
    k_c = partial_rope(k_c.reshape(B, S, C_HEADS, HEAD_DIM), cos64, sin64)
    y_c = moba_attention(q_c, k_c, v_c.reshape(B, S, C_HEADS, HEAD_DIM))
    y = jnp.concatenate([y_a, y_b, y_c], axis=-1)
    return jnp.einsum('bsm,md->bsd', y, w_out)

def swiglu(h, w_gate, w_up, w_down):
    a = jnp.einsum('bsd,df->bsf', h, w_gate)
    u = jnp.einsum('bsd,df->bsf', h, w_up)
    return jnp.einsum('bsf,fd->bsd', jax.nn.silu(a) * u, w_down)

def moe_swiglu(h, w_router, w_gate, w_up, w_down):
    logits = jnp.einsum('bsd,de->bse', h.astype(F32), w_router.astype(F32))
    top_val, top_idx = lax.top_k(logits, TOP_K_EXPERTS)
    top_w = jax.nn.softmax(top_val, axis=-1)
    combine = jnp.sum(jax.nn.one_hot(top_idx, N_EXPERTS, dtype=F32) * top_w[..., None], axis=-2)
    out = jnp.zeros_like(h)
    for e in range(N_EXPERTS):
        out = out + combine[..., e:e + 1].astype(h.dtype) * swiglu(h, w_gate[e], w_up[e], w_down[e])
    return out

def second_inputs(seed: int = 0) -> dict:
    key = jax.random.key(seed)
    ks = jax.random.split(key, 20)
    n_dense = (DEPTH_2 + 1) // 2
    n_moe = DEPTH_2 // 2

    def nrm(k, shape, scale):
        return jax.random.normal(k, shape, F32) * scale

    x = nrm(ks[0], (BATCH, SEQ, D_MODEL), 1.0)
    c = nrm(ks[1], (BATCH, D_MODEL), 1.0)
    offset = jax.random.randint(ks[2], (BATCH, 1), 0, MAX_POS_OFFSET, dtype=jnp.int32)
    positions = offset + jnp.arange(SEQ, dtype=jnp.int32)[None, :]
    w_in = nrm(ks[3], (DEPTH_2, D_MODEL, D_IN), D_MODEL ** -0.5)
    w_out = nrm(ks[4], (DEPTH_2, D_MIX, D_MODEL), D_MIX ** -0.5)
    diff_lambda = nrm(ks[5], (DEPTH_2, 4, B_QK_DIM), 0.1)
    diff_subln = 1.0 + nrm(ks[6], (DEPTH_2, HEAD_DIM), 0.01)
    w_ada = nrm(ks[7], (DEPTH_2, D_MODEL, 6 * D_MODEL), 0.5 * D_MODEL ** -0.5)
    b_ada = nrm(ks[8], (DEPTH_2, 6 * D_MODEL), 0.01)
    g_attn = 1.0 + nrm(ks[9], (DEPTH_2, D_MODEL), 0.01)
    g_ffn = 1.0 + nrm(ks[10], (DEPTH_2, D_MODEL), 0.01)
    w_ff_gate = nrm(ks[11], (n_dense, D_MODEL, D_FF), D_MODEL ** -0.5)
    w_ff_up = nrm(ks[12], (n_dense, D_MODEL, D_FF), D_MODEL ** -0.5)
    w_ff_down = nrm(ks[13], (n_dense, D_FF, D_MODEL), D_FF ** -0.5)
    w_router = nrm(ks[14], (n_moe, D_MODEL, N_EXPERTS), D_MODEL ** -0.5)
    w_exp_gate = nrm(ks[15], (n_moe, N_EXPERTS, D_MODEL, D_FF_EXPERT), D_MODEL ** -0.5)
    w_exp_up = nrm(ks[16], (n_moe, N_EXPERTS, D_MODEL, D_FF_EXPERT), D_MODEL ** -0.5)
    w_exp_down = nrm(ks[17], (n_moe, N_EXPERTS, D_FF_EXPERT, D_MODEL), D_FF_EXPERT ** -0.5)
    g_final = 1.0 + nrm(ks[18], (D_MODEL,), 0.01)
    return {'x': x, 'c': c, 'positions': positions, 'w_in': w_in, 'w_out': w_out,
            'diff_lambda': diff_lambda, 'diff_subln': diff_subln, 'w_ada': w_ada, 'b_ada': b_ada,
            'g_attn': g_attn, 'g_ffn': g_ffn, 'w_ff_gate': w_ff_gate, 'w_ff_up': w_ff_up,
            'w_ff_down': w_ff_down, 'w_router': w_router, 'w_exp_gate': w_exp_gate,
            'w_exp_up': w_exp_up, 'w_exp_down': w_exp_down, 'g_final': g_final}

def second_block(x, c, positions, w_in, w_out, diff_lambda, diff_subln, w_ada, b_ada,
              g_attn, g_ffn, w_ff_gate, w_ff_up, w_ff_down, w_router, w_exp_gate,
              w_exp_up, w_exp_down, g_final):
    cos64, sin64 = rope_tables(positions, HEAD_DIM)
    cos32, sin32 = rope_tables(positions, B_QK_DIM)
    c_act = jax.nn.silu(c)
    for layer in range(DEPTH_2):
        mod = jnp.einsum('bd,dn->bn', c_act, w_ada[layer]) + b_ada[layer]
        sh1, sc1, gt1, sh2, sc2, gt2 = [m[:, None, :] for m in jnp.split(mod, 6, axis=-1)]
        lam_init = 0.8 - 0.6 * math.exp(-0.3 * layer)
        h = rms_norm(x, g_attn[layer]) * (1.0 + sc1) + sh1
        y = hybrid_mixer(h, cos64, sin64, cos32, sin32, w_in[layer], w_out[layer],
                         diff_lambda[layer], diff_subln[layer], lam_init)
        x = x + gt1 * y
        h = rms_norm(x, g_ffn[layer]) * (1.0 + sc2) + sh2
        j = layer // 2
        if layer % 2 == 0:
            f = swiglu(h, w_ff_gate[j], w_ff_up[j], w_ff_down[j])
        else:
            f = moe_swiglu(h, w_router[j], w_exp_gate[j], w_exp_up[j], w_exp_down[j])
        x = x + gt2 * f
    return rms_norm(x, g_final)


def setup_inputs(seed=0):
    out = dict(first_inputs(seed))
    for name, value in second_inputs(seed + 1).items():
        if name != "x":
            out[name + "_2"] = value
    return out


def reference(
    x, c, ctx, c_ctx, ada_w, ada_b, norm1_w, norm2_w, w_in, b_in, hy_conv_w, hy_conv_b, hy_f_w1,
    hy_f_b1, hy_f_w2, hy_f_b2, hy_f_w3, hy_f_freq, hy_decay, hy_skip, ml_conv_w, ml_conv_b,
    ml_norm_w, w_branch, w_out, moe_rg_w, moe_rg_b, moe_re_w, moe_re_b, moe_w_gate, moe_w_up,
    moe_w_down, norm_f_w, c_2, positions_2, w_in_2, w_out_2, diff_lambda_2, diff_subln_2,
    w_ada_2, b_ada_2, g_attn_2, g_ffn_2, w_ff_gate_2, w_ff_up_2, w_ff_down_2, w_router_2,
    w_exp_gate_2, w_exp_up_2, w_exp_down_2, g_final_2,
):
    x = first_block(
        x, c, ctx, c_ctx, ada_w, ada_b, norm1_w, norm2_w, w_in, b_in, hy_conv_w, hy_conv_b,
        hy_f_w1, hy_f_b1, hy_f_w2, hy_f_b2, hy_f_w3, hy_f_freq, hy_decay, hy_skip, ml_conv_w,
        ml_conv_b, ml_norm_w, w_branch, w_out, moe_rg_w, moe_rg_b, moe_re_w, moe_re_b,
        moe_w_gate, moe_w_up, moe_w_down, norm_f_w,
    )
    return second_block(
        x, c_2, positions_2, w_in_2, w_out_2, diff_lambda_2, diff_subln_2, w_ada_2, b_ada_2,
        g_attn_2, g_ffn_2, w_ff_gate_2, w_ff_up_2, w_ff_down_2, w_router_2, w_exp_gate_2,
        w_exp_up_2, w_exp_down_2, g_final_2,
    )


_drawn_inputs = setup_inputs


def setup_inputs(seed=0):
    import zlib

    import numpy as np

    out = dict(_drawn_inputs(seed))
    spreads = {}
    factors = {'norm1_w': 3.059,
     'norm2_w': 5.322,
     'hy_f_freq': 3.845,
     'ml_conv_b': 8.0,
     'ml_norm_w': 5.69,
     'moe_rg_b': 8.0,
     'moe_re_b': 8.0,
     'diff_lambda_2': 3.7,
     'diff_subln_2': 8.0,
     'g_attn_2': 6.464,
     'g_ffn_2': 5.451,
     'g_final_2': 5.578}
    for name, (base, spread) in spreads.items():
        noise = np.random.default_rng([zlib.crc32(name.encode()), seed]).standard_normal(out[name].shape)
        drawn = base * np.exp(spread * noise) if base else spread * noise
        out[name] = __import__('jax').numpy.asarray(drawn.astype(out[name].dtype))
    for name, factor in factors.items():
        out[name] = (out[name] * factor).astype(out[name].dtype)
    return out
```

```python
import math
from contextlib import ExitStack

import concourse.bass as bass
import numpy as np
from concourse import mybir

F32 = mybir.dt.float32
I32 = mybir.dt.int32
ALU = mybir.AluOpType
ACT = mybir.ActivationFunctionType
AX = mybir.AxisListType

P = 128
T = 256
NT = T // P
D = 1024
KD = D // P
DBR = D // 2
NBR = DBR // P
NH = 4
GW, GR = 64, T // 64
ML0 = 3 * DBR + DBR
MLG0 = ML0 + 4 * DBR
GATE0 = MLG0 + 16
E1, E1H = 16, D // 4
FF = 2816
CH = 256
NCH = FF // CH
E2 = 8
A_H, B_H, C_H, HD = 6, 4, 6, 64
O_QA, O_KA, O_VA, O_QI, O_KI, O_WI = 0, 384, 448, 512, 768, 832
O_QB, O_KB, O_VB, O_QC, O_KC, O_VC, D_IN = 836, 1092, 1348, 1604, 1988, 2372, 2756
TOPK = T // 4
EPS, SUB_EPS = 1e-6, 1e-5
MASKED = -1e30
TAKEN = -3e38
ROUND = 12582912.0
TWO_PI = (6.28125, 0.0019350051879882812, 3.019916150957033e-07)
PI = 3.1415925

NS = 3
SLOT = 6144

CONST = {}
_at = 0
for _n, _w in (("ident", P), ("ones", P), ("feats", T), ("cs", NT * T), ("ss", NT * T), ("ict", NT * T),
               ("ist", NT * T), ("ccsc", 2 * P), ("cl", NT * T), ("sl", NT * T), ("causal", NT * T),
               ("upto", NT * T), ("from", NT * T), ("negsel", NH * P), ("tneg", NT), ("inv", 12), ("zero", 8), ("quarter", 4)):
    CONST[_n] = (_at, _w)
    _at += _w
NCONST = _at

COLS = [("c", "c", 0, 8), ("c_ctx", "c_ctx", 0, 8), ("c_2", "c_2", 0, 8), ("n1", "norm1_w", 0, 8), ("n2", "norm2_w", 0, 8),
        ("ga0", "g_attn_2", 0, 8), ("ga1", "g_attn_2", 8, 8), ("gf0", "g_ffn_2", 0, 8), ("gf1", "g_ffn_2", 8, 8),
        ("hcb", "hy_conv_b", 0, 12), ("mcb", "ml_conv_b", 0, 8), ("skip", "hy_skip", 0, 8),
        ("ab0", "ada_b", 0, 48), ("ab1", "b_ada_2", 0, 48), ("ab2", "b_ada_2", 48, 48),
        ("bz", "b_in", 0, 24), ("bg", "b_in_gate", 0, 24),
        ("hcw", "hy_conv_w", 0, 108), ("mcw", "ml_conv_w", 0, 72)]
COL = {}
_at = 0
for _n, _s, _r, _k in COLS:
    COL[_n] = _at
    _at += _k
NCOLB = -(-_at // P)


def shape_constants():
    blob = np.zeros((P, NCONST), np.float32)

    def put(name, a):
        o, w = CONST[name]
        blob[: a.shape[0], o:o + w] = a.reshape(a.shape[0], w)

    def rows(a):
        return a.reshape(NT, P, -1).transpose(1, 0, 2)

    put("ident", np.eye(P))
    put("ones", np.ones((P, P)))
    t = np.arange(T, dtype=np.float32) / np.float32(T)
    bands = np.linspace(1e-4, 15, 16, dtype=np.float32)
    ang = np.float32(2 * math.pi) * t[:, None] * bands[None, :]
    put("feats", np.concatenate([t[:, None], np.cos(ang), np.sin(ang)], -1).T)
    w = np.outer(np.arange(T), 2 * np.arange(T) + 1) * (math.pi / (2 * T))
    put("cs", rows(np.cos(w)))
    put("ss", rows(np.sin(w)))
    put("ict", rows(np.cos(w).T / T))
    put("ist", rows(-np.sin(w).T / T))
    f = np.outer(np.arange(P), np.arange(P)) * (2 * math.pi / P)
    put("ccsc", np.concatenate([np.cos(f), np.sin(f)], -1))
    g = np.outer(np.arange(T), np.arange(T)) * (2 * math.pi / T)
    put("cl", rows(np.cos(g) / math.sqrt(T * P)))
    put("sl", rows(-np.sin(g) / math.sqrt(T * P)))
    low = np.tril(np.ones((T, T)))
    put("causal", rows(np.where(low > 0, 0.0, MASKED)))
    put("upto", rows(low.T))
    put("from", rows(low))
    sel = np.zeros((NH, NH, P))
    for h in range(NH):
        sel[h, h] = -1.0
    put("negsel", sel)
    put("tneg", -t.reshape(NT, P).T)
    inv = [1.0 / (500000.0 ** (np.arange(0, r, 2, dtype=np.float32) / r)) for r in (16, 8)]
    put("quarter", (np.arange(P)[:, None] // 32 == np.arange(4)).astype(np.float32))
    put("inv", np.tile(np.concatenate(inv).astype(np.float32), (P, 1)))
    return blob


STAGES = [("ada0", 12, 0), ("in1", 8, 0), ("merge", 6, 0), ("out1", 2, 0), ("moe1", E1 - 1, NS), ("moe1_last", 1, 0),
          ("ada1", 12, 0), ("in2_0", 6, 0), ("out2_0", 2, 0), ("ff", NCH, 0),
          ("ada2", 12, 0), ("in2_1", 6, 0), ("out2_1", 2, 0), ("moe2", NCH * E2, NCH)]


def unit_plan():
    plan, n, used, full = {}, 0, [0] * NS, [0] * NS
    for at, (name, count, body) in enumerate(STAGES):
        if body:
            last = [max(c for c in range(body) if c % NS == s) for s in range(NS)]
            per_slot = [len(range(s, body, NS)) for s in range(NS)]
            entries = []
            for c in range(body):
                s = c % NS
                free = n + c - NS + 1 if c >= NS else n - body + last[s] + 1
                assert c >= NS or free >= used[s]
                entries.append((s, free, full[s] + 1 + c // NS))
            n += count
            for s in range(NS):
                used[s] = n - body + last[s] + 1
                full[s] += count // body * per_slot[s]
            plan[name] = (entries, body, per_slot)
            continue
        ahead = [(k, b) for _, k, b in STAGES[at:]]
        loop = next(i for i, (_, b) in enumerate(ahead) if b) if any(b for _, b in ahead) else None
        final = n + sum(k for k, _ in ahead[:loop]) - 1
        turn = (ahead[loop][1] - 1 - final) % NS
        entries = []
        for _ in range(count):
            s = (n + turn) % NS
            entries.append((s, used[s], full[s] + 1))
            n += 1
            used[s], full[s] = n, full[s] + 1
        plan[name] = (entries, 0, None)
    return plan


PLAN = unit_plan()
START = {}
for _i, (_n, _k, _) in enumerate(STAGES):
    START[_n] = sum(k for _, k, _ in STAGES[:_i])

IN1_COLS = (0, DBR, 2 * DBR, ML0, ML0 + DBR, 3 * DBR, ML0 + 2 * DBR, ML0 + 3 * DBR)
IN2_COLS = tuple((c, min(512, D_IN - c)) for c in range(0, D_IN, 512))
ZQ, ZK, ZFN = 12, 16, 20

R_Z, R_KF, R_KC, R_V1, R_OG, R_VT, ARENA = 0, 6144, 10240, 11264, 13328, 14352, 15376
R_H3, R_SQ, R_PQ, R_DEC, R_W3, R_EXP, R_ROWS = 0, 4096, 8192, 8192, 10240, 12288, 14336
R_PJ, R_FM, R_SM, R_PT, R_IX, R_SEL = 0, 5512, 10376, 12424, 13448, 13960
R_SG, R_AT, R_YA = 0, 512, 1024

FM_COLS = (0, 128, 256, 384, 320, 512, 640, 768, 704, 836, 964, 1092, 1220, 1604, 1732, 1860, 1988, 2116, 2244)
FM_QA, FM_KA, FM_QI, FM_KI, FM_QB, FM_KB, FM_QC, FM_KC = 0, (3, 4), 5, (7, 8), 9, 11, 13, 16
NFM = len(FM_COLS)

JOBS = [(br, h0, n, qb) for br, h0, n in (("B", 0, 4), ("B", 4, 4), ("C", 0, 4), ("C", 4, 2), ("A", 0, 4), ("A", 4, 2))
        for qb in range(NT)]
RMS = ("ctx", "x1", "x2", "final1", "a0", "f0", "a1", "f1", "final2")
TRS = ("ctx", "x1", "x2", "a0", "f0", "a1", "f1")
PAIRS, TILE = {4: (0, 2, 1, 3), 2: (0, 1)}, {4: 1, 2: 2}
LAM_INIT = [0.8 - 0.6 * math.exp(-0.3 * l) for l in range(2)]


def build(nc, A, blob_in, out):
    with ExitStack() as ctx:
        def sb(name, shape, dt=F32):
            return ctx.enter_context(nc.sbuf_tensor(name, shape, dt))

        sems = {}

        def sem(name):
            if name not in sems:
                sems[name] = ctx.enter_context(nc.semaphore(name))
            return sems[name]

        ring = sb("ring", [P, NS, SLOT])
        blob = sb("blob", [P, NCONST])
        colv = sb("colv", [P, NCOLB * P])
        x = sb("x", [P, NT, D])
        xn = sb("xn", [P, NT * D])
        hT = sb("hT", [P, KD, T])
        late = sb("late", [P, 2 * D])
        grow = sb("grow", [P, 2, D])
        arena = sb("arena", [P, ARENA])
        rowv = sb("rowv", [P, 2 * DBR])
        mlnw = sb("mlnw", [P, DBR])
        subln = sb("subln", [P, 2, HD])
        lamt = sb("lamt", [P, 8])
        lamj = sb("lamj", [P, 32])
        rb1 = sb("rb1", [P, 20])
        wmlg = sb("wmlg", [P, KD, 16])
        rw1 = sb("rw1", [P, KD, 20])
        rw2 = sb("rw2", [P, KD, E2])
        gb = sb("gb", [NH, 4])
        fcol = sb("fcol", [64, 3])
        cact = sb("cact", [P, 24])
        mod = sb("mod", [P, 48])
        modc = sb("modc", [P, 16])
        ga = sb("ga", [P, 16])
        gac = sb("gac", [P, 8])
        kn = sb("kn", [P, 8])
        st = sb("st", [P, 16])
        comb = sb("comb", [P, NT, E1])
        rt = sb("rt", [P, NT, 96])
        gcol = sb("gcol", [P, 32])
        en = sb("en", [P, 16])
        dn = sb("dn", [P, 16])
        posi = sb("posi", [P, NT], I32)
        posf = sb("posf", [P, NT])
        ang = sb("ang", [P, 4, NT, 12])
        cosn = sb("cosn", [P, NT, 12])
        sinn = sb("sinn", [P, NT, 12])
        amx = sb("amx", [P, 2, 4])
        asum = sb("asum", [P, 2, 4])
        ars = sb("ars", [P, 2, 8])
        top = sb("top", [P, 8])
        wix = sb("wix", [P, NT, 4])
        ps = ctx.enter_context(nc.psum_tensor("ps", [P, 8, 512], F32))

        def const(name, n=P):
            o, w = CONST[name]
            return blob[0:n, o:o + w]

        def const2(name):
            return const(name).rearrange("p (b n) -> p b n", b=NT)

        def region(off, *shape):
            n = int(np.prod(shape))
            v = arena[:, off:off + n]
            if len(shape) == 1:
                return v
            names = "abcd"[:len(shape)]
            return v.rearrange(f"p ({' '.join(names)}) -> p {' '.join(names)}", **dict(zip(names, shape)))

        def col(name, k, n=1):
            return colv[:, COL[name] + k:COL[name] + k + n]

        ident = const("ident")
        vrows = region(R_ROWS, NCOLB, P)
        fw1 = region(R_ROWS + 512, 64)[0:33]
        fw2 = region(R_ROWS + 576, 64)[0:64]
        lamr = region(R_ROWS + 640, 2, 4, 32)
        gates = late[0:NH, :].rearrange("p (i d n) -> p i d n", i=2, d=2)
        z = region(R_Z, 24, T)
        kf = region(R_KF, 2, 2, 2 * DBR)
        kc = region(R_KC, NBR, T)
        v1 = region(R_V1, 4, NH, P + 1)
        og = region(R_OG, NT, DBR)
        vt = region(R_VT, NT, DBR)
        macc = region(R_KF, KD, T)
        sgm = region(R_KF + KD * T, 2, NBR, T)
        xn2 = xn[:, :].rearrange("p (b n) -> p b n", b=NT)
        hTc = late[:, :].rearrange("p (k n) -> p k n", k=KD)
        all_ps = ps[:, :, :].rearrange("p b n -> p (b n)")
        full = [sem(f"slot{s}_full") for s in range(NS)]
        used = sem("units_used")
        DMA3 = 48

        block = ctx.enter_context(nc.Block())

        @block.sync
        def _(sp):
            def enter(entry):
                s, free, _ = entry
                if free:
                    sp.wait_ge(used, free)
                return s

            def columns(s, src, width):
                dst = ring[:, s, 0:KD * width].rearrange("p (k n) -> p k n", k=KD)
                for a, b in ((0, 3), (3, 6), (6, 8)):
                    sp.dma_start(dst[:, a:b, :], src[a * P:b * P, :].rearrange("(k p) n -> p k n", p=P)).then_inc(full[s], 16)

            def chunk(s, wg, wu, wd):
                for i, w in enumerate((wg, wu)):
                    sp.dma_start(ring[:, s, i * 2048:(i + 1) * 2048].rearrange("p (k n) -> p k n", k=KD),
                                 w.rearrange("(k p) n -> p k n", p=P)).then_inc(full[s], 16)
                sp.dma_start(ring[:, s, 4096:SLOT].rearrange("p (k n) -> p k n", k=2),
                             wd.rearrange("(k p) n -> p k n", p=P)).then_inc(full[s], 16)

            def ada(name, w):
                for j, entry in enumerate(PLAN[name][0]):
                    columns(enter(entry), w[:, j * 512:(j + 1) * 512], 512)

            ada("ada0", A["ada_w"][0])
            for c, entry in zip(IN1_COLS, PLAN["in1"][0]):
                columns(enter(entry), A["w_in"][0, :, c:c + 512], 512)
            for j, entry in enumerate(PLAN["merge"][0]):
                s = enter(entry)
                k, half = divmod(j, 2)
                src = A["w_in"][0, :, GATE0 + j * 512:GATE0 + (j + 1) * 512]
                dst = ring[:, s, 0:4096].rearrange("p (k n) -> p k n", k=KD)
                for a in (0, 4):
                    sp.dma_start(dst[:, a:a + 4, :],
                                 src[a * P:(a + 4) * P, :].rearrange("(k p) n -> p k n", p=P)).then_inc(full[s], 16)
                sp.dma_start(ring[:, s, 4096:SLOT].rearrange("p (k n) -> p k n", k=NBR),
                             A["w_branch"][0, k, :, half * 512:(half + 1) * 512].rearrange("(k p) n -> p k n", p=P)
                             ).then_inc(full[s], 16)
            for j, entry in enumerate(PLAN["out1"][0]):
                columns(enter(entry), A["w_out"][0, :, j * 512:(j + 1) * 512], 512)
            g1, u1, d1 = A["moe_w_gate"][0], A["moe_w_up"][0], A["moe_w_down"][0]
            entries, body, _ = PLAN["moe1"]
            with sp.Fori(0, (E1 - 1) // body) as i:
                for c, (s, free, _) in enumerate(entries):
                    sp.wait_ge(used, i * body + free)
                    e = i * body + c
                    chunk(s, g1[bass.ds(e, 1)].rearrange("a k n -> (a k) n"), u1[bass.ds(e, 1)].rearrange("a k n -> (a k) n"),
                          d1[bass.ds(e, 1)].rearrange("a k n -> (a k) n"))
            chunk(enter(PLAN["moe1_last"][0][0]), g1[E1 - 1], u1[E1 - 1], d1[E1 - 1])

            for l in range(2):
                ada(f"ada{l + 1}", A["w_ada_2"][l])
                for (c, w), entry in zip(IN2_COLS, PLAN[f"in2_{l}"][0]):
                    columns(enter(entry), A["w_in_2"][l, :, c:c + w], w)
                for j, entry in enumerate(PLAN[f"out2_{l}"][0]):
                    columns(enter(entry), A["w_out_2"][l, :, j * 512:(j + 1) * 512], 512)
                if l == 0:
                    for c, entry in enumerate(PLAN["ff"][0]):
                        h = slice(c * CH, (c + 1) * CH)
                        chunk(enter(entry), A["w_ff_gate_2"][0, :, h], A["w_ff_up_2"][0, :, h], A["w_ff_down_2"][0, h, :])
            g2, u2, d2 = A["w_exp_gate_2"][0], A["w_exp_up_2"][0], A["w_exp_down_2"][0]
            entries, body, _ = PLAN["moe2"]
            with sp.Fori(0, E2) as e:
                for c, (s, free, _) in enumerate(entries):
                    sp.wait_ge(used, e * body + free)
                    h = slice(c * CH, (c + 1) * CH)
                    chunk(s, g2[bass.ds(e, 1), :, h].rearrange("a k n -> (a k) n"),
                          u2[bass.ds(e, 1), :, h].rearrange("a k n -> (a k) n"),
                          d2[bass.ds(e, 1), h, :].rearrange("a k n -> (a k) n"))
            sp.wait_ge(sem("y_final"), 1)
            sp.dma_start(out[0].rearrange("(b p) d -> p b d", p=P), xn2).then_inc(sem("stored"), 16)
            sp.wait_ge(sem("stored"), 16)

        @block.gpsimd
        def _(pool):
            pool.dma_start(blob[:, :], blob_in).then_inc(sem("consts_in"), 16)
            for name, src, r0, n in COLS:
                a = A[src]
                flat = a.rearrange(" ".join("abcd"[:a.ndim]) + " -> (" + " ".join("abcd"[:a.ndim]) + ")") if a.ndim > 1 else a
                v = flat[r0 * P:(r0 + n) * P].rearrange("(r p) -> r p", p=P)
                at, done = COL[name], 0
                while done < n:
                    b, p = divmod(at + done, P)
                    m = min(n - done, P - p)
                    pool.dma_start(vrows[p:p + m, b, :], v[done:done + m, :]).then_inc(sem("cols_in"), 16)
                    done += m
            pool.dma_start(fw1[:, :], A["hy_f_w1"][0]).then_inc(sem("filter_in"), 16)
            pool.dma_start(fw2[:, :], A["hy_f_w2"][0]).then_inc(sem("filter_in"), 16)
            pool.dma_start(region(R_W3, 2048)[0:64, :], A["hy_f_w3"][0]).then_inc(sem("filter_in"), 16)
            for i, name in enumerate(("hy_f_b1", "hy_f_b2", "hy_f_freq")):
                pool.dma_start(fcol[:, i:i + 1], A[name][0].rearrange("(p a) -> p a", a=1), allow_slow_non_contiguous=True).then_inc(sem("filter_in"), 16)
            pool.dma_start(region(R_DEC, 2048), A["hy_decay"][0].rearrange("o d c -> (o d c)").partition_broadcast(P)
                           ).then_inc(sem("decay_in"), 16)
            pool.dma_start(hT[:, :, :].rearrange("p k n -> p (k n)").rearrange("p (b d) -> p b d", b=NT),
                           A["ctx"][0].rearrange("(b p) d -> p b d", p=P)).then_inc(sem("ctx_in"), 16)
            pool.dma_start(x[:, :, :], A["x"][0].rearrange("(b p) d -> p b d", p=P)).then_inc(sem("x_in"), 16)
            pool.dma_start(rowv[:, :], A["b_in"][0, ML0 + 2 * DBR:MLG0].partition_broadcast(P)).then_inc(sem("rows_in"), 16)
            pool.dma_start(mlnw[:, :], A["ml_norm_w"][0].partition_broadcast(P)).then_inc(sem("rows_in"), 16)
            pool.dma_start(gb[:, :], A["b_in"][0, MLG0:GATE0].rearrange("(g h) -> h g", h=NH), allow_slow_non_contiguous=True).then_inc(sem("rows_in"), 16)
            pool.dma_start(wmlg[:, :, :], A["w_in"][0, :, MLG0:GATE0].rearrange("(k p) n -> p k n", p=P)).then_inc(sem("rows_in"), 16)
            pool.dma_start(rb1[:, 0:4], A["moe_rg_b"][0].partition_broadcast(P)).then_inc(sem("rows_in"), 16)
            pool.dma_start(rb1[:, 4:20], A["moe_re_b"][0].partition_broadcast(P)).then_inc(sem("rows_in"), 16)
            pool.dma_start(rw1[:, :, 0:4], A["moe_rg_w"][0].rearrange("(k p) n -> p k n", p=P)).then_inc(sem("rows_in"), 16)
            pool.dma_start(rw1[:, :, 4:20], A["moe_re_w"][0].rearrange("(k p) n -> p k n", p=P)).then_inc(sem("rows_in"), 16)
            pool.dma_start(rw2[:, :, :], A["w_router_2"][0].rearrange("(k p) n -> p k n", p=P)).then_inc(sem("rows_in"), 16)
            pool.dma_start(subln[:, :, :].rearrange("p a b -> p (a b)"),
                           A["diff_subln_2"].rearrange("a b -> (a b)").partition_broadcast(P)).then_inc(sem("rows_in"), 16)
            pool.dma_start(lamr[:, :, :, :].rearrange("p a b c -> p (a b c)"),
                           A["diff_lambda_2"].rearrange("a b c -> (a b c)").partition_broadcast(P)).then_inc(sem("rows_in"), 16)
            pool.dma_start(posi[:, :], A["positions_2"][0].rearrange("(b p) -> p b", p=P), allow_slow_non_contiguous=True).then_inc(sem("rows_in"), 16)
            pool.wait_ge(sem("ml_gates"), 1)
            pool.dma_start(late[:, 0:D], A["norm_f_w"].partition_broadcast(P)).then_inc(sem("late_in"), 16)
            pool.dma_start(late[:, D:2 * D], A["g_final_2"].partition_broadcast(P)).then_inc(sem("late_in"), 16)

        N_COLS_IN = sum(1 + (COL[n] // P != (COL[n] + k - 1) // P) for n, _, _, k in COLS)
        N_ROWS_IN = 12

        @block.tensor
        def _(pe):
            mm = nc.tensor.matmul

            def unit(entry):
                s, _, n = entry
                pe.wait_ge(full[s], DMA3 * n)
                return s

            def w512(s, k, a=0, n=512, width=512):
                return ring[:, s, k * width + a:k * width + a + n]

            pe.wait_ge(sem("consts_in"), 16)
            pe.wait_ge(sem("cols_in"), 16 * N_COLS_IN)
            total = sum(k for *_, k in COLS)
            for b in range(NCOLB):
                n = min(P, total - b * P)
                last = nc.tensor.transpose(ps[:, 0, b * P:b * P + n], vrows[0:n, b, :], ident[0:n, 0:n])
            last.then_inc(sem("cols_t"), 1)

            pe.wait_ge(sem("filter_in"), 96)
            mm(ps[0:64, 1, 0:T], fw1[:, :], const("feats", 33), start=True, stop=True).then_inc(sem("filter_mm"), 1)
            pe.wait_ge(sem("filter_h"), 1)
            mm(ps[0:64, 2, 0:T], fw2[:, :], region(R_SQ + 512, T)[0:64, :], start=True, stop=True).then_inc(sem("filter_mm"), 1)
            pe.wait_ge(sem("filter_h"), 2)
            h2 = region(R_SQ + 768, T)
            for b in range(NT):
                if b:
                    pe.wait_ge(sem("filter_h3"), b)
                for n in range(4):
                    last = mm(ps[:, 4 + n, :], h2[0:64, b * P:(b + 1) * P], region(R_W3, 2048)[0:64, n * 512:(n + 1) * 512],
                              start=True, stop=True)
                last.then_inc(sem("filter_mm"), 1)
            pe.wait_ge(sem("filter_sq"), 1)
            sq = region(R_SQ, NT, 2, 2, DBR)
            for o in range(2):
                for c in range(NBR):
                    for i, (d, b) in enumerate((d, b) for d in range(2) for b in range(NT)):
                        last = mm(ps[:, 1, o * NBR + c:o * NBR + c + 1], sq[:, b, o, d, c * P:(c + 1) * P], const("ones")[:, 0:1],
                                  start=i == 0, stop=i == 3)
            last.then_inc(sem("filter_ssum"), 1)
            pe.wait_ge(sem("filter_pq"), 1)
            pe.wait_ge(sem("kn_in"), 1)
            pq = region(R_PQ, NT, 2, 2, DBR)
            for o in range(2):
                for ri, table in enumerate(("cs", "ss")):
                    for m in range(NT):
                        for b in range(NT):
                            last = mm(ps[:, 4 * o + 2 * ri + m, :], const2(table)[:, b, m * P:(m + 1) * P], pq[:, b, o, ri, :],
                                      start=b == 0, stop=b == NT - 1)
            last.then_inc(sem("spectra_mm"), 1)

            def ada(a):
                if a == 0:
                    pe.wait_ge(sem("c_act"), 1)
                    pe.wait_ge(sem("spectra_in"), 1)
                else:
                    pe.wait_ge(sem("block_done"), a)
                n = 2 if a == 0 else 1
                for j, entry in enumerate(PLAN[f"ada{a}"][0]):
                    s = unit(entry)
                    for m in range(4):
                        o = (4 * j + m) * n
                        for k in range(KD):
                            rhs = cact[:, k:k + 9:8] if a == 0 else cact[:, 16 + k:17 + k]
                            last = mm(ps[:, 0, o:o + n], w512(s, k, m * P, P), rhs, start=k == 0, stop=k == KD - 1)
                    last.then_inc(used, 1)
                pe.wait_ge(sem("diag"), a + 1)
                for g in range(16):
                    last = mm(ps[:, 2 + g // 4, (g % 4) * P:(g % 4 + 1) * P], const("ones"), xn[:, g * P:(g + 1) * P],
                              start=True, stop=True)
                last.then_inc(sem("gaterow_mm"), 1)

            def turn(name, banks_free=()):
                i = TRS.index(name)
                for s_, v_ in banks_free:
                    pe.wait_ge(sem(s_), v_)
                pe.wait_ge(sem("normed"), i + 1)
                for k in range(KD):
                    for b in range(NT):
                        last = nc.tensor.transpose(ps[:, 4 + k // 2, (k % 2) * T + b * P:(k % 2) * T + (b + 1) * P],
                                                   xn2[:, b, k * P:(k + 1) * P], ident)
                last.then_inc(sem("turned"), 1)

            def columns_by(s, src, bank):
                for m in range(4):
                    for k in range(KD):
                        last = mm(ps[:, bank + m // 2, (m % 2) * T:(m % 2 + 1) * T], w512(s, k, m * P, P), src[:, k, :],
                                  start=k == 0, stop=k == KD - 1)
                return last

            def rows_by(s, src, bank, n=512):
                for b in range(NT):
                    for k in range(KD):
                        last = mm(ps[:, bank + b, 0:n], src[:, k, b * P:(b + 1) * P], w512(s, k, 0, n, n),
                                  start=k == 0, stop=k == KD - 1)
                return last

            ada(0)
            turn("ctx", [("gaterow_in", 1)])
            turn("x1", [("hT_ready", 1)])
            pe.wait_ge(sem("hT_ready"), 2)

            entries = PLAN["in1"][0]
            for g in range(4):
                s = unit(entries[g])
                columns_by(s, hT, 2 * g).then_inc(used, 1)
            s = unit(entries[4])
            pe.wait_ge(sem("z_in"), 1)
            columns_by(s, hT, 0).then_inc(sem("k_mm"), 1)
            pe.wait_ge(sem("z_in"), 2)
            columns_by(s, hTc, 2).then_inc(used, 1)
            s = unit(entries[5])
            pe.wait_ge(sem("z_in"), 3)
            columns_by(s, hT, 4).then_inc(used, 1)
            s = unit(entries[6])
            pe.wait_ge(sem("z_in"), 4)
            rows_by(s, hT, 6).then_inc(sem("vo_mm"), 1)
            pe.wait_ge(sem("z_in"), 5)
            rows_by(s, hTc, 0).then_inc(used, 1)
            s = unit(entries[7])
            pe.wait_ge(sem("z_in"), 6)
            rows_by(s, hT, 2).then_inc(used, 1)
            pe.wait_ge(sem("rows_in"), 16 * N_ROWS_IN)
            pe.wait_ge(sem("z_in"), 7)
            pe.wait_ge(sem("vo_in"), 1)
            for g in range(4):
                for i, src in enumerate((hTc, hT)):
                    for k in range(KD):
                        last = mm(ps[0:NH, 4 + g, i * T:(i + 1) * T], wmlg[:, k, g * NH:(g + 1) * NH], src[:, k, :],
                                  start=k == 0, stop=k == KD - 1)
            last.then_inc(sem("gates_mm"), 1)

            pe.wait_ge(sem("vo_in"), 3)
            for b in range(NT):
                for g in range(4):
                    last = mm(ps[:, 2 * b + g // 2, (g % 2) * T:(g % 2 + 1) * T], z[:, ZFN + g, b * P:(b + 1) * P], const("ccsc"),
                              start=True, stop=True)
            last.then_inc(sem("fnet_mm"), 1)
            pe.wait_ge(sem("fnet_in"), 1)
            pe.wait_ge(sem("vo_in"), 4)
            ab = xn[:, :].rearrange("p (b g n) -> p b g n", b=NT, g=4)
            for g in range(4):
                for i, (b, table) in enumerate((b, t) for b in range(NT) for t in range(2)):
                    last = mm(ps[:, 4 + g // 2, (g % 2) * T:(g % 2 + 1) * T], ab[:, b, g, table * P:(table + 1) * P],
                              const2(("cl", "sl")[table])[:, b, :], start=i == 0, stop=i == 3)
            last.then_inc(sem("fnet_mm"), 1)

            for o in range(2):
                pe.wait_ge(sem("hy_u"), o + 1)
                for b in range(NT):
                    for c in range(NBR):
                        last = nc.tensor.transpose(ps[:, b, c * P:(c + 1) * P], z[:, c, b * P:(b + 1) * P], ident)
                last.then_inc(sem("hy_t"), 1)
                pe.wait_ge(sem("hy_rows"), o + 1)
                for ri, table in enumerate(("cs", "ss")):
                    for m in range(NT):
                        for b in range(NT):
                            last = mm(ps[:, 2 * ri + m, :], const2(table)[:, b, m * P:(m + 1) * P], vt[:, b, :],
                                      start=b == 0, stop=b == NT - 1)
                last.then_inc(sem("hy_spec"), 1)
                pe.wait_ge(sem("hy_y"), o + 1)
                yy = xn[:, :].rearrange("p (r m n) -> p r m n", r=2, m=NT)
                for c in range(NBR):
                    for i, (r, m) in enumerate((r, m) for r in range(2) for m in range(NT)):
                        last = mm(ps[:, 6 + c // 2, (c % 2) * T:(c % 2 + 1) * T], yy[:, r, m, c * P:(c + 1) * P],
                                  const2(("ict", "ist")[r])[:, m, :], start=i == 0, stop=i == 3)
                last.then_inc(sem("hy_inv"), 1)

            gi, gf, _, gm = (region(R_KF + i * 1024, 2, 512) for i in range(4))
            pe.wait_ge(sem("ml_gates"), 1)
            for d in range(2):
                for sbk in range(4):
                    nc.tensor.transpose(ps[:, 0, (d * 4 + sbk) * 4:(d * 4 + sbk) * 4 + 4], gi[0:NH, d, sbk * P:(sbk + 1) * P], ident[0:NH, 0:NH])
                for b in range(NT):
                    o = 32 + (d * 2 + b) * 4
                    nc.tensor.transpose(ps[:, 1, o:o + 4], gf[0:NH, d, T + b * P:T + (b + 1) * P], ident[0:NH, 0:NH])
                for h in range(NH):
                    last = mm(ps[:, 2 + 2 * d + h // 2, (h % 2) * T:(h % 2 + 1) * T], const("negsel", NH)[:, h * P:(h + 1) * P],
                              gm[0:NH, d, T:2 * T], start=True, stop=True)
            last.then_inc(sem("ml_cols_mm"), 1)
            pe.wait_ge(sem("ml_qk"), 1)
            pe.wait_ge(sem("ml_cols"), 2)
            for h in range(NH):
                if h:
                    pe.wait_ge(sem("ml_p"), 2 * h)
                for sbk in range(4):
                    k_ = kc[:, h, sbk * P:(sbk + 1) * P] if sbk < 2 else z[:, ZK + h, (sbk - 2) * P:(sbk - 1) * P]
                    last = mm(ps[:, 6 + sbk // 2, (sbk % 2) * T:(sbk % 2 + 1) * T], k_, z[:, ZQ + h, :], start=True, stop=True)
                last.then_inc(sem("ml_s"), 1)
                for d in range(2):
                    j = 2 * h + d
                    pe.wait_ge(sem("ml_p"), j + 1)
                    if j >= 2:
                        pe.wait_ge(sem("ml_h"), j - 1)
                    w = xn[:, (j % 2) * 1024:(j % 2 + 1) * 1024].rearrange("p (s n) -> p s n", s=4)
                    for b in range(NT):
                        for sbk in range(4):
                            last = mm(ps[:, j % 2, b * T:b * T + P + 1], w[:, sbk, b * P:(b + 1) * P], v1[:, sbk, h, :],
                                      start=sbk == 0, stop=sbk == 3)
                    last.then_inc(sem("ml_pv"), 1)
            pe.wait_ge(sem("ml_y"), 1)
            for c in range(NH):
                for b in range(NT):
                    last = nc.tensor.transpose(ps[:, 2 + c // 2, (c % 2) * T + b * P:(c % 2) * T + (b + 1) * P],
                                               vt[:, b, c * P:(c + 1) * P], ident)
            last.then_inc(sem("ml_t"), 1)

            pe.wait_ge(sem("ml_yT"), 1)
            pe.wait_ge(sem("fnet_in"), 2)
            for j, entry in enumerate(PLAN["merge"][0]):
                s = unit(entry)
                k, base = j // 2, 4 * (j % 2)
                if j >= 2:
                    pe.wait_ge(sem("merged"), j - 1)
                columns_by(s, hT, base).then_inc(sem("mg_mm"), 1)
                y0 = (0, ZFN, ZQ)[k]
                for m in range(4):
                    for c in range(NBR):
                        last = mm(ps[:, base + 2 + m // 2, (m % 2) * T:(m % 2 + 1) * T],
                                  ring[:, s, 4096 + c * 512 + m * P:4096 + c * 512 + (m + 1) * P], z[:, y0 + c, :],
                                  start=c == 0, stop=c == NBR - 1)
                last.then_inc(used, 1)

            def out_proj(name, src):
                for half, entry in enumerate(PLAN[name][0]):
                    s = unit(entry)
                    rows_by(s, src, 2 * half).then_inc(used, 1)

            def chunk_mm(s, n, first, last_, evacuated=None):
                for hb in range(2):
                    pe.wait_ge(sem("act_ready"), n - 1 + hb)
                    for i in range(2):
                        for k in range(KD):
                            o = i * 2048 + k * CH + hb * P
                            m_ = mm(ps[:, hb, i * T:(i + 1) * T], ring[:, s, o:o + P], hT[:, k, :],
                                    start=k == 0, stop=k == KD - 1)
                    m_.then_inc(sem("gu_mm"), 1)
                if first:
                    pe.wait_ge(sem("y_read"), evacuated)
                for hb in range(2):
                    pe.wait_ge(sem("act_ready"), n + 1 + hb)
                    for b in range(NT):
                        for half in range(2):
                            o = 4096 + hb * 1024 + half * 512
                            m_ = mm(ps[:, 4 + 2 * b + half, :], region(R_AT, 2, T)[:, hb, b * P:(b + 1) * P], ring[:, s, o:o + 512],
                                    start=first and hb == 0, stop=last_ and hb == 1)
                m_.then_inc(used, 1)

            def router(rw, n, i):
                for b in range(NT):
                    for k in range(KD):
                        last = mm(ps[:, 3, b * 32:b * 32 + n], hT[:, k, b * P:(b + 1) * P], rw[:, k, :],
                                  start=k == 0, stop=k == KD - 1)
                last.then_inc(sem("router_mm"), 1)

            pe.wait_ge(sem("merged"), 6)
            out_proj("out1", macc)
            turn("x2", [])
            pe.wait_ge(sem("hT_ready"), 3)
            router(rw1, 20, 0)
            entries, body, per_slot = PLAN["moe1"]
            with pe.Fori(0, (E1 - 1) // body) as i:
                for c, (s, _, f) in enumerate(entries):
                    pe.wait_ge(full[s], i * (DMA3 * per_slot[s]) + DMA3 * f)
                    chunk_mm(s, i * (2 * body) + 2 * c + 2, True, True, i * body + c + 1)
            s = unit(PLAN["moe1_last"][0][0])
            chunk_mm(s, 2 * (E1 - 1) + 2, True, True, E1)
            hidden, outputs = 2 * E1, E1 + 1

            for l in range(2):
                ada(l + 1)
                turn(f"a{l}", [("gaterow_in", l + 2)])
                pe.wait_ge(sem("hT_ready"), 4 + 2 * l)
                for j, ((c, w), entry) in enumerate(zip(IN2_COLS, PLAN[f"in2_{l}"][0])):
                    s = unit(entry)
                    if j >= 4:
                        pe.wait_ge(sem("pj_in"), 6 * l + j - 3)
                    rows_by(s, hT, 2 * (j % 4), w).then_inc(used, 1)
                pj = region(R_PJ, NT, D_IN)
                fm = region(R_FM, NFM, T)
                pe.wait_ge(sem("roped"), l + 1)
                n_t = -(-NFM // 4)
                for q in range(n_t):
                    if q >= 2:
                        pe.wait_ge(sem("fm_in"), n_t * l + q - 1)
                    for i in range(4 * q, min(NFM, 4 * q + 4)):
                        for b in range(NT):
                            last = nc.tensor.transpose(
                                ps[:, 2 * (q % 2) + (i % 4) // 2, (i % 2) * T + b * P:(i % 2) * T + (b + 1) * P],
                                pj[:, b, FM_COLS[i]:FM_COLS[i] + P], ident)
                    last.then_inc(sem("fm_mm"), 1)
                pe.wait_ge(sem("fm_in"), n_t * (l + 1))
                for qb in range(NT):
                    ns = (qb + 1) * P
                    for h in range(4):
                        p0 = 64 * (h % 2)
                        last = mm(ps[:, 4 + 2 * qb + h % 2, (h // 2) * T:(h // 2) * T + ns],
                                  fm[p0:p0 + 64, FM_QI + h // 2, qb * P:(qb + 1) * P], fm[p0:p0 + 64, FM_KI[h % 2], 0:ns],
                                  start=True, stop=True)
                    last.then_inc(sem("ix_mm"), 1)

                sm = region(R_SM, 2, 4, T)
                pt = region(R_PT, 4, NT, P)

                def scores(j):
                    br, h0, n, qb = JOBS[j]
                    ns = (qb + 1) * P
                    if j >= 2:
                        pe.wait_ge(sem("masked"), len(JOBS) * l + j - 1)
                    if j == 0:
                        pe.wait_ge(sem("qb_masked"), l + 1)
                    for k in range(n):
                        if br == "B":
                            i, tile = k, k
                            q_, k_ = hT[:, h0 + i, :], fm[:, FM_KB + h0 // 4, :]
                        else:
                            i, tile = PAIRS[n][k], TILE[n] * k
                            h = h0 + i
                            rows = slice(64 * (h % 2), 64 * (h % 2) + 64)
                            q_ = fm[rows, (FM_QA if br == "A" else FM_QC) + h // 2, :]
                            k_ = fm[rows, FM_KA[h % 2] if br == "A" else FM_KC + h // 2, :]
                        last = mm(ps[:, 2 * (j % 2) + tile // 2, (tile % 2) * T:(tile % 2) * T + ns],
                                  q_[:, qb * P:(qb + 1) * P], k_[:, 0:ns], start=True, stop=True)
                    last.then_inc(sem("s_mm"), 1)

                scores(0)
                for j, (br, h0, n, qb) in enumerate(JOBS):
                    if j + 1 < len(JOBS):
                        scores(j + 1)
                    done = len(JOBS) * l + j
                    heads = n // 2 if br == "B" else n
                    pe.wait_ge(sem("probs"), done + 1)
                    if j == 0:
                        pe.wait_ge(sem("ix_in"), 2 * (l + 1))
                    for i in range(heads):
                        for sbk in range(qb + 1):
                            src = sm[:, j % 2, 2 * i if br == "B" else i, sbk * P:(sbk + 1) * P]
                            o = (i * 2 + sbk) * P
                            last = nc.tensor.transpose(ps[:, 4 + o // 512, o % 512:o % 512 + P], src, ident)
                    last.then_inc(sem("pt_mm"), 1)
                    pe.wait_ge(sem("pt_in"), done + 1)
                    if j >= 2:
                        pe.wait_ge(sem("o_in"), done - 1)
                    for i in range(heads):
                        v_ = {"A": O_VA, "B": O_VB + (h0 // 2 + i) * HD, "C": O_VC + (h0 + PAIRS[n][i]) * HD}[br]
                        for sbk in range(qb + 1):
                            last = mm(ps[:, 6 + j % 2, i * HD:(i + 1) * HD], pt[:, i, sbk, :], pj[:, sbk, v_:v_ + HD],
                                      start=sbk == 0, stop=sbk == qb)
                    last.then_inc(sem("o_mm"), 1)
                pe.wait_ge(sem("y_rows"), l + 1)
                for k in range(KD):
                    for b in range(NT):
                        last = nc.tensor.transpose(ps[:, 4 + k // 2, (k % 2) * T + b * P:(k % 2) * T + (b + 1) * P],
                                                   xn2[:, b, k * P:(k + 1) * P], ident)
                last.then_inc(sem("y_t"), 1)
                pe.wait_ge(sem("yT"), l + 1)
                out_proj(f"out2_{l}", hT)
                turn(f"f{l}", [])
                pe.wait_ge(sem("hT_ready"), 5 + 2 * l)
                if l == 0:
                    for c, entry in enumerate(PLAN["ff"][0]):
                        s = unit(entry)
                        chunk_mm(s, hidden + 2 * c + 2, c == 0, c == NCH - 1, outputs + 1)
                    hidden, outputs = hidden + 2 * NCH, outputs + 1
            router(rw2, E2, 1)
            entries, body, per_slot = PLAN["moe2"]
            with pe.Fori(0, E2) as e:
                for c, (s, _, f) in enumerate(entries):
                    pe.wait_ge(full[s], e * (DMA3 * per_slot[s]) + DMA3 * f)
                    chunk_mm(s, e * (2 * body) + hidden + 2 * c + 2, c == 0, c == body - 1, e + outputs + 1)

        @block.scalar
        def _(act):
            ac = nc.scalar.activation

            def sqrt_of(i, width, src, dst):
                act.wait_ge(sem("ms"), i)
                ac(dst, src, ACT.Sqrt).then_inc(sem("std"), 1)

            act.wait_ge(sem("cols"), 1)
            ac(cact[:, :], col("c", 0, 24), ACT.Silu).then_inc(sem("c_act"), 1)
            for i in range(2):
                act.wait_ge(sem("filter_a"), i + 1)
                ac(region(R_SQ + 512 + 256 * i, T)[0:64, :], region(R_SQ, T)[0:64, :], ACT.Sin).then_inc(sem("filter_h"), 1)
            act.wait_ge(sem("decay_in"), 16)
            ac(region(R_DEC, 2048), region(R_DEC, 2048), ACT.Abs)
            act.drain()
            for b in range(NT):
                if b:
                    act.wait_ge(sem("filter_h3"), b)
                ac(region(R_EXP, 2048), region(R_DEC, 2048), ACT.Exp, scale=const("tneg")[:, b:b + 1]).then_inc(sem("decay"), 1)
            act.wait_ge(sem("lam_in"), 1)
            ac(lamt[:, 0:4], lamt[:, 0:4], ACT.Exp).then_inc(sem("lam_exp"), 1)
            act.wait_ge(sem("ang_in"), 1)
            ac(sinn[:, :, :], ang[:, 2, :, :], ACT.Sin)
            ac(cosn[:, :, :], ang[:, 3, :, :], ACT.Sin).then_inc(sem("rope_in"), 1)
            act.wait_ge(sem("kn_in"), 1)
            ac(kn[:, :], kn[:, :], ACT.Sqrt).then_inc(sem("kn_sqrt"), 1)

            std = st[:, 2:4]
            sqrt_of(1, 2, st[:, 0:2], std)
            sqrt_of(2, 2, st[:, 0:2], std)

            for g, (dst, b0, bank) in enumerate(((z[:, 0:4], 0, 0), (z[:, 4:8], 4, 2), (z[:, 8:12], 8, 4), (z[:, 12:16], 16, 6),
                                                 (z[:, 16:20], 20, 0), (kc, 20, 2), (z[:, 20:24], 12, 4))):
                if g == 4:
                    act.wait_ge(sem("k_mm"), 1)
                else:
                    act.wait_ge(used, START["in1"] + g + (g < 4))
                for m in range(4):
                    last = ac(dst[:, m, :], ps[:, bank + m // 2, (m % 2) * T:(m % 2 + 1) * T], ACT.Identity, bias=col("bz", b0 + m))
                last.then_inc(sem("z_in"), 1)
            act.wait_ge(sem("vo_in"), 3)
            ac(og, og, ACT.Sigmoid).then_inc(sem("o_gate"), 1)

            act.wait_ge(sem("fnet_mm"), 1)
            ac(xn[:, :], all_ps[:, 0:2048], ACT.Copy).then_inc(sem("fnet_in"), 1)
            act.wait_ge(sem("fnet_mm"), 2)
            ac(z[:, ZFN:ZFN + 4, :], ps[:, 4:6, :].rearrange("p b (a n) -> p (b a) n", a=2), ACT.Copy).then_inc(sem("fnet_in"), 1)
            for o in range(2):
                act.wait_ge(sem("hy_t"), o + 1)
                ac(vt, ps[:, 0:2, :], ACT.Copy).then_inc(sem("hy_rows"), 1)

            _, gf, _, gm = (region(R_KF + i * 1024, 1024)[0:NH, :] for i in range(4))
            act.wait_ge(sem("ml_f"), 1)
            ac(gm, gf, ACT.Abs)
            act.drain()
            ac(gm, gm, ACT.Exp, scale=-1.0)
            act.drain()
            ac(gm, gm, ACT.Ln, bias=1.0).then_inc(sem("ml_softplus"), 1)
            act.wait_ge(sem("conv_qk"), 1)
            ac(z[:, ZQ:ZQ + 8, :], z[:, ZQ:ZQ + 8, :], ACT.Silu)
            ac(kc, kc, ACT.Silu).then_inc(sem("ml_silu"), 1)
            act.wait_ge(sem("ml_cols_mm"), 1)
            ac(en[:, :], ps[:, 1, 32:48], ACT.Exp, scale=-1.0).then_inc(sem("ml_cols"), 1)
            for j in range(8):
                act.wait_ge(sem("ml_w"), j + 1)
                w = xn[:, (j % 2) * 1024:(j % 2 + 1) * 1024]
                ac(w, w, ACT.Exp).then_inc(sem("ml_exp"), 1)
            sqrt_of(3, 8, st[:, 0:8], st[:, 8:16])
            act.wait_ge(sem("ml_t"), 1)
            ac(z[:, ZQ:ZQ + 4, :], ps[:, 2:4, :].rearrange("p b (a n) -> p (b a) n", a=2), ACT.Copy).then_inc(sem("ml_yT"), 1)

            for j in range(6):
                k, half = divmod(j, 2)
                act.wait_ge(sem("mg_mm"), j + 1)
                if j >= 2:
                    act.wait_ge(sem("merged"), j - 1)
                for m in range(4):
                    last = ac(sgm[:, j % 2, m, :], ps[:, 4 * (j % 2) + m // 2, (m % 2) * T:(m % 2 + 1) * T], ACT.Sigmoid,
                              bias=col("bg", k * 8 + half * 4 + m))
                last.then_inc(sem("mg_sig"), 1)

            def chunk_silu(n):
                for hb in range(2):
                    act.wait_ge(sem("gu_mm"), n - 1 + hb)
                    act.wait_ge(sem("act_ready"), n - 1 + hb)
                    ac(region(R_SG, 2, T)[:, hb, :], ps[:, hb, 0:T], ACT.Silu).then_inc(sem("gate_silu"), 1)

            sqrt_of(4, 2, st[:, 0:2], std)
            for b in range(NT):
                act.wait_ge(sem("rt_max"), b + 1)
                ac(rt[:, b, 24:28], rt[:, b, 0:4], ACT.Exp, bias=rt[:, b, 28:29], accum_out=rt[:, b, 29:30])
                ac(rt[:, b, 31:32], rt[:, b, 30:31], ACT.Exp).then_inc(sem("rt_exp"), 1)
            with act.Fori(0, E1) as e:
                chunk_silu(e * 2 + 2)
            hidden = 2 * E1
            sqrt_of(5, 2, st[:, 0:2], std)

            for l in range(2):
                sqrt_of(6 + 3 * l, 2, st[:, 0:2], std)
                for j, (c, w) in enumerate(IN2_COLS):
                    act.wait_ge(used, START[f"in2_{l}"] + j + 1)
                    bank = 2 * (j % 4)
                    ac(region(R_PJ, NT, D_IN)[:, :, c:c + w], ps[:, bank:bank + 2, 0:w], ACT.Copy).then_inc(sem("pj_in"), 1)
                n_t = -(-NFM // 4)
                fm = region(R_FM, NFM, T)
                for q in range(n_t):
                    act.wait_ge(sem("fm_mm"), n_t * l + q + 1)
                    n = min(4, NFM - 4 * q)
                    src = ps[:, 2 * (q % 2):2 * (q % 2) + 2, :].rearrange("p b (a n) -> p (b a) n", a=2)
                    ac(fm[:, 4 * q:4 * q + n, :], src[:, 0:n, :], ACT.Copy).then_inc(sem("fm_in"), 1)
                for qb in range(NT):
                    act.wait_ge(sem("ix_mm"), NT * l + qb + 1)
                    if qb:
                        act.wait_ge(sem("ix_used"), NT * l + qb)
                    ns = (qb + 1) * P
                    src = ps[:, 4 + 2 * qb:6 + 2 * qb, :].rearrange("p b (a n) -> p (b a) n", a=2)
                    ac(region(R_SM, 4, T)[:, :, 0:ns], src[:, :, 0:ns], ACT.Relu).then_inc(sem("ix_in"), 1)
                sm = region(R_SM, 2, 4, T)
                pt = region(R_PT, 4 * NT * P)

                def exps(j):
                    _, _, n, qb = JOBS[j]
                    ns = (qb + 1) * P
                    act.wait_ge(sem("row_max"), len(JOBS) * l + j + 1)
                    for i in range(n):
                        last = ac(sm[:, j % 2, i, 0:ns], sm[:, j % 2, i, 0:ns], ACT.Exp, bias=amx[:, j % 2, i:i + 1],
                                  accum_out=asum[:, j % 2, i:i + 1])
                    last.then_inc(sem("exped"), 1)

                exps(0)
                for j, (br, h0, n, qb) in enumerate(JOBS):
                    if j + 1 < len(JOBS):
                        exps(j + 1)
                    heads = n // 2 if br == "B" else n
                    act.wait_ge(sem("pt_mm"), len(JOBS) * l + j + 1)
                    if qb:
                        ac(pt[:, 0:heads * 2 * P], all_ps[:, 2048:2048 + heads * 2 * P], ACT.Copy).then_inc(sem("pt_in"), 1)
                    else:
                        ac(pt[:, 0:heads * 2 * P].rearrange("p (h s n) -> p h s n", s=2, n=P)[:, :, 0, :],
                           all_ps[:, 2048:2048 + heads * 2 * P].rearrange("p (h s n) -> p h s n", s=2, n=P)[:, :, 0, :],
                           ACT.Copy).then_inc(sem("pt_in"), 1)
                sqrt_of(7 + 3 * l, 8, st[:, 0:8], st[:, 8:16])
                act.wait_ge(sem("y_t"), l + 1)
                ac(hT[:, :, :], ps[:, 4:8, :].rearrange("p b (a n) -> p (b a) n", a=2), ACT.Copy).then_inc(sem("yT"), 1)
                sqrt_of(8 + 3 * l, 2, st[:, 0:2], std)
                if l == 0:
                    for c in range(NCH):
                        chunk_silu(hidden + 2 * c + 2)
                    hidden += 2 * NCH
            for b in range(NT):
                act.wait_ge(sem("rt_max"), NT + b + 1)
                ac(rt[:, b, 31:32], rt[:, b, 30:31], ACT.Exp).then_inc(sem("rt_exp"), 1)
            with act.Fori(0, E2 * NCH) as c:
                chunk_silu(c * 2 + hidden + 2)
            sqrt_of(12, 2, st[:, 0:2], std)

        @block.vector
        def _(dve):
            v = nc.vector
            fence = dve.drain

            def bc(ap, *shape):
                return ap.to_broadcast(list(shape))

            def reduce_angle(r, a, k):
                v.tensor_scalar(k, a, 1.0 / (2 * math.pi), ROUND, ALU.mult, ALU.add)
                fence()
                v.tensor_scalar(k, k, ROUND, None, ALU.subtract)
                fence()
                v.scalar_tensor_tensor(r, k, -TWO_PI[0], a, ALU.mult, ALU.add)
                fence()
                v.scalar_tensor_tensor(r, k, -TWO_PI[1], r, ALU.mult, ALU.add)
                fence()
                v.scalar_tensor_tensor(r, k, -TWO_PI[2], r, ALU.mult, ALU.add)
                fence()
                return v.tensor_scalar(r, r, PI, -PI, ALU.min, ALU.max)

            v.memset(dn[:, :], 0.0).then_inc(sem("act_ready"), 2)
            v.memset(st[:, :], 0.0).then_inc(sem("y_read"), 1)
            dve.wait_ge(sem("cols_t"), 1)
            total = sum(k for *_, k in COLS)
            v.tensor_copy(colv[:, 0:total], ps[:, 0, 0:total]).then_inc(sem("cols"), 1)

            dve.wait_ge(sem("filter_in"), 96)
            a, k = (region(R_SQ + i * 256 + 1024, T)[0:64, :] for i in range(2))
            for i in range(2):
                dve.wait_ge(sem("filter_mm"), i + 1)
                v.tensor_scalar(a, ps[0:64, 1 + i, 0:T], fcol[:, i:i + 1], fcol[:, 2:3], ALU.add, ALU.mult)
                fence()
                reduce_angle(region(R_SQ, T)[0:64, :], a, k).then_inc(sem("filter_a"), 1)
            h3 = region(R_H3, NT, 2, 2, DBR)
            for b in range(NT):
                dve.wait_ge(sem("filter_mm"), 3 + b)
                dve.wait_ge(sem("decay"), b + 1)
                v.tensor_tensor(region(R_H3, NT, 2048)[:, b, :], all_ps[:, 2048:4096], region(R_EXP, 2048), ALU.mult
                                ).then_inc(sem("filter_h3"), 1)
            fence()
            v.memset(h3[0:1, 0, :, 1, :], 0.0)
            dve.wait_ge(sem("rows_in"), 16 * N_ROWS_IN)
            for l in range(2):
                for i in range(2):
                    v.tensor_tensor_reduce(lamj[:, :], lamr[:, l, 2 * i, :], lamr[:, l, 2 * i + 1, :], 1.0, 0.0,
                                           ALU.mult, ALU.add, lamt[:, 2 * l + i:2 * l + i + 1])
                    fence()
            v.tensor_copy(posf[:, :], posi[:, :]).then_inc(sem("lam_in"), 1)
            fence()
            for b in range(NT):
                v.tensor_scalar(ang[:, 0, b, :], const("inv"), posf[:, b:b + 1], None, ALU.mult)
            fence()
            reduce_angle(ang[:, 2, :, :], ang[:, 0, :, :], ang[:, 1, :, :])
            fence()
            v.scalar_tensor_tensor(ang[:, 3, :, :], ang[:, 2, :, :], -1.0, ang[:, 2, :, :], ALU.mult, ALU.max)
            fence()
            v.tensor_scalar(ang[:, 3, :, :], ang[:, 3, :, :], -1.0, math.pi / 2, ALU.mult, ALU.add).then_inc(sem("ang_in"), 1)
            v.tensor_tensor(region(R_SQ, 4096), region(R_H3, 4096), region(R_H3, 4096), ALU.mult).then_inc(sem("filter_sq"), 1)
            pq = region(R_PQ, NT, 2, 2, DBR)
            for o in range(2):
                v.tensor_tensor(pq[:, :, o, 0, :], h3[:, :, o, 0, :], h3[:, :, o, 1, :], ALU.add)
                last = v.tensor_tensor(pq[:, :, o, 1, :], h3[:, :, o, 1, :], h3[:, :, o, 0, :], ALU.subtract)
            last.then_inc(sem("filter_pq"), 1)
            dve.wait_ge(sem("filter_ssum"), 1)
            v.tensor_scalar(kn[:, :], ps[:, 1, 0:8], EPS, None, ALU.add).then_inc(sem("kn_in"), 1)
            dve.wait_ge(sem("kn_sqrt"), 1)
            v.reciprocal(kn[:, :], kn[:, :])
            dve.wait_ge(sem("lam_exp"), 1)
            for l in range(2):
                v.tensor_scalar(lamt[:, 4 + l:5 + l], lamt[:, 2 * l:2 * l + 1], lamt[:, 2 * l + 1:2 * l + 2], LAM_INIT[l],
                                ALU.subtract, ALU.add)
            dve.wait_ge(sem("spectra_mm"), 1)
            v.tensor_copy(region(R_KF, 4096), all_ps[:, :]).then_inc(sem("spectra_in"), 1)
            v.memset(v1[:, :, :, P:P + 1], 1.0)

            def ada(a, n1, n2):
                dve.wait_ge(used, START[f"ada{a}"] + 12)
                if a == 0:
                    both = ps[:, 0, 0:96].rearrange("p (c i) -> p c i", i=2)
                    v.tensor_tensor(mod[:, :], both[:, :, 0], col("ab0", 0, 48), ALU.add)
                    v.tensor_tensor(modc[:, :], both[:, 0:16, 1], col("ab0", 0, 16), ALU.add)
                    fence()
                    v.scalar_tensor_tensor(gac[:, :], modc[:, 8:16], 1.0, col(n1, 0, 8), ALU.add, ALU.mult)
                else:
                    v.tensor_tensor(mod[:, :], ps[:, 0, 0:48], col(f"ab{a}", 0, 48), ALU.add)
                    fence()
                v.scalar_tensor_tensor(ga[:, 0:8], mod[:, 8:16], 1.0, col(n1, 0, 8), ALU.add, ALU.mult)
                v.scalar_tensor_tensor(ga[:, 8:16], mod[:, 32:40], 1.0, col(n2, 0, 8), ALU.add, ALU.mult)
                for g in range(16):
                    c = 16 + g if g < 8 else 32 + g
                    last = v.tensor_scalar(xn[:, g * P:(g + 1) * P], ident, mod[:, c:c + 1], None, ALU.mult)
                last.then_inc(sem("diag"), 1)
                dve.wait_ge(sem("gaterow_mm"), a + 1)
                v.tensor_copy(grow[:, :, :].rearrange("p a n -> p (a n)"), all_ps[:, 1024:3072]).then_inc(sem("gaterow_in"), 1)

            def rstd(i, src):
                for b in range(NT):
                    v.tensor_tensor_reduce(xn2[:, b, :], src[:, b, :], src[:, b, :], 1.0, 0.0, ALU.mult, ALU.add, st[:, b:b + 1])
                fence()
                v.tensor_scalar(st[:, 0:2], st[:, 0:2], 1.0 / D, EPS, ALU.mult, ALU.add).then_inc(sem("ms"), 1)
                dve.wait_ge(sem("std"), i)
                v.reciprocal(st[:, 4:6], st[:, 2:4])
                fence()

            def norm(i, src, n, dst, gain, shift):
                rstd(i, src)
                for b in range(NT):
                    last = v.tensor_scalar(xn2[:, b, :], src[:, b, :], st[:, 4 + b:5 + b], None, ALU.mult)
                last.then_inc(sem("normed"), 1)
                dve.wait_ge(sem("turned"), n)
                for k in range(KD):
                    last = v.tensor_scalar(dst[:, k, :], ps[:, 4 + k // 2, (k % 2) * T:(k % 2 + 1) * T],
                                           gain[:, k:k + 1], shift[:, k:k + 1], ALU.mult, ALU.add)
                last.then_inc(sem("hT_ready"), 1)

            ada(0, "n1", "n2")
            dve.wait_ge(sem("ctx_in"), 16)
            norm(1, hT[:, :, :].rearrange("p k n -> p (k n)").rearrange("p (b d) -> p b d", b=NT), 1, hTc, gac, modc)
            dve.wait_ge(sem("x_in"), 16)
            norm(2, x, 2, hT, ga, mod)

            def conv(j0, count, w, wcount, bias):
                acc = xn[:, 0:2 * T].rearrange("p (a r c) -> p a r c", a=2, c=GW)
                with dve.Fori(0, count // 2) as i:
                    blocks = (i, i + count // 2)
                    grids = [z[:, bass.ds(b + j0, 1), :].rearrange("p a (r c) -> p (a r) c", c=GW) for b in blocks]
                    for a, b in enumerate(blocks):
                        v.tensor_copy(acc[:, a], bc(colv[:, bass.ds(b + COL[bias], 1)].unsqueeze(2), P, GR, GW))
                    fence()
                    for dr in (-1, 0, 1):
                        for dc in (-1, 0, 1):
                            if dr == dc == 0:
                                continue
                            ro, co = slice(max(0, -dr), GR - max(0, dr)), slice(max(0, -dc), GW - max(0, dc))
                            ri, ci = slice(max(0, dr), GR - max(0, -dr)), slice(max(0, dc), GW - max(0, -dc))
                            tap = ((dr + 1) * 3 + dc + 1) * wcount + COL[w]
                            for a, b in enumerate(blocks):
                                v.scalar_tensor_tensor(acc[:, a, ro, co], grids[a][:, ri, ci], colv[:, bass.ds(b + tap, 1)],
                                                       acc[:, a, ro, co], ALU.mult, ALU.add)
                            fence()
                    for a, b in enumerate(blocks):
                        v.scalar_tensor_tensor(grids[a], grids[a], colv[:, bass.ds(b + 4 * wcount + COL[w], 1)], acc[:, a],
                                               ALU.mult, ALU.add)
                    fence()

            dve.wait_ge(sem("z_in"), 3)
            conv(0, 12, "hcw", 12, "hcb")
            v.memset(dn[:, 4:5], 0.0).then_inc(sem("hy_u"), 1)
            dve.wait_ge(sem("vo_mm"), 1)
            for i, (sb0, bank) in enumerate(((2, 6), (0, 0))):
                if i:
                    dve.wait_ge(used, START["in1"] + 7)
                for b in range(NT):
                    last = v.tensor_tensor(v1[:, sb0 + b, :, 0:P], ps[:, bank + b, :].rearrange("p (h n) -> p h n", h=NH),
                                           rowv[:, 0:DBR].rearrange("p (h n) -> p h n", h=NH), ALU.add)
                last.then_inc(sem("vo_in"), 1)
            dve.wait_ge(used, START["in1"] + 8)
            for b in range(NT):
                last = v.tensor_tensor(og[:, b, :], ps[:, 2 + b, :], rowv[:, DBR:2 * DBR], ALU.add)
            last.then_inc(sem("vo_in"), 1)

            dve.wait_ge(sem("gates_mm"), 1)
            for g in range(4):
                last = v.tensor_scalar(gates[:, g % 2, g // 2, :], ps[0:NH, 4 + g, :], gb[:, g:g + 1], None, ALU.add)
            last.then_inc(sem("vo_in"), 1)

            yy = xn[:, :].rearrange("p (r n) -> p r n", r=2)
            dve.wait_ge(sem("fnet_mm"), 2)
            flat_vt = region(R_VT, 1024)
            for o in range(2):
                dve.wait_ge(sem("hy_spec"), o + 1)
                ur, us = all_ps[:, 0:1024], all_ps[:, 1024:2048]
                kr, ki = (kf[:, o, r, :] for r in range(2))
                v.tensor_tensor(yy[:, 0, :], ur, kr, ALU.mult)
                v.tensor_tensor(flat_vt, us, ki, ALU.mult)
                v.tensor_tensor(yy[:, 1, :], ur, ki, ALU.mult)
                fence()
                v.tensor_tensor(yy[:, 0, :], yy[:, 0, :], flat_vt, ALU.add)
                fence()
                v.tensor_tensor(flat_vt, us, kr, ALU.mult)
                fence()
                v.tensor_tensor(yy[:, 1, :], yy[:, 1, :], flat_vt, ALU.subtract).then_inc(sem("hy_y"), 1)
                fence()
                vt4 = region(R_VT, NBR, T)
                for c in range(NBR):
                    v.tensor_scalar(vt4[:, c, :], z[:, c, :], col("skip", o * NBR + c), None, ALU.mult)
                dve.wait_ge(sem("hy_inv"), o + 1)
                fence()
                for c in range(NBR):
                    v.scalar_tensor_tensor(vt4[:, c, :], ps[:, 6 + c // 2, (c % 2) * T:(c % 2 + 1) * T],
                                           kn[:, o * NBR + c:o * NBR + c + 1], vt4[:, c, :], ALU.mult, ALU.add)
                fence()
                v.tensor_tensor(z[:, 0:4, :], vt4, z[:, 4 * (o + 1):4 * (o + 2), :], ALU.mult).then_inc(sem("hy_u"), 1)

            fence()
            gi, gf, gB, gm = (region(R_KF + i * 1024, 2, 512)[0:NH] for i in range(4))
            v.tensor_copy(gf, gates[:, 1, :, :]).then_inc(sem("ml_f"), 1)
            v.tensor_copy(gi, gates[:, 0, :, :])
            fence()
            v.tensor_scalar(gates[:, 1, :, :], gf, 0.0, None, ALU.min)
            dve.wait_ge(sem("ml_softplus"), 1)
            fence()
            v.tensor_tensor(gf, gates[:, 1, :, :], gm, ALU.subtract)
            fence()
            v.memset(gm, 0.0)
            fence()

            def scans(dst, src, op, second):
                v.tensor_tensor_scan(dst[:, 0, :], src[:, 0, :], second(src[:, 0, :]), 0.0, op, op)
                v.tensor_tensor_scan(dst[:, 1, 0:T][:, ::-1], src[:, 1, 0:T][:, ::-1], second(src[:, 1, 0:T][:, ::-1]), 0.0, op, op)
                fence()
                v.tensor_tensor_scan(dst[:, 1, T:2 * T][:, ::-1], src[:, 1, T:2 * T][:, ::-1],
                                     second(src[:, 1, T:2 * T][:, ::-1]), dst[:, 1, 0:1], op, op)
                fence()

            scans(gB, gf, ALU.add, lambda s: gm[:, 0, 0:s.shape[-1]])
            v.tensor_tensor(gi, gi, gB, ALU.subtract)
            fence()
            scans(gm, gi, ALU.max, lambda s: s)
            v.tensor_tensor(gf, gB, gm, ALU.add).then_inc(sem("ml_gates"), 1)

            conv(ZQ, 8, "mcw", 8, "mcb")
            acc = xn[:, 0:4 * T].rearrange("p (h n) -> p h n", h=NH)
            for h in range(NH):
                v.tensor_scalar(acc[:, h, :], kc[:, h, :], col("mcw", 4 * 8 + 4 + h), col("mcb", 4 + h), ALU.mult, ALU.add)
            fence()
            for tap, (o, i) in ((3, (slice(1, T), slice(0, T - 1))), (5, (slice(0, T - 1), slice(1, T)))):
                for h in range(NH):
                    v.scalar_tensor_tensor(acc[:, h, o], kc[:, h, i], col("mcw", tap * 8 + 4 + h), acc[:, h, o], ALU.mult, ALU.add)
                fence()
            v.tensor_copy(kc, acc).then_inc(sem("conv_qk"), 1)
            dve.wait_ge(sem("ml_silu"), 1)
            v.tensor_scalar(z[:, ZQ:ZQ + 4, :], z[:, ZQ:ZQ + 4, :], float(P) ** -0.5, None, ALU.mult).then_inc(sem("ml_qk"), 1)
            dve.wait_ge(sem("ml_cols_mm"), 1)
            v.tensor_copy(gcol[:, :], ps[:, 0, 0:32]).then_inc(sem("ml_cols"), 1)
            dve.wait_ge(sem("ml_cols"), 2)
            fence()

            hh = region(R_VT, NT, NH, P)

            def weight_args(j):
                h, d = divmod(j, 2)
                w = xn[:, (j % 2) * 1024:(j % 2 + 1) * 1024].rearrange("p (s n) -> p s n", s=4)
                if j >= 2:
                    dve.wait_ge(sem("ml_pv"), j - 1)
                for s in range(4):
                    c = (d * 4 + s) * 4 + h
                    last = v.tensor_scalar(w[:, s, :], ps[:, 2 + 2 * d + h // 2, (h % 2) * T:(h % 2 + 1) * T], gcol[:, c:c + 1], 0.0,
                                           ALU.add, ALU.min)
                last.then_inc(sem("ml_w"), 1)

            weight_args(0)
            for j in range(8):
                h, d = divmod(j, 2)
                if j + 1 < 8:
                    weight_args(j + 1)
                w = xn[:, (j % 2) * 1024:(j % 2 + 1) * 1024]
                dve.wait_ge(sem("ml_exp"), j + 1)
                v.tensor_tensor(w[:, 512:1024], w[:, 512:1024], const(("upto", "from")[d]), ALU.mult)
                dve.wait_ge(sem("ml_s"), h + 1)
                fence()
                v.tensor_tensor(w, w, all_ps[:, 3072:4096], ALU.mult).then_inc(sem("ml_p"), 1)
                dve.wait_ge(sem("ml_pv"), j + 1)
                den = ps[:, j % 2, :].rearrange("p (b n) -> p b n", b=NT)
                v.tensor_scalar(dn[:, 4:6], den[:, :, P], -1.0, None, ALU.mult)
                fence()
                for b in range(NT):
                    o = (d * 2 + b) * 4 + h
                    v.tensor_scalar(dn[:, b:b + 1], den[:, b, P:P + 1], dn[:, 4 + b:5 + b], en[:, o:o + 1], ALU.max, ALU.max)
                fence()
                v.reciprocal(dn[:, 2:4], dn[:, 0:2])
                fence()
                for b in range(NT):
                    if d == 0:
                        last = v.tensor_scalar(hh[:, b, h, :], den[:, b, 0:P], dn[:, 2 + b:3 + b], None, ALU.mult)
                    else:
                        last = v.scalar_tensor_tensor(hh[:, b, h, :], den[:, b, 0:P], dn[:, 2 + b:3 + b], hh[:, b, h, :],
                                                      ALU.mult, ALU.add)
                last.then_inc(sem("ml_h"), 1)
            fence()
            flat = region(R_VT, 8, P)
            sqs = xn[:, 0:1024].rearrange("p (a n) -> p a n", a=8)
            v.tensor_tensor(sqs, flat, flat, ALU.mult)
            fence()
            v.tensor_reduce(st[:, 0:8], sqs, AX.X, ALU.add)
            fence()
            v.tensor_scalar(st[:, 0:8], st[:, 0:8], 1.0 / P, EPS, ALU.mult, ALU.add).then_inc(sem("ms"), 1)
            dve.wait_ge(sem("std"), 3)
            v.reciprocal(st[:, 8:16], st[:, 8:16])
            fence()
            v.tensor_tensor(flat, flat, bc(st[:, 8:16].unsqueeze(2), P, 8, P), ALU.mult)
            fence()
            v.tensor_tensor(vt, vt, bc(mlnw[:, :].unsqueeze(1), P, NT, DBR), ALU.mult)
            dve.wait_ge(sem("o_gate"), 1)
            fence()
            v.tensor_tensor(vt, vt, og, ALU.mult).then_inc(sem("ml_y"), 1)

            for j in range(6):
                k, half = divmod(j, 2)
                dve.wait_ge(used, START["merge"] + j + 1)
                dve.wait_ge(sem("mg_sig"), j + 1)
                base = 4 * (j % 2) + 2
                proj = ps[:, base:base + 2, :].rearrange("p b (a n) -> p (b a) n", a=2)
                part = macc[:, half * 4:half * 4 + 4, :]
                if k == 0:
                    v.tensor_tensor(part, sgm[:, j % 2], proj, ALU.mult).then_inc(sem("merged"), 1)
                else:
                    v.tensor_tensor(sgm[:, j % 2], sgm[:, j % 2], proj, ALU.mult)
                    fence()
                    v.tensor_tensor(part, part, sgm[:, j % 2], ALU.add).then_inc(sem("merged"), 1)

            def out_add(stage):
                for half in range(2):
                    h = slice(half * 512, (half + 1) * 512)
                    dve.wait_ge(used, START[stage] + half + 1)
                    v.tensor_tensor(xn2[:, :, h], ps[:, 2 * half:2 * half + 2, :], bc(grow[:, 0, h].unsqueeze(1), P, NT, 512), ALU.mult)
                    fence()
                    v.tensor_tensor(x[:, :, h], x[:, :, h], xn2[:, :, h], ALU.add)
                fence()

            def first_of(dst, val, m, n, eq, cs):
                v.tensor_scalar(eq, val, m, None, ALU.is_equal)
                fence()
                v.tensor_tensor_scan(cs, eq, const("zero")[:, 0:n], 0.0, ALU.add, ALU.add)
                fence()
                v.scalar_tensor_tensor(dst, cs, 1.0, eq, ALU.is_equal, ALU.mult)
                fence()

            def top2(b, val, n):
                r = rt[:, b, :]
                v.tensor_reduce(r[:, 32:33], val, AX.X, ALU.max)
                fence()
                first_of(r[:, 48:48 + n], val, r[:, 32:33], n, r[:, 64:64 + n], r[:, 72:72 + n])
                v.scalar_tensor_tensor(r[:, 80:80 + n], r[:, 48:48 + n], TAKEN, val, ALU.mult, ALU.add)
                fence()
                v.tensor_reduce(r[:, 33:34], r[:, 80:80 + n], AX.X, ALU.max)
                fence()
                first_of(r[:, 56:56 + n], r[:, 80:80 + n], r[:, 33:34], n, r[:, 64:64 + n], r[:, 72:72 + n])
                v.tensor_tensor(r[:, 30:31], r[:, 33:34], r[:, 32:33], ALU.subtract).then_inc(sem("rt_max"), 1)

            def top2_weights(b, n, scale, dst):
                r = rt[:, b, :]
                v.tensor_scalar(r[:, 34:35], r[:, 31:32], 1.0, None, ALU.add)
                fence()
                v.reciprocal(r[:, 35:36], r[:, 34:35])
                fence()
                if scale is not None:
                    v.tensor_tensor(r[:, 35:36], r[:, 35:36], scale, ALU.mult)
                    fence()
                v.tensor_tensor(r[:, 36:37], r[:, 35:36], r[:, 31:32], ALU.mult)
                fence()
                v.tensor_scalar(r[:, 64:64 + n], r[:, 48:48 + n], r[:, 35:36], None, ALU.mult)
                fence()
                v.scalar_tensor_tensor(dst, r[:, 56:56 + n], r[:, 36:37], r[:, 64:64 + n], ALU.mult, ALU.add)
                fence()

            def router1():
                dve.wait_ge(sem("router_mm"), 1)
                for b in range(NT):
                    r = rt[:, b, :]
                    v.tensor_tensor(r[:, 0:20], ps[:, 3, b * 32:b * 32 + 20], rb1[:, :], ALU.add)
                    fence()
                    v.tensor_reduce(r[:, 38:39], r[:, 0:4], AX.X, ALU.max)
                    fence()
                    v.tensor_scalar(r[:, 28:29], r[:, 38:39], -1.0, None, ALU.mult)
                    first_of(r[:, 40:44], r[:, 0:4], r[:, 38:39], 4, r[:, 64:68], r[:, 72:76])
                    v.tensor_scalar(r[:, 44:48], r[:, 4:8], r[:, 40:41], None, ALU.mult)
                    for g in range(1, 4):
                        fence()
                        v.scalar_tensor_tensor(r[:, 44:48], r[:, 4 + 4 * g:8 + 4 * g], r[:, 40 + g:41 + g], r[:, 44:48],
                                               ALU.mult, ALU.add)
                    fence()
                    top2(b, r[:, 44:48], 4)
                for b in range(NT):
                    r = rt[:, b, :]
                    dve.wait_ge(sem("rt_exp"), b + 1)
                    v.reciprocal(r[:, 39:40], r[:, 29:30])
                    fence()
                    top2_weights(b, 4, r[:, 39:40], r[:, 88:92])
                    for g in range(4):
                        v.tensor_scalar(comb[:, b, 4 * g:4 * g + 4], r[:, 88:92], r[:, 40 + g:41 + g], None, ALU.mult)

            def router2():
                dve.wait_ge(sem("router_mm"), 2)
                for b in range(NT):
                    v.tensor_copy(rt[:, b, 0:E2], ps[:, 3, b * 32:b * 32 + E2])
                fence()
                for b in range(NT):
                    top2(b, rt[:, b, 0:E2], E2)
                for b in range(NT):
                    dve.wait_ge(sem("rt_exp"), NT + b + 1)
                    top2_weights(b, E2, None, comb[:, b, 0:E2])

            ya = region(R_YA, NT, D)

            def chunk_act(n):
                for hb in range(2):
                    dve.wait_ge(sem("gate_silu"), n - 1 + hb)
                    v.tensor_tensor(region(R_AT, 2, T)[:, hb, :], region(R_SG, 2, T)[:, hb, :], ps[:, hb, T:2 * T], ALU.mult
                                    ).then_inc(sem("act_ready"), 1)

            def expert_add(e, count):
                fence()
                dve.wait_ge(used, count)
                for b in range(NT):
                    last = v.scalar_tensor_tensor(ya[:, b, :], all_ps[:, 2048 + b * 1024:3072 + b * 1024],
                                                  comb[:, b, bass.ds(e, 1)], ya[:, b, :], ALU.mult, ALU.add)
                last.then_inc(sem("y_read"), 1)

            def ffn_add(src):
                v.tensor_tensor(xn2, src, bc(grow[:, 1, :].unsqueeze(1), P, NT, D), ALU.mult).then_inc(sem("y_read"), 1)
                fence()
                return v.tensor_tensor(x[:, :, :], x[:, :, :], xn2, ALU.add)

            out_add("out1")
            norm(4, x, 3, hT, ga[:, 8:16], mod[:, 24:32])
            v.memset(ya, 0.0)
            router1()
            with dve.Fori(0, E1) as e:
                chunk_act(e * 2 + 2)
                expert_add(e, e + START["moe1"] + 1)
            hidden = 2 * E1
            fence()
            ffn_add(ya).then_inc(sem("block_done"), 1)
            fence()
            rstd(5, x)
            dve.wait_ge(sem("late_in"), 32)
            for b in range(NT):
                v.scalar_tensor_tensor(x[:, b, :], x[:, b, :], st[:, 4 + b:5 + b], late[:, 0:D], ALU.mult, ALU.mult)
            fence()

            for l in range(2):
                ada(l + 1, f"ga{l}", f"gf{l}")
                norm(6 + 3 * l, x, 4 + 2 * l, hT, ga, mod)
                pj = region(R_PJ, NT, D_IN)
                dve.wait_ge(sem("pj_in"), 6 * (l + 1))
                spans = ((O_QA, A_H + 1, HD, 8, 0), (O_QI, 5, HD, 8, 0), (O_QB, 16, 32, 4, 8), (O_QC, 2 * C_H, HD, 8, 0))
                for b in range(NT):
                    at, parts = R_SM + b * 1024, []
                    for off, heads, w, half, f in spans:
                        n = heads * half
                        heads_ = pj[:, b, off:off + heads * w].rearrange("p (h n) -> p h n", n=w)
                        x1, x2 = heads_[:, :, 0:half], heads_[:, :, half:2 * half]
                        c_, s_ = (bc(t[:, b, f:f + half].unsqueeze(1), P, heads, half) for t in (cosn, sinn))
                        t_ = [region(at + i * n, heads, half) for i in range(4)]
                        at += 4 * n
                        for t, a_, w_ in zip(t_, (x1, x2, x2, x1), (c_, s_, c_, s_)):
                            v.tensor_tensor(t, a_, w_, ALU.mult)
                        parts.append((x1, x2, t_))
                    fence()
                    for x1, x2, t_ in parts:
                        v.tensor_tensor(x1, t_[0], t_[1], ALU.subtract)
                        last = v.tensor_tensor(x2, t_[2], t_[3], ALU.add)
                    v.tensor_scalar(wix[:, b, :], pj[:, b, O_WI:O_WI + 4], 0.5 * 0.125, None, ALU.mult)
                last.then_inc(sem("roped"), 1)
                fence()
                dve.wait_ge(sem("fm_in"), -(-NFM // 4) * (l + 1))
                fm = region(R_FM, NFM, T)
                for i in range(2 * B_H):
                    last = v.tensor_scalar(hT[:, i, :], fm[:, FM_QB + i // 4, :], const("quarter")[:, i % 4:i % 4 + 1], None, ALU.mult)
                last.then_inc(sem("qb_masked"), 1)

                causal = const2("causal")
                sel = region(R_SEL, 2, T)
                for qb in range(NT):
                    ns = (qb + 1) * P
                    dve.wait_ge(sem("ix_in"), NT * l + qb + 1)
                    rel = region(R_SM, 4, T)
                    sc = [region(R_IX, 2, T)[:, i, 0:ns] for i in range(2)]
                    v.tensor_scalar(sc[0], rel[:, 0, 0:ns], wix[:, qb, 0:1], None, ALU.mult)
                    for h in range(1, 4):
                        fence()
                        last = v.scalar_tensor_tensor(sc[0], rel[:, PAIRS[4][h], 0:ns], wix[:, qb, h:h + 1], sc[0], ALU.mult, ALU.add)
                    last.then_inc(sem("ix_used"), 1)
                    fence()
                    v.tensor_tensor(sc[0], sc[0], causal[:, qb, 0:ns], ALU.add)
                    for i in range(TOPK // 8):
                        fence()
                        v.max(top[:, :], sc[i % 2])
                        fence()
                        v.match_replace(sc[(i + 1) % 2], top[:, :], sc[i % 2], TAKEN)
                    fence()
                    v.tensor_scalar(sc[1], sc[0], TAKEN / 1.5, MASKED, ALU.is_gt, ALU.mult)
                    fence()
                    v.tensor_tensor(sel[:, qb, 0:ns], sc[1], causal[:, qb, 0:ns], ALU.add)
                    fence()

                sm = region(R_SM, 2, 4, T)

                def mask_scores(j):
                    br, h0, n, qb = JOBS[j]
                    ns = (qb + 1) * P
                    dve.wait_ge(sem("s_mm"), len(JOBS) * l + j + 1)
                    if j >= 2:
                        dve.wait_ge(sem("pt_mm"), len(JOBS) * l + j - 1)
                    scale = float(32 if br == "B" else HD) ** -0.5
                    mask = (sel if br == "A" else causal)[:, qb, 0:ns]
                    bank = 2 * (j % 2)
                    s_ = ps[:, bank:bank + 2, :].rearrange("p b (a n) -> p (b a) n", a=2)
                    s_ = s_[:, 0:n, 0:ns] if br == "B" or n == 4 else s_[:, 0:4:2, 0:ns]
                    v.scalar_tensor_tensor(sm[:, j % 2, 0:n, 0:ns], s_, scale, bc(mask.unsqueeze(1), P, n, ns), ALU.mult, ALU.add
                                           ).then_inc(sem("masked"), 1)
                    fence()
                    v.tensor_reduce(amx[:, j % 2, 0:n], sm[:, j % 2, 0:n, 0:ns], AX.X, ALU.max)
                    fence()
                    v.tensor_scalar(amx[:, j % 2, 0:n], amx[:, j % 2, 0:n], -1.0, None, ALU.mult).then_inc(sem("row_max"), 1)

                def probs(j):
                    br, h0, n, qb = JOBS[j]
                    ns = (qb + 1) * P
                    fence()
                    dve.wait_ge(sem("exped"), len(JOBS) * l + j + 1)
                    last = v.reciprocal(ars[:, j % 2, 0:n], asum[:, j % 2, 0:n])
                    if br == "B":
                        fence()
                        for i in range(0, n, 2):
                            v.tensor_scalar(sm[:, j % 2, i + 1, 0:ns], sm[:, j % 2, i + 1, 0:ns], ars[:, j % 2, i + 1:i + 2],
                                            lamt[:, 4 + l:5 + l], ALU.mult, ALU.mult)
                        fence()
                        for i in range(0, n, 2):
                            last = v.scalar_tensor_tensor(sm[:, j % 2, i, 0:ns], sm[:, j % 2, i, 0:ns], ars[:, j % 2, i:i + 1],
                                                          sm[:, j % 2, i + 1, 0:ns], ALU.mult, ALU.subtract)
                    last.then_inc(sem("probs"), 1)

                def outputs_in(j):
                    br, h0, n, qb = JOBS[j]
                    dve.wait_ge(sem("o_mm"), len(JOBS) * l + j + 1)
                    heads = n // 2 if br == "B" else n
                    c = {"A": h0 * HD, "B": A_H * HD + h0 // 2 * HD, "C": (A_H + B_H + h0) * HD}[br]
                    dst = xn2[:, qb, c:c + heads * HD].rearrange("p (h n) -> p h n", n=HD)
                    src = ps[:, 6 + j % 2, 0:heads * HD].rearrange("p (h n) -> p h n", n=HD)
                    if br == "B":
                        last = v.tensor_copy(dst, src)
                    elif n == 2:
                        last = v.tensor_tensor(dst, src, bc(ars[:, j % 2, 0:n].unsqueeze(2), P, n, HD), ALU.mult)
                    else:
                        last = v.tensor_tensor(dst.rearrange("p (a b) n -> p b a n", a=2), src.rearrange("p (b a) n -> p b a n", b=2),
                                               bc(ars[:, j % 2, 0:4].rearrange("p (b a) -> p b a", b=2).unsqueeze(3), P, 2, 2, HD),
                                               ALU.mult)
                    last.then_inc(sem("o_in"), 1)

                mask_scores(0)
                for j in range(len(JOBS)):
                    if j + 1 < len(JOBS):
                        mask_scores(j + 1)
                    probs(j)
                    if j:
                        outputs_in(j - 1)
                outputs_in(len(JOBS) - 1)
                fence()
                yb = xn2[:, :, A_H * HD:(A_H + B_H) * HD]
                sq2 = region(R_SM, NT, B_H * HD)
                v.tensor_tensor(sq2, yb, yb, ALU.mult)
                fence()
                v.tensor_reduce(st[:, 0:8], region(R_SM, 8, HD), AX.X, ALU.add)
                fence()
                v.tensor_scalar(st[:, 0:8], st[:, 0:8], 1.0 / HD, SUB_EPS, ALU.mult, ALU.add).then_inc(sem("ms"), 1)
                dve.wait_ge(sem("std"), 7 + 3 * l)
                v.reciprocal(st[:, 8:16], st[:, 8:16])
                fence()
                for b in range(NT):
                    yb_ = yb[:, b, :].rearrange("p (h n) -> p h n", n=HD)
                    v.tensor_tensor(yb_, yb_, bc(st[:, 8 + 4 * b:12 + 4 * b].unsqueeze(2), P, B_H, HD), ALU.mult)
                fence()
                for b in range(NT):
                    yb_ = yb[:, b, :].rearrange("p (h n) -> p h n", n=HD)
                    last = v.scalar_tensor_tensor(yb_, yb_, 1.0 - LAM_INIT[l], bc(subln[:, l, :].unsqueeze(1), P, B_H, HD),
                                                  ALU.mult, ALU.mult)
                last.then_inc(sem("y_rows"), 1)

                out_add(f"out2_{l}")
                norm(8 + 3 * l, x, 5 + 2 * l, hT, ga[:, 8:16], mod[:, 24:32])
                if l == 0:
                    for c in range(NCH):
                        chunk_act(hidden + 2 * c + 2)
                    dve.wait_ge(used, START["ff"] + NCH)
                    hidden += 2 * NCH
                    ffn_add(ps[:, 4:8, :].rearrange("p (b a) n -> p b (a n)", b=NT)).then_inc(sem("block_done"), 1)
                    fence()
            v.memset(ya, 0.0)
            router2()
            with dve.Fori(0, E2) as e:
                for c in range(NCH):
                    chunk_act(e * (2 * NCH) + hidden + 2 * c + 2)
                expert_add(e, e * NCH + START["moe2"] + NCH)
            fence()
            ffn_add(ya)
            fence()
            rstd(12, x)
            dve.wait_ge(sem("late_in"), 32)
            for b in range(NT):
                last = v.scalar_tensor_tensor(xn2[:, b, :], x[:, b, :], st[:, 4 + b:5 + b], late[:, D:2 * D], ALU.mult, ALU.mult)
            last.then_inc(sem("y_final"), 1)


_INS = ["x", "c", "ctx", "c_ctx", "ada_w", "ada_b", "norm1_w", "norm2_w", "w_in", "b_in", "hy_conv_w", "hy_conv_b", "hy_f_w1",
        "hy_f_b1", "hy_f_w2", "hy_f_b2", "hy_f_w3", "hy_f_freq", "hy_decay", "hy_skip", "ml_conv_w", "ml_conv_b",
        "ml_norm_w", "w_branch", "w_out", "moe_rg_w", "moe_rg_b", "moe_re_w", "moe_re_b", "moe_w_gate", "moe_w_up",
        "moe_w_down", "norm_f_w", "c_2", "positions_2", "w_in_2", "w_out_2", "diff_lambda_2", "diff_subln_2",
        "w_ada_2", "b_ada_2", "g_attn_2", "g_ffn_2", "w_ff_gate_2", "w_ff_up_2", "w_ff_down_2", "w_router_2",
        "w_exp_gate_2", "w_exp_up_2", "w_exp_down_2", "g_final_2"]


def kernel(**inputs):
    import concourse.bacc as bacc
    from concourse.bass_utils import run_bass_kernel_spmd

    nc = bacc.Bacc("TRN2", target_bir_lowering=False, num_devices=1)
    arrays, aps = {}, {}
    for name in _INS:
        a = np.ascontiguousarray(inputs[name])
        arrays[f"in_{name}"] = a
        aps[name] = nc.dram_tensor(f"in_{name}", a.shape, mybir.dt.from_np(a.dtype), kind="ExternalInput").ap()
    aps["b_in_gate"] = aps["b_in"][:, GATE0:GATE0 + 3 * D]
    arrays["in_tables"] = shape_constants()
    tables = nc.dram_tensor("in_tables", (P, NCONST), F32, kind="ExternalInput").ap()
    out = nc.dram_tensor("out_y", (1, T, D), F32, kind="ExternalOutput").ap()
    build(nc, aps, tables, out)
    got = run_bass_kernel_spmd(nc, [arrays], core_ids=[0])
    return got.results[0]["out_y"]
```

```python
import math
from contextlib import ExitStack

import concourse.bass as bass
import numpy as np
from concourse import mybir

F32 = mybir.dt.float32
I32 = mybir.dt.int32
ALU = mybir.AluOpType
ACT = mybir.ActivationFunctionType
AX = mybir.AxisListType

P = 128
T = 256
NT = T // P
D = 1024
KD = D // P
DBR = D // 2
NBR = DBR // P
NH = 4
GW, GR = 64, T // 64
ML0 = 3 * DBR + DBR
MLG0 = ML0 + 4 * DBR
GATE0 = MLG0 + 16
E1, E1H = 16, D // 4
FF = 2816
CH = 256
NCH = FF // CH
E2 = 8
A_H, B_H, C_H, HD = 6, 4, 6, 64
O_QA, O_KA, O_VA, O_QI, O_KI, O_WI = 0, 384, 448, 512, 768, 832
O_QB, O_KB, O_VB, O_QC, O_KC, O_VC, D_IN = 836, 1092, 1348, 1604, 1988, 2372, 2756
TOPK = T // 4
EPS, SUB_EPS = 1e-6, 1e-5
MASKED = -1e30
TAKEN = -3e38
ROUND = 12582912.0
TWO_PI = (6.28125, 0.0019350051879882812, 3.019916150957033e-07)
PI = 3.1415925

NS = 3
SLOT = 6144

CONST = {}
_at = 0
for _n, _w in (("ident", P), ("ones", P), ("feats", T), ("cs", NT * T), ("ss", NT * T), ("ict", NT * T),
               ("ist", NT * T), ("ccsc", 2 * P), ("cl", NT * T), ("sl", NT * T), ("causal", NT * T),
               ("upto", NT * T), ("from", NT * T), ("negsel", NH * P), ("tneg", NT), ("inv", 12), ("zero", 8), ("quarter", 4)):
    CONST[_n] = (_at, _w)
    _at += _w
NCONST = _at

COLS = [("c", "c", 0, 8), ("c_ctx", "c_ctx", 0, 8), ("c_2", "c_2", 0, 8), ("n1", "norm1_w", 0, 8), ("n2", "norm2_w", 0, 8),
        ("ga0", "g_attn_2", 0, 8), ("ga1", "g_attn_2", 8, 8), ("gf0", "g_ffn_2", 0, 8), ("gf1", "g_ffn_2", 8, 8),
        ("hcb", "hy_conv_b", 0, 12), ("mcb", "ml_conv_b", 0, 8), ("skip", "hy_skip", 0, 8),
        ("ab0", "ada_b", 0, 48), ("ab1", "b_ada_2", 0, 48), ("ab2", "b_ada_2", 48, 48),
        ("bz", "b_in", 0, 24), ("bg", "b_in_gate", 0, 24),
        ("hcw", "hy_conv_w", 0, 108), ("mcw", "ml_conv_w", 0, 72)]
COL = {}
_at = 0
for _n, _s, _r, _k in COLS:
    COL[_n] = _at
    _at += _k
NCOLB = -(-_at // P)


def shape_constants():
    blob = np.zeros((P, NCONST), np.float32)

    def put(name, a):
        o, w = CONST[name]
        blob[: a.shape[0], o:o + w] = a.reshape(a.shape[0], w)

    def rows(a):
        return a.reshape(NT, P, -1).transpose(1, 0, 2)

    put("ident", np.eye(P))
    put("ones", np.ones((P, P)))
    t = np.arange(T, dtype=np.float32) / np.float32(T)
    bands = np.linspace(1e-4, 15, 16, dtype=np.float32)
    ang = np.float32(2 * math.pi) * t[:, None] * bands[None, :]
    put("feats", np.concatenate([t[:, None], np.cos(ang), np.sin(ang)], -1).T)
    w = np.outer(np.arange(T), 2 * np.arange(T) + 1) * (math.pi / (2 * T))
    put("cs", rows(np.cos(w)))
    put("ss", rows(np.sin(w)))
    put("ict", rows(np.cos(w).T / T))
    put("ist", rows(-np.sin(w).T / T))
    f = np.outer(np.arange(P), np.arange(P)) * (2 * math.pi / P)
    put("ccsc", np.concatenate([np.cos(f), np.sin(f)], -1))
    g = np.outer(np.arange(T), np.arange(T)) * (2 * math.pi / T)
    put("cl", rows(np.cos(g) / math.sqrt(T * P)))
    put("sl", rows(-np.sin(g) / math.sqrt(T * P)))
    low = np.tril(np.ones((T, T)))
    put("causal", rows(np.where(low > 0, 0.0, MASKED)))
    put("upto", rows(low.T))
    put("from", rows(low))
    sel = np.zeros((NH, NH, P))
    for h in range(NH):
        sel[h, h] = -1.0
    put("negsel", sel)
    put("tneg", -t.reshape(NT, P).T)
    inv = [1.0 / (500000.0 ** (np.arange(0, r, 2, dtype=np.float32) / r)) for r in (16, 8)]
    put("quarter", (np.arange(P)[:, None] // 32 == np.arange(4)).astype(np.float32))
    put("inv", np.tile(np.concatenate(inv).astype(np.float32), (P, 1)))
    return blob


G1 = E1 // 4
NA = 12
STAGES = ([("ada0", NA, 0), ("in1", 8, 0), ("ada1", 4, 0)] + 6 * [("ada1", 1, 0), ("merge", 1, 0)]
          + 2 * [("ada1", 1, 0), ("out1", 1, 0)] + [("moe1", E1, 4), ("in2_0", 6, 0), ("out2_0", 2, 0)]
          + NCH * [("ada2", 1, 0), ("ff", 1, 0)] + [("ada2", 1, 0), ("in2_1", 6, 0), ("out2_1", 2, 0), ("moe2", NCH * E2, NCH)])
TURNS = {4: ((0, 1, 2, 1), (0, 2, 1)), NCH: (tuple(c % NS for c in range(NCH)), (2, 0, 1))}


def unit_plan():
    plan, n, used, full = {}, 0, [0] * NS, [0] * NS
    for at, (name, count, body) in enumerate(STAGES):
        entries = []
        if body:
            slots = TURNS[body][0]
            per_slot = [slots.count(s) for s in range(NS)]
            for c, s in enumerate(slots):
                before = [b for b in range(c) if slots[b] == s]
                after = [b for b in range(body) if slots[b] == s]
                free = n + before[-1] + 1 if before else n - body + after[-1] + 1
                if not before:
                    free = max(free, used[s])
                assert free <= n + c
                entries.append((s, free, full[s] + 1 + len(before)))
            n += count
            for s in range(NS):
                used[s] = n - body + max(b for b in range(body) if slots[b] == s) + 1
                full[s] += count // body * per_slot[s]
            plan[name] = (entries, body, per_slot)
            continue
        ahead = STAGES[at:]
        loop = next(i for i, (_, _, b) in enumerate(ahead) if b)
        final = n + sum(k for _, k, _ in ahead[:loop])
        turn = TURNS[ahead[loop][2]][1]
        for _ in range(count):
            s = turn[(n - final) % NS]
            entries.append((s, used[s], full[s] + 1))
            n += 1
            used[s], full[s] = n, full[s] + 1
        plan[name] = (plan.get(name, ((),))[0] + tuple(entries), 0, None)
    return plan


PLAN = unit_plan()
START = {}
USED = {}
_at = 0
for _n, _k, _body in STAGES:
    if _body:
        START[_n] = _at
    USED.setdefault(_n, []).extend(range(_at + 1, _at + _k + 1))
    _at += _k

IN1_COLS = (0, DBR, 2 * DBR, ML0, ML0 + DBR, 3 * DBR, ML0 + 2 * DBR, ML0 + 3 * DBR)
IN2_COLS = tuple((c, min(512, D_IN - c)) for c in range(0, D_IN, 512))
ZQ, ZK, ZFN = 12, 16, 20

R_Z, R_KF, R_KC, R_V1, R_OG, R_VT, ARENA = 0, 6144, 10240, 11264, 13328, 14352, 15376
R_H3, R_SQ, R_PQ, R_DEC, R_W3, R_EXP, R_ROWS = 0, 4096, 8192, 8192, 10240, 12288, 14336
R_PJ, R_FM, R_SM, R_PT, R_IX, R_SEL = 0, 5512, 10376, 12424, 13448, 13960
R_SG, R_AT, R_YA, R_HE, R_SE, R_ST, R_YE, R_IOTA = 0, 512, 1024, 3072, 4096, 4352, 4608, 5632

FM_COLS = (0, 128, 256, 384, 320, 512, 640, 768, 704, 836, 964, 1092, 1220, 1604, 1732, 1860, 1988, 2116, 2244)
FM_QA, FM_KA, FM_QI, FM_KI, FM_QB, FM_KB, FM_QC, FM_KC = 0, (3, 4), 5, (7, 8), 9, 11, 13, 16
NFM = len(FM_COLS)

JOBS = [(br, h0, n, qb) for br, h0, n in (("B", 0, 4), ("B", 4, 4), ("C", 0, 4), ("C", 4, 2), ("A", 0, 4), ("A", 4, 2))
        for qb in range(NT)]
RMS = ("ctx", "x1", "x2", "final1", "a0", "f0", "a1", "f1", "final2")
TRS = ("ctx", "x1", "x2", "a0", "f0", "a1", "f1")
PAIRS, TILE = {4: (0, 2, 1, 3), 2: (0, 1)}, {4: 1, 2: 2}
LAM_INIT = [0.8 - 0.6 * math.exp(-0.3 * l) for l in range(2)]


def build(nc, A, blob_in, out):
    with ExitStack() as ctx:
        def sb(name, shape, dt=F32):
            return ctx.enter_context(nc.sbuf_tensor(name, shape, dt))

        sems = {}

        def sem(name):
            if name not in sems:
                sems[name] = ctx.enter_context(nc.semaphore(name))
            return sems[name]

        ring = sb("ring", [P, NS, SLOT])
        blob = sb("blob", [P, NCONST])
        colv = sb("colv", [P, NCOLB * P])
        x = sb("x", [P, NT, D])
        xn = sb("xn", [P, NT * D])
        hT = sb("hT", [P, KD, T])
        late = sb("late", [P, 2 * D])
        grow = sb("grow", [P, 2, D])
        arena = sb("arena", [P, ARENA])
        rowv = sb("rowv", [P, 2 * DBR])
        mlnw = sb("mlnw", [P, DBR])
        subln = sb("subln", [P, 2, HD])
        lamt = sb("lamt", [P, 8])
        rb1 = sb("rb1", [P, 20])
        wmlg = sb("wmlg", [P, KD, 16])
        rw1 = sb("rw1", [P, KD, 20])
        rw2 = sb("rw2", [P, KD, E2])
        gb = sb("gb", [NH, 4])
        fcol = sb("fcol", [64, 3])
        cact = sb("cact", [P, 24])
        mod = sb("mod", [P, 48])
        modn = sb("modn", [P, 48])
        modc = sb("modc", [P, 16])
        ga = sb("ga", [P, 16])
        gac = sb("gac", [P, 8])
        kn = sb("kn", [P, 8])
        st = sb("st", [P, 16])
        comb = sb("comb", [P, NT, E1 + 4])
        msk = sb("msk", [P, NT, E2])
        slots = sb("slots", [P, NT, E2 + 1])
        wslot = sb("wslot", [P, 4])
        flags = sb("flags", [P, 2], I32)
        rt = sb("rt", [P, NT, 96])
        gcol = sb("gcol", [P, 32])
        en = sb("en", [P, 16])
        dn = sb("dn", [P, 16])
        posi = sb("posi", [P, NT], I32)
        posf = sb("posf", [P, NT])
        ang = rt[:, :, :].rearrange("p b n -> p (b n)")[:, 0:96].rearrange("p (a b n) -> p a b n", a=4, b=NT)
        lamj = rt[:, 1, 0:32]
        cosn = sb("cosn", [P, NT, 12])
        sinn = sb("sinn", [P, NT, 12])
        amx = sb("amx", [P, 2, 4])
        asum = sb("asum", [P, 2, 4])
        ars = sb("ars", [P, 2, 8])
        top = sb("top", [P, 8])
        wix = sb("wix", [P, NT, 4])
        ps = ctx.enter_context(nc.psum_tensor("ps", [P, 8, 512], F32))

        def const(name, n=P):
            o, w = CONST[name]
            return blob[0:n, o:o + w]

        def const2(name):
            return const(name).rearrange("p (b n) -> p b n", b=NT)

        def region(off, *shape):
            n = int(np.prod(shape))
            v = arena[:, off:off + n]
            if len(shape) == 1:
                return v
            names = "abcd"[:len(shape)]
            return v.rearrange(f"p ({' '.join(names)}) -> p {' '.join(names)}", **dict(zip(names, shape)))

        def col(name, k, n=1):
            return colv[:, COL[name] + k:COL[name] + k + n]

        ident = const("ident")
        vrows = region(R_ROWS, NCOLB, P)
        fw1 = region(R_ROWS + 512, 64)[0:33]
        fw2 = region(R_ROWS + 576, 64)[0:64]
        lamr = region(R_ROWS + 640, 2, 4, 32)
        gates = late[0:NH, :].rearrange("p (i d n) -> p i d n", i=2, d=2)
        z = region(R_Z, 24, T)
        kf = region(R_KF, 2, 2, 2 * DBR)
        kc = region(R_KC, NBR, T)
        v1 = region(R_V1, 4, NH, P + 1)
        og = region(R_OG, NT, DBR)
        vt = region(R_VT, NT, DBR)
        macc = region(R_KF, KD, T)
        sgm = region(R_KF + KD * T, 2, NBR, T)
        xn2 = xn[:, :].rearrange("p (b n) -> p b n", b=NT)
        hTc = late[:, :].rearrange("p (k n) -> p k n", k=KD)
        all_ps = ps[:, :, :].rearrange("p b n -> p (b n)")
        full = [sem(f"slot{s}_full") for s in range(NS)]
        used = sem("units_used")
        DMA3 = 48

        block = ctx.enter_context(nc.Block())

        @block.sync
        def _(sp):
            def enter(entry):
                s, free, _ = entry
                if free:
                    sp.wait_ge(used, free)
                return s

            def columns(s, src, width):
                dst = ring[:, s, 0:KD * width].rearrange("p (k n) -> p k n", k=KD)
                for a, b in ((0, 3), (3, 6), (6, 8)):
                    sp.dma_start(dst[:, a:b, :], src[a * P:b * P, :].rearrange("(k p) n -> p k n", p=P)).then_inc(full[s], 16)

            def chunk(s, wg, wu, wd):
                for i, w in enumerate((wg, wu)):
                    sp.dma_start(ring[:, s, i * 2048:(i + 1) * 2048].rearrange("p (k n) -> p k n", k=KD),
                                 w.rearrange("(k p) n -> p k n", p=P)).then_inc(full[s], 16)
                sp.dma_start(ring[:, s, 4096:SLOT].rearrange("p (k n) -> p k n", k=2),
                             wd.rearrange("(k p) n -> p k n", p=P)).then_inc(full[s], 16)

            def straight(name, j):
                s = enter(PLAN[name][0][j])
                h, c = slice(j * 512, (j + 1) * 512), slice(j * CH, (j + 1) * CH)
                if name == "ada0":
                    columns(s, A["ada_w"][0, :, h], 512)
                elif name in ("ada1", "ada2"):
                    columns(s, A["w_ada_2"][int(name[3]) - 1, :, h], 512)
                elif name == "in1":
                    columns(s, A["w_in"][0, :, IN1_COLS[j]:IN1_COLS[j] + 512], 512)
                elif name == "out1":
                    columns(s, A["w_out"][0, :, h], 512)
                elif name.startswith("in2"):
                    o, w = IN2_COLS[j]
                    columns(s, A["w_in_2"][int(name[-1]), :, o:o + w], w)
                elif name.startswith("out2"):
                    columns(s, A["w_out_2"][int(name[-1]), :, h], 512)
                elif name == "ff":
                    chunk(s, A["w_ff_gate_2"][0, :, c], A["w_ff_up_2"][0, :, c], A["w_ff_down_2"][0, c, :])
                else:
                    gate_and_branch(s, j)

            def gate_and_branch(s, j):
                k, half = divmod(j, 2)
                src = A["w_in"][0, :, GATE0 + j * 512:GATE0 + (j + 1) * 512]
                dst = ring[:, s, 0:4096].rearrange("p (k n) -> p k n", k=KD)
                for a in (0, 4):
                    sp.dma_start(dst[:, a:a + 4, :],
                                 src[a * P:(a + 4) * P, :].rearrange("(k p) n -> p k n", p=P)).then_inc(full[s], 16)
                sp.dma_start(ring[:, s, 4096:SLOT].rearrange("p (k n) -> p k n", k=NBR),
                             A["w_branch"][0, k, :, half * 512:(half + 1) * 512].rearrange("(k p) n -> p k n", p=P)
                             ).then_inc(full[s], 16)

            loop1 = next(i for i, stage in enumerate(STAGES) if stage[0] == "moe1")
            done = {}
            for name, n, _ in STAGES[:loop1]:
                for j in range(done.get(name, 0), done.get(name, 0) + n):
                    straight(name, j)
                done[name] = done.get(name, 0) + n
            g1, u1, d1 = A["moe_w_gate"][0], A["moe_w_up"][0], A["moe_w_down"][0]
            entries, body, _ = PLAN["moe1"]
            with sp.Fori(0, G1) as i:
                for c, (s, free, _) in enumerate(entries):
                    sp.wait_ge(used, i * body + free)
                    e = i * body + c
                    chunk(s, *(w[bass.ds(e, 1)].rearrange("a k n -> (a k) n") for w in (g1, u1, d1)))

            for name, n, _ in STAGES[loop1 + 1:-1]:
                for j in range(done.get(name, 0), done.get(name, 0) + n):
                    straight(name, j)
                done[name] = done.get(name, 0) + n
            g2, u2, d2 = A["w_exp_gate_2"][0], A["w_exp_up_2"][0], A["w_exp_down_2"][0]
            entries, body, _ = PLAN["moe2"]
            with sp.Fori(0, E2) as e:
                for c, (s, free, _) in enumerate(entries):
                    sp.wait_ge(used, e * body + free)
                    h = slice(c * CH, (c + 1) * CH)
                    chunk(s, g2[bass.ds(e, 1), :, h].rearrange("a k n -> (a k) n"),
                          u2[bass.ds(e, 1), :, h].rearrange("a k n -> (a k) n"),
                          d2[bass.ds(e, 1), h, :].rearrange("a k n -> (a k) n"))
            sp.wait_ge(sem("y_final"), 1)
            sp.dma_start(out[0].rearrange("(b p) d -> p b d", p=P), xn2).then_inc(sem("stored"), 16)
            sp.wait_ge(sem("stored"), 16)

        @block.gpsimd
        def _(pool):
            pool.dma_start(blob[:, :], blob_in).then_inc(sem("consts_in"), 16)
            for name, src, r0, n in COLS:
                a = A[src]
                flat = a.rearrange(" ".join("abcd"[:a.ndim]) + " -> (" + " ".join("abcd"[:a.ndim]) + ")") if a.ndim > 1 else a
                v = flat[r0 * P:(r0 + n) * P].rearrange("(r p) -> r p", p=P)
                at, done = COL[name], 0
                while done < n:
                    b, p = divmod(at + done, P)
                    m = min(n - done, P - p)
                    pool.dma_start(vrows[p:p + m, b, :], v[done:done + m, :]).then_inc(sem("cols_in"), 16)
                    done += m
            pool.dma_start(fw1[:, :], A["hy_f_w1"][0]).then_inc(sem("filter_in"), 16)
            pool.dma_start(fw2[:, :], A["hy_f_w2"][0]).then_inc(sem("filter_in"), 16)
            pool.dma_start(region(R_W3, 2048)[0:64, :], A["hy_f_w3"][0]).then_inc(sem("filter_in"), 16)
            for i, name in enumerate(("hy_f_b1", "hy_f_b2", "hy_f_freq")):
                pool.dma_start(fcol[:, i:i + 1], A[name][0].rearrange("(p a) -> p a", a=1), allow_slow_non_contiguous=True).then_inc(sem("filter_in"), 16)
            pool.dma_start(region(R_DEC, 2048), A["hy_decay"][0].rearrange("o d c -> (o d c)").partition_broadcast(P)
                           ).then_inc(sem("decay_in"), 16)
            pool.dma_start(hT[:, :, :].rearrange("p k n -> p (k n)").rearrange("p (b d) -> p b d", b=NT),
                           A["ctx"][0].rearrange("(b p) d -> p b d", p=P)).then_inc(sem("ctx_in"), 16)
            pool.dma_start(x[:, :, :], A["x"][0].rearrange("(b p) d -> p b d", p=P)).then_inc(sem("x_in"), 16)
            pool.dma_start(rowv[:, :], A["b_in"][0, ML0 + 2 * DBR:MLG0].partition_broadcast(P)).then_inc(sem("rows_in"), 16)
            pool.dma_start(mlnw[:, :], A["ml_norm_w"][0].partition_broadcast(P)).then_inc(sem("rows_in"), 16)
            pool.dma_start(gb[:, :], A["b_in"][0, MLG0:GATE0].rearrange("(g h) -> h g", h=NH), allow_slow_non_contiguous=True).then_inc(sem("rows_in"), 16)
            pool.dma_start(wmlg[:, :, :], A["w_in"][0, :, MLG0:GATE0].rearrange("(k p) n -> p k n", p=P)).then_inc(sem("rows_in"), 16)
            pool.dma_start(rb1[:, 0:4], A["moe_rg_b"][0].partition_broadcast(P)).then_inc(sem("rows_in"), 16)
            pool.dma_start(rb1[:, 4:20], A["moe_re_b"][0].partition_broadcast(P)).then_inc(sem("rows_in"), 16)
            pool.dma_start(rw1[:, :, 0:4], A["moe_rg_w"][0].rearrange("(k p) n -> p k n", p=P)).then_inc(sem("rows_in"), 16)
            pool.dma_start(rw1[:, :, 4:20], A["moe_re_w"][0].rearrange("(k p) n -> p k n", p=P)).then_inc(sem("rows_in"), 16)
            pool.dma_start(rw2[:, :, :], A["w_router_2"][0].rearrange("(k p) n -> p k n", p=P)).then_inc(sem("rows_in"), 16)
            pool.dma_start(subln[:, :, :].rearrange("p a b -> p (a b)"),
                           A["diff_subln_2"].rearrange("a b -> (a b)").partition_broadcast(P)).then_inc(sem("rows_in"), 16)
            pool.dma_start(lamr[:, :, :, :].rearrange("p a b c -> p (a b c)"),
                           A["diff_lambda_2"].rearrange("a b c -> (a b c)").partition_broadcast(P)).then_inc(sem("rows_in"), 16)
            pool.dma_start(posi[:, :], A["positions_2"][0].rearrange("(b p) -> p b", p=P), allow_slow_non_contiguous=True).then_inc(sem("rows_in"), 16)
            pool.wait_ge(sem("ml_gates"), 1)
            pool.dma_start(late[:, 0:D], A["norm_f_w"].partition_broadcast(P)).then_inc(sem("late_in"), 16)
            pool.dma_start(late[:, D:2 * D], A["g_final_2"].partition_broadcast(P)).then_inc(sem("late_in"), 16)

        N_COLS_IN = sum(1 + (COL[n] // P != (COL[n] + k - 1) // P) for n, _, _, k in COLS)
        N_ROWS_IN = 12

        @block.tensor
        def _(pe):
            mm = nc.tensor.matmul

            def unit(entry):
                s, _, n = entry
                pe.wait_ge(full[s], DMA3 * n)
                return s

            def w512(s, k, a=0, n=512, width=512):
                return ring[:, s, k * width + a:k * width + a + n]

            def ada(a, u, bank):
                pe.wait_ge(sem("ada_sum"), NA * a + u + 1)
                s = PLAN[f"ada{a}"][0][u][0]
                n = 2 if a == 0 and u < 4 else 1
                at = (8 * u if u < 4 else 16 + 4 * u) if a == 0 else 4 * u
                for m in range(4):
                    o = at + m * n
                    if a == 0:
                        for k in range(4, KD):
                            mm(ps[:, bank, o:o + n], w512(s, k, m * P, P), cact[:, k:k + 8 * n - 7:8], start=k == 4, stop=False,
                               skip_group_check=True)
                    for i in range(n):
                        last = mm(ps[:, bank, o + i:o + i + 1], ring[:, s, 4096 + i * 512 + m * P:4096 + i * 512 + (m + 1) * P],
                                  const("ones")[:, 0:1], start=a > 0, stop=True, skip_group_check=True)
                last.then_inc(used, 1)

            def gate_rows(a):
                pe.wait_ge(sem("diag"), a + 1)
                for g in range(16):
                    last = mm(ps[:, 4 + g // 4, (g % 4) * P:(g % 4 + 1) * P], const("ones"), xn[:, g * P:(g + 1) * P],
                              start=True, stop=True)
                last.then_inc(sem("gaterow_mm"), 1)

            pe.wait_ge(sem("consts_in"), 16)
            pe.wait_ge(sem("cols_in"), 16 * N_COLS_IN)
            total = sum(k for *_, k in COLS)
            for b in range(NCOLB):
                n = min(P, total - b * P)
                last = nc.tensor.transpose(ps[:, 0, b * P:b * P + n], vrows[0:n, b, :], ident[0:n, 0:n])
            last.then_inc(sem("cols_t"), 1)

            pe.wait_ge(sem("filter_in"), 96)
            mm(ps[0:64, 1, 0:T], fw1[:, :], const("feats", 33), start=True, stop=True).then_inc(sem("filter_mm"), 1)
            pe.wait_ge(sem("filter_h"), 1)
            mm(ps[0:64, 2, 0:T], fw2[:, :], region(R_SQ + 512, T)[0:64, :], start=True, stop=True).then_inc(sem("filter_mm"), 1)
            pe.wait_ge(sem("filter_h"), 2)
            h2 = region(R_SQ + 768, T)
            for b in range(NT):
                ada(0, b, 3)
                if b:
                    pe.wait_ge(sem("filter_h3"), b)
                for n in range(4):
                    last = mm(ps[:, 4 + n, :], h2[0:64, b * P:(b + 1) * P], region(R_W3, 2048)[0:64, n * 512:(n + 1) * 512],
                              start=True, stop=True)
                last.then_inc(sem("filter_mm"), 1)
            ada(0, 2, 3)
            pe.wait_ge(sem("filter_sq"), 1)
            sq = region(R_SQ, NT, 2, 2, DBR)
            for o in range(2):
                for c in range(NBR):
                    for i, (d, b) in enumerate((d, b) for d in range(2) for b in range(NT)):
                        last = mm(ps[:, 1, o * NBR + c:o * NBR + c + 1], sq[:, b, o, d, c * P:(c + 1) * P], const("ones")[:, 0:1],
                                  start=i == 0, stop=i == 3)
            last.then_inc(sem("filter_ssum"), 1)
            for u in range(3, 8):
                ada(0, u, 3)
            pe.wait_ge(sem("mod_in"), 1)
            pe.wait_ge(sem("filter_pq"), 1)
            pe.wait_ge(sem("kn_in"), 1)
            pq = region(R_PQ, NT, 2, 2, DBR)
            for o in range(2):
                for ri, table in enumerate(("cs", "ss")):
                    for m in range(NT):
                        for b in range(NT):
                            last = mm(ps[:, 4 * o + 2 * ri + m, :], const2(table)[:, b, m * P:(m + 1) * P], pq[:, b, o, ri, :],
                                      start=b == 0, stop=b == NT - 1)
            last.then_inc(sem("spectra_mm"), 1)

            pe.wait_ge(sem("spectra_in"), 1)
            for u in range(8, NA):
                ada(0, u, 3)

            def turn(name):
                i = TRS.index(name)
                pe.wait_ge(sem("normed"), i + 1)
                for k in range(KD):
                    for b in range(NT):
                        last = nc.tensor.transpose(ps[:, 4 + k // 2, (k % 2) * T + b * P:(k % 2) * T + (b + 1) * P],
                                                   xn2[:, b, k * P:(k + 1) * P], ident)
                last.then_inc(sem("turned"), 1)

            def columns_by(s, src, bank):
                for m in range(4):
                    for k in range(KD):
                        last = mm(ps[:, bank + m // 2, (m % 2) * T:(m % 2 + 1) * T], w512(s, k, m * P, P), src[:, k, :],
                                  start=k == 0, stop=k == KD - 1)
                return last

            def rows_by(s, src, bank, n=512):
                for b in range(NT):
                    for k in range(KD):
                        last = mm(ps[:, bank + b, 0:n], src[:, k, b * P:(b + 1) * P], w512(s, k, 0, n, n),
                                  start=k == 0, stop=k == KD - 1)
                return last

            turn("ctx")
            pe.wait_ge(sem("hT_ready"), 1)
            turn("x1")
            pe.wait_ge(sem("hT_ready"), 2)

            entries = PLAN["in1"][0]
            for g in range(4):
                s = unit(entries[g])
                if g == 2:
                    pe.wait_ge(sem("gaterow_in"), 1)
                columns_by(s, hT, 2 * g).then_inc(used, 1)
                if g == 0:
                    gate_rows(0)
            s = unit(entries[4])
            pe.wait_ge(sem("z_in"), 1)
            columns_by(s, hT, 0).then_inc(sem("k_mm"), 1)
            pe.wait_ge(sem("z_in"), 2)
            columns_by(s, hTc, 2).then_inc(used, 1)
            s = unit(entries[5])
            pe.wait_ge(sem("z_in"), 3)
            columns_by(s, hT, 4).then_inc(used, 1)
            s = unit(entries[6])
            pe.wait_ge(sem("z_in"), 4)
            rows_by(s, hT, 6).then_inc(sem("vo_mm"), 1)
            pe.wait_ge(sem("z_in"), 5)
            rows_by(s, hTc, 0).then_inc(used, 1)
            s = unit(entries[7])
            pe.wait_ge(sem("z_in"), 6)
            rows_by(s, hT, 2).then_inc(used, 1)
            pe.wait_ge(sem("rows_in"), 16 * N_ROWS_IN)
            pe.wait_ge(sem("z_in"), 7)
            pe.wait_ge(sem("vo_in"), 1)
            for g in range(4):
                for i, src in enumerate((hTc, hT)):
                    for k in range(KD):
                        last = mm(ps[0:NH, 4 + g, i * T:(i + 1) * T], wmlg[:, k, g * NH:(g + 1) * NH], src[:, k, :],
                                  start=k == 0, stop=k == KD - 1)
            last.then_inc(sem("gates_mm"), 1)

            pe.wait_ge(sem("vo_in"), 3)
            for b in range(NT):
                for g in range(4):
                    last = mm(ps[:, 2 * b + g // 2, (g % 2) * T:(g % 2 + 1) * T], z[:, ZFN + g, b * P:(b + 1) * P], const("ccsc"),
                              start=True, stop=True)
            last.then_inc(sem("fnet_mm"), 1)
            pe.wait_ge(sem("fnet_in"), 1)
            pe.wait_ge(sem("vo_in"), 4)
            ab = xn[:, :].rearrange("p (b g n) -> p b g n", b=NT, g=4)
            for g in range(4):
                for i, (b, table) in enumerate((b, t) for b in range(NT) for t in range(2)):
                    last = mm(ps[:, 4 + g // 2, (g % 2) * T:(g % 2 + 1) * T], ab[:, b, g, table * P:(table + 1) * P],
                              const2(("cl", "sl")[table])[:, b, :], start=i == 0, stop=i == 3)
            last.then_inc(sem("fnet_mm"), 1)

            for o in range(2):
                pe.wait_ge(sem("hy_u"), o + 1)
                for b in range(NT):
                    for c in range(NBR):
                        last = nc.tensor.transpose(ps[:, b, c * P:(c + 1) * P], z[:, c, b * P:(b + 1) * P], ident)
                last.then_inc(sem("hy_t"), 1)
                pe.wait_ge(sem("hy_rows"), o + 1)
                for ri, table in enumerate(("cs", "ss")):
                    for m in range(NT):
                        for b in range(NT):
                            last = mm(ps[:, 2 * ri + m, :], const2(table)[:, b, m * P:(m + 1) * P], vt[:, b, :],
                                      start=b == 0, stop=b == NT - 1)
                last.then_inc(sem("hy_spec"), 1)
                pe.wait_ge(sem("fnet_in"), 2)
                ada(1, 2 * o, 4)
                pe.wait_ge(sem("hy_y"), o + 1)
                yy = xn[:, :].rearrange("p (r m n) -> p r m n", r=2, m=NT)
                for c in range(NBR):
                    for i, (r, m) in enumerate((r, m) for r in range(2) for m in range(NT)):
                        last = mm(ps[:, 6 + c // 2, (c % 2) * T:(c % 2 + 1) * T], yy[:, r, m, c * P:(c + 1) * P],
                                  const2(("ict", "ist")[r])[:, m, :], start=i == 0, stop=i == 3)
                last.then_inc(sem("hy_inv"), 1)
                ada(1, 2 * o + 1, 4)

            gi, gf, _, gm = (region(R_KF + i * 1024, 2, 512) for i in range(4))
            pe.wait_ge(sem("ml_gates"), 1)
            pe.wait_ge(sem("mod_in"), 3)
            for d in range(2):
                for sbk in range(4):
                    nc.tensor.transpose(ps[:, 0, (d * 4 + sbk) * 4:(d * 4 + sbk) * 4 + 4], gi[0:NH, d, sbk * P:(sbk + 1) * P], ident[0:NH, 0:NH])
                for b in range(NT):
                    o = 32 + (d * 2 + b) * 4
                    nc.tensor.transpose(ps[:, 1, o:o + 4], gf[0:NH, d, T + b * P:T + (b + 1) * P], ident[0:NH, 0:NH])
                for h in range(NH):
                    last = mm(ps[:, 2 + 2 * d + h // 2, (h % 2) * T:(h % 2 + 1) * T], const("negsel", NH)[:, h * P:(h + 1) * P],
                              gm[0:NH, d, T:2 * T], start=True, stop=True)
            last.then_inc(sem("ml_cols_mm"), 1)
            pe.wait_ge(sem("ml_qk"), 1)
            pe.wait_ge(sem("ml_cols"), 2)
            for h in range(NH):
                if h:
                    pe.wait_ge(sem("ml_p"), 2 * h)
                for sbk in range(4):
                    k_ = kc[:, h, sbk * P:(sbk + 1) * P] if sbk < 2 else z[:, ZK + h, (sbk - 2) * P:(sbk - 1) * P]
                    last = mm(ps[:, 6 + sbk // 2, (sbk % 2) * T:(sbk % 2 + 1) * T], k_, z[:, ZQ + h, :], start=True, stop=True)
                last.then_inc(sem("ml_s"), 1)
                for d in range(2):
                    j = 2 * h + d
                    pe.wait_ge(sem("ml_p"), j + 1)
                    if j >= 2:
                        pe.wait_ge(sem("ml_h"), j - 1)
                    w = xn[:, (j % 2) * 1024:(j % 2 + 1) * 1024].rearrange("p (s n) -> p s n", s=4)
                    for b in range(NT):
                        for sbk in range(4):
                            last = mm(ps[:, j % 2, b * T:b * T + P + 1], w[:, sbk, b * P:(b + 1) * P], v1[:, sbk, h, :],
                                      start=sbk == 0, stop=sbk == 3)
                    last.then_inc(sem("ml_pv"), 1)
            pe.wait_ge(sem("ml_y"), 1)
            for c in range(NH):
                for b in range(NT):
                    last = nc.tensor.transpose(ps[:, 2 + c // 2, (c % 2) * T + b * P:(c % 2) * T + (b + 1) * P],
                                               vt[:, b, c * P:(c + 1) * P], ident)
            last.then_inc(sem("ml_t"), 1)

            pe.wait_ge(sem("ml_yT"), 1)
            pe.wait_ge(sem("fnet_in"), 2)
            for j, entry in enumerate(PLAN["merge"][0]):
                k, base = j // 2, 4 * (j % 2)
                if j >= 2:
                    pe.wait_ge(sem("merged"), j - 1)
                ada(1, 4 + j, base + 3)
                s = unit(entry)
                columns_by(s, hT, base).then_inc(sem("mg_mm"), 1)
                pe.wait_ge(sem("mod_in"), 4 + j)
                y0 = (0, ZFN, ZQ)[k]
                for m in range(4):
                    for c in range(NBR):
                        last = mm(ps[:, base + 2 + m // 2, (m % 2) * T:(m % 2 + 1) * T],
                                  ring[:, s, 4096 + c * 512 + m * P:4096 + c * 512 + (m + 1) * P], z[:, y0 + c, :],
                                  start=c == 0, stop=c == NBR - 1)
                last.then_inc(used, 1)

            def out_proj(name, src):
                for half, entry in enumerate(PLAN[name][0]):
                    if name == "out1":
                        ada(1, 10 + half, 4 + half)
                    s = unit(entry)
                    rows_by(s, src, 2 * half).then_inc(used, 1)

            def chunk_mm(s, n, first, last_, read, src=hT, cols=T, base=4):
                for hb in range(2):
                    pe.wait_ge(sem("act_ready"), n - 1 + hb)
                    for i in range(2):
                        for k in range(KD):
                            o = i * 2048 + k * CH + hb * P
                            m_ = mm(ps[:, hb, i * cols:(i + 1) * cols], ring[:, s, o:o + P], src[:, k, :],
                                    start=k == 0, stop=k == KD - 1)
                    m_.then_inc(sem("gu_mm"), 1)
                if first:
                    pe.wait_ge(*read)
                for hb in range(2):
                    pe.wait_ge(sem("act_ready"), n + 1 + hb)
                    for b in range(cols // P):
                        for half in range(2):
                            o = 4096 + hb * 1024 + half * 512
                            m_ = mm(ps[:, base + 2 * b + half, :], region(R_AT, 2, T)[:, hb, b * P:(b + 1) * P],
                                    ring[:, s, o:o + 512], start=first and hb == 0, stop=last_ and hb == 1)
                m_.then_inc(used, 1)

            def moe_mm(name, i, jobs, experts, chunks, hidden):
                entries, body, per_slot = PLAN[name]
                sel, selT, ye, he = region(R_SE, NT, P), region(R_ST, T), region(R_YE, D), region(R_HE, KD, P)
                g, t, y = sem(f"{name}_gathered"), sem(f"{name}_placed"), sem(f"{name}_ye")
                ready, hte, selt = sem(f"{name}_sel"), sem(f"{name}_he"), sem(f"{name}_selT")

                pe.wait_ge(sem("masks"), i + 1)
                for b in range(NT):
                    for s_ in range(b + 1):
                        last = mm(ps[:, 3, 128 + b * 16:128 + b * 16 + jobs], const2("upto")[:, s_, b * P:(b + 1) * P],
                                  msk[:, s_, 0:jobs], start=s_ == 0, stop=s_ == b)
                last.then_inc(sem("counted"), 1)
                pe.wait_ge(sem("flag"), i + 1)
                over = pe.value_load(flags[P - 1:P, i:i + 1], min_val=0, max_val=1)

                def gather(j):
                    pe.wait_ge(ready, j + 1)
                    for k in range(KD):
                        for b in range(NT):
                            last = mm(ps[:, 2 + k // 4, (k % 4) * P:(k % 4 + 1) * P], xn2[:, b, k * P:(k + 1) * P], sel[:, b, :],
                                      start=b == 0, stop=b == NT - 1)
                    last.then_inc(g, 1)

                def place(j):
                    for b in range(NT):
                        nc.tensor.transpose(ps[:, 0, b * P:(b + 1) * P], sel[:, b, :], ident)
                    for b in range(NT):
                        last = mm(ps[:, 0, T:T + experts], sel[:, b, :], comb[:, b, bass.ds(j * experts, experts)],
                                  start=b == 0, stop=b == NT - 1)
                    last.then_inc(t, 1)

                with pe.If(over > 0):
                    with pe.Fori(0, jobs) as j:
                        for c, (s, _, f) in enumerate(entries):
                            pe.wait_ge(full[s], j * (DMA3 * per_slot[s]) + DMA3 * f)
                            chunk_mm(s, j * (2 * body) + hidden + 2 * c + 2, c % chunks == 0, c % chunks == chunks - 1,
                                     (sem(f"{name}_y_read"), j * experts + c // chunks + 1))
                with pe.Else():
                    pe.wait_ge(sem(f"{name}_zero"), 1)
                    for q in range(4):
                        mm(ps[:, 4 + q, :], selT[:, 0:P], ye[:, 0:512], start=True, stop=True)
                    gather(0)
                    place(0)
                    with pe.Fori(0, jobs) as j:
                        pe.wait_ge(hte, j + 1)
                        pe.wait_ge(selt, j + 1)
                        for c, (s, _, f) in enumerate(entries):
                            pe.wait_ge(full[s], j * (DMA3 * per_slot[s]) + DMA3 * f)
                            chunk_mm(s, j * (2 * body) + hidden + 2 * c + 2, c % chunks == 0, c % chunks == chunks - 1,
                                     (y, j * experts + c // chunks + 1), he, P, 2)
                        pe.wait_ge(y, j * experts + experts + 1)
                        gather(j + 1)
                        for b in range(NT):
                            for half in range(2):
                                mm(ps[:, 4 + 2 * b + half, :], selT[:, b * P:(b + 1) * P], ye[:, half * 512:(half + 1) * 512],
                                   start=False, stop=True, skip_group_check=True)
                        place(j + 1)
                pe.drain()

            def router(rw, n, i):
                for b in range(NT):
                    for k in range(KD):
                        last = mm(ps[:, 3, b * 32:b * 32 + n], hT[:, k, b * P:(b + 1) * P], rw[:, k, :],
                                  start=k == 0, stop=k == KD - 1)
                last.then_inc(sem("router_mm"), 1)

            pe.wait_ge(sem("merged"), 6)
            out_proj("out1", macc)
            turn("x2")
            pe.wait_ge(sem("hT_ready"), 3)
            router(rw1, 20, 0)
            moe_mm("moe1", 0, G1, 4, 1, 0)
            hidden = 2 * E1

            for l in range(2):
                pe.wait_ge(sem("block_done"), l + 1)
                turn(f"a{l}")
                pe.wait_ge(sem("hT_ready"), 4 + 2 * l)
                for j, ((c, w), entry) in enumerate(zip(IN2_COLS, PLAN[f"in2_{l}"][0])):
                    s = unit(entry)
                    if j == 2:
                        pe.wait_ge(sem("gaterow_in"), l + 2)
                    if j >= 4:
                        pe.wait_ge(sem("pj_in"), 6 * l + j - 3)
                    rows_by(s, hT, 2 * (j % 4), w).then_inc(used, 1)
                    if j == 0:
                        gate_rows(l + 1)
                pj = region(R_PJ, NT, D_IN)
                fm = region(R_FM, NFM, T)
                pe.wait_ge(sem("roped"), l + 1)
                n_t = -(-NFM // 4)
                for q in range(n_t):
                    if q >= 2:
                        pe.wait_ge(sem("fm_in"), n_t * l + q - 1)
                    for i in range(4 * q, min(NFM, 4 * q + 4)):
                        for b in range(NT):
                            last = nc.tensor.transpose(
                                ps[:, 2 * (q % 2) + (i % 4) // 2, (i % 2) * T + b * P:(i % 2) * T + (b + 1) * P],
                                pj[:, b, FM_COLS[i]:FM_COLS[i] + P], ident)
                    last.then_inc(sem("fm_mm"), 1)
                pe.wait_ge(sem("fm_in"), n_t * (l + 1))
                for qb in range(NT):
                    ns = (qb + 1) * P
                    for h in range(4):
                        p0 = 64 * (h % 2)
                        last = mm(ps[:, 4 + 2 * qb + h % 2, (h // 2) * T:(h // 2) * T + ns],
                                  fm[p0:p0 + 64, FM_QI + h // 2, qb * P:(qb + 1) * P], fm[p0:p0 + 64, FM_KI[h % 2], 0:ns],
                                  start=True, stop=True)
                    last.then_inc(sem("ix_mm"), 1)

                sm = region(R_SM, 2, 4, T)
                pt = region(R_PT, 4, NT, P)

                def scores(j):
                    br, h0, n, qb = JOBS[j]
                    ns = (qb + 1) * P
                    if j >= 2:
                        pe.wait_ge(sem("masked"), len(JOBS) * l + j - 1)
                    if j == 0:
                        pe.wait_ge(sem("qb_masked"), l + 1)
                    for k in range(n):
                        if br == "B":
                            i, tile = k, k
                            q_, k_ = hT[:, h0 + i, :], fm[:, FM_KB + h0 // 4, :]
                        else:
                            i, tile = PAIRS[n][k], TILE[n] * k
                            h = h0 + i
                            rows = slice(64 * (h % 2), 64 * (h % 2) + 64)
                            q_ = fm[rows, (FM_QA if br == "A" else FM_QC) + h // 2, :]
                            k_ = fm[rows, FM_KA[h % 2] if br == "A" else FM_KC + h // 2, :]
                        last = mm(ps[:, 2 * (j % 2) + tile // 2, (tile % 2) * T:(tile % 2) * T + ns],
                                  q_[:, qb * P:(qb + 1) * P], k_[:, 0:ns], start=True, stop=True)
                    last.then_inc(sem("s_mm"), 1)

                scores(0)
                for j, (br, h0, n, qb) in enumerate(JOBS):
                    if j + 1 < len(JOBS):
                        scores(j + 1)
                    done = len(JOBS) * l + j
                    heads = n // 2 if br == "B" else n
                    pe.wait_ge(sem("probs"), done + 1)
                    if j == 0:
                        pe.wait_ge(sem("ix_in"), 2 * (l + 1))
                    for i in range(heads):
                        for sbk in range(qb + 1):
                            src = sm[:, j % 2, 2 * i if br == "B" else i, sbk * P:(sbk + 1) * P]
                            o = (i * 2 + sbk) * P
                            last = nc.tensor.transpose(ps[:, 4 + o // 512, o % 512:o % 512 + P], src, ident)
                    last.then_inc(sem("pt_mm"), 1)
                    pe.wait_ge(sem("pt_in"), done + 1)
                    if j >= 2:
                        pe.wait_ge(sem("o_in"), done - 1)
                    for i in range(heads):
                        v_ = {"A": O_VA, "B": O_VB + (h0 // 2 + i) * HD, "C": O_VC + (h0 + PAIRS[n][i]) * HD}[br]
                        for sbk in range(qb + 1):
                            last = mm(ps[:, 6 + j % 2, i * HD:(i + 1) * HD], pt[:, i, sbk, :], pj[:, sbk, v_:v_ + HD],
                                      start=sbk == 0, stop=sbk == qb)
                    last.then_inc(sem("o_mm"), 1)
                pe.wait_ge(sem("y_rows"), l + 1)
                for k in range(KD):
                    for b in range(NT):
                        last = nc.tensor.transpose(ps[:, 4 + k // 2, (k % 2) * T + b * P:(k % 2) * T + (b + 1) * P],
                                                   xn2[:, b, k * P:(k + 1) * P], ident)
                last.then_inc(sem("y_t"), 1)
                pe.wait_ge(sem("yT"), l + 1)
                out_proj(f"out2_{l}", hT)
                turn(f"f{l}")
                pe.wait_ge(sem("hT_ready"), 5 + 2 * l)
                if l == 0:
                    for c, entry in enumerate(PLAN["ff"][0]):
                        ada(2, c, 2)
                        s = unit(entry)
                        chunk_mm(s, hidden + 2 * c + 2, c == 0, c == NCH - 1, (sem("hT_ready"), 5))
                    ada(2, NA - 1, 2)
                    hidden += 2 * NCH
            router(rw2, E2, 1)
            moe_mm("moe2", 1, E2, 1, NCH, hidden)

        @block.scalar
        def _(act):
            ac = nc.scalar.activation

            def sqrt_of(i, width, src, dst):
                act.wait_ge(sem("ms"), i)
                ac(dst, src, ACT.Sqrt).then_inc(sem("std"), 1)

            act.wait_ge(sem("cols"), 1)
            ac(cact[:, :], col("c", 0, 24), ACT.Silu).then_inc(sem("c_act"), 1)
            for i in range(2):
                act.wait_ge(sem("filter_a"), i + 1)
                ac(region(R_SQ + 512 + 256 * i, T)[0:64, :], region(R_SQ, T)[0:64, :], ACT.Sin).then_inc(sem("filter_h"), 1)
            act.wait_ge(sem("decay_in"), 16)
            ac(region(R_DEC, 2048), region(R_DEC, 2048), ACT.Abs)
            act.drain()
            for b in range(NT):
                if b:
                    act.wait_ge(sem("filter_h3"), b)
                ac(region(R_EXP, 2048), region(R_DEC, 2048), ACT.Exp, scale=const("tneg")[:, b:b + 1]).then_inc(sem("decay"), 1)
            act.wait_ge(sem("lam_in"), 1)
            ac(lamt[:, 0:4], lamt[:, 0:4], ACT.Exp).then_inc(sem("lam_exp"), 1)
            act.wait_ge(sem("ang_in"), 1)
            ac(sinn[:, :, :], ang[:, 2, :, :], ACT.Sin)
            ac(cosn[:, :, :], ang[:, 3, :, :], ACT.Sin).then_inc(sem("rope_in"), 1)
            act.wait_ge(sem("kn_in"), 1)
            ac(kn[:, :], kn[:, :], ACT.Sqrt).then_inc(sem("kn_sqrt"), 1)

            std = st[:, 2:4]
            sqrt_of(1, 2, st[:, 0:2], std)
            sqrt_of(2, 2, st[:, 0:2], std)

            for g, (dst, b0, bank) in enumerate(((z[:, 0:4], 0, 0), (z[:, 4:8], 4, 2), (z[:, 8:12], 8, 4), (z[:, 12:16], 16, 6),
                                                 (z[:, 16:20], 20, 0), (kc, 20, 2), (z[:, 20:24], 12, 4))):
                if g == 4:
                    act.wait_ge(sem("k_mm"), 1)
                else:
                    act.wait_ge(used, USED["in1"][g if g < 4 else g - 1])
                for m in range(4):
                    last = ac(dst[:, m, :], ps[:, bank + m // 2, (m % 2) * T:(m % 2 + 1) * T], ACT.Identity, bias=col("bz", b0 + m))
                last.then_inc(sem("z_in"), 1)
            act.wait_ge(sem("conv_qk"), 1)
            ac(z[:, ZQ:ZQ + 8, :], z[:, ZQ:ZQ + 8, :], ACT.Silu)
            ac(kc, kc, ACT.Silu).then_inc(sem("ml_silu"), 1)
            act.wait_ge(sem("vo_in"), 3)
            ac(og, og, ACT.Sigmoid).then_inc(sem("o_gate"), 1)

            act.wait_ge(sem("fnet_mm"), 1)
            ac(xn[:, :], all_ps[:, 0:2048], ACT.Copy).then_inc(sem("fnet_in"), 1)
            act.wait_ge(sem("fnet_mm"), 2)
            ac(z[:, ZFN:ZFN + 4, :], ps[:, 4:6, :].rearrange("p b (a n) -> p (b a) n", a=2), ACT.Copy).then_inc(sem("fnet_in"), 1)
            for o in range(2):
                act.wait_ge(sem("hy_t"), o + 1)
                ac(vt, ps[:, 0:2, :], ACT.Copy).then_inc(sem("hy_rows"), 1)

            _, gf, _, gm = (region(R_KF + i * 1024, 1024)[0:NH, :] for i in range(4))
            act.wait_ge(sem("ml_f"), 1)
            ac(gm, gf, ACT.Abs)
            act.drain()
            ac(gm, gm, ACT.Exp, scale=-1.0)
            act.drain()
            ac(gm, gm, ACT.Ln, bias=1.0).then_inc(sem("ml_softplus"), 1)
            act.wait_ge(sem("ml_cols_mm"), 1)
            ac(en[:, :], ps[:, 1, 32:48], ACT.Exp, scale=-1.0).then_inc(sem("ml_cols"), 1)
            for j in range(8):
                act.wait_ge(sem("ml_w"), j + 1)
                w = xn[:, (j % 2) * 1024:(j % 2 + 1) * 1024]
                ac(w, w, ACT.Exp).then_inc(sem("ml_exp"), 1)
            sqrt_of(3, 8, st[:, 0:8], st[:, 8:16])
            act.wait_ge(sem("ml_t"), 1)
            ac(z[:, ZQ:ZQ + 4, :], ps[:, 2:4, :].rearrange("p b (a n) -> p (b a) n", a=2), ACT.Copy).then_inc(sem("ml_yT"), 1)

            for j in range(6):
                k, half = divmod(j, 2)
                act.wait_ge(sem("mg_mm"), j + 1)
                if j >= 2:
                    act.wait_ge(sem("merged"), j - 1)
                for m in range(4):
                    last = ac(sgm[:, j % 2, m, :], ps[:, 4 * (j % 2) + m // 2, (m % 2) * T:(m % 2 + 1) * T], ACT.Sigmoid,
                              bias=col("bg", k * 8 + half * 4 + m))
                last.then_inc(sem("mg_sig"), 1)

            def chunk_silu(n, cols=T):
                for hb in range(2):
                    act.wait_ge(sem("gu_mm"), n - 1 + hb)
                    act.wait_ge(sem("act_ready"), n - 1 + hb)
                    ac(region(R_SG, 2, T)[:, hb, 0:cols], ps[:, hb, 0:cols], ACT.Silu).then_inc(sem("gate_silu"), 1)

            def moe_silu(i, units, hidden):
                act.wait_ge(sem("flag"), i + 1)
                over = act.value_load(flags[P - 1:P, i:i + 1], min_val=0, max_val=1)
                with act.If(over > 0):
                    with act.Fori(0, units) as c:
                        chunk_silu(c * 2 + hidden + 2)
                with act.Else():
                    with act.Fori(0, units) as c:
                        chunk_silu(c * 2 + hidden + 2, P)
                act.drain()

            sqrt_of(4, 2, st[:, 0:2], std)
            for b in range(NT):
                act.wait_ge(sem("rt_max"), b + 1)
                ac(rt[:, b, 24:28], rt[:, b, 0:4], ACT.Exp, bias=rt[:, b, 28:29], accum_out=rt[:, b, 29:30])
                ac(rt[:, b, 31:32], rt[:, b, 30:31], ACT.Exp).then_inc(sem("rt_exp"), 1)
            moe_silu(0, E1, 0)
            hidden = 2 * E1
            sqrt_of(5, 2, st[:, 0:2], std)

            for l in range(2):
                sqrt_of(6 + 3 * l, 2, st[:, 0:2], std)
                for j, (c, w) in enumerate(IN2_COLS):
                    act.wait_ge(used, USED[f"in2_{l}"][j])
                    bank = 2 * (j % 4)
                    ac(region(R_PJ, NT, D_IN)[:, :, c:c + w], ps[:, bank:bank + 2, 0:w], ACT.Copy).then_inc(sem("pj_in"), 1)
                n_t = -(-NFM // 4)
                fm = region(R_FM, NFM, T)
                for q in range(n_t):
                    act.wait_ge(sem("fm_mm"), n_t * l + q + 1)
                    n = min(4, NFM - 4 * q)
                    src = ps[:, 2 * (q % 2):2 * (q % 2) + 2, :].rearrange("p b (a n) -> p (b a) n", a=2)
                    ac(fm[:, 4 * q:4 * q + n, :], src[:, 0:n, :], ACT.Copy).then_inc(sem("fm_in"), 1)
                for qb in range(NT):
                    act.wait_ge(sem("ix_mm"), NT * l + qb + 1)
                    if qb:
                        act.wait_ge(sem("ix_used"), NT * l + qb)
                    ns = (qb + 1) * P
                    src = ps[:, 4 + 2 * qb:6 + 2 * qb, :].rearrange("p b (a n) -> p (b a) n", a=2)
                    ac(region(R_SM, 4, T)[:, :, 0:ns], src[:, :, 0:ns], ACT.Relu).then_inc(sem("ix_in"), 1)
                sm = region(R_SM, 2, 4, T)
                pt = region(R_PT, 4 * NT * P)

                def exps(j):
                    _, _, n, qb = JOBS[j]
                    ns = (qb + 1) * P
                    act.wait_ge(sem("row_max"), len(JOBS) * l + j + 1)
                    for i in range(n):
                        last = ac(sm[:, j % 2, i, 0:ns], sm[:, j % 2, i, 0:ns], ACT.Exp, bias=amx[:, j % 2, i:i + 1],
                                  accum_out=asum[:, j % 2, i:i + 1])
                    last.then_inc(sem("exped"), 1)

                exps(0)
                for j, (br, h0, n, qb) in enumerate(JOBS):
                    if j + 1 < len(JOBS):
                        exps(j + 1)
                    heads = n // 2 if br == "B" else n
                    act.wait_ge(sem("pt_mm"), len(JOBS) * l + j + 1)
                    if qb:
                        ac(pt[:, 0:heads * 2 * P], all_ps[:, 2048:2048 + heads * 2 * P], ACT.Copy).then_inc(sem("pt_in"), 1)
                    else:
                        ac(pt[:, 0:heads * 2 * P].rearrange("p (h s n) -> p h s n", s=2, n=P)[:, :, 0, :],
                           all_ps[:, 2048:2048 + heads * 2 * P].rearrange("p (h s n) -> p h s n", s=2, n=P)[:, :, 0, :],
                           ACT.Copy).then_inc(sem("pt_in"), 1)
                sqrt_of(7 + 3 * l, 8, st[:, 0:8], st[:, 8:16])
                act.wait_ge(sem("y_t"), l + 1)
                ac(hT[:, :, :], ps[:, 4:8, :].rearrange("p b (a n) -> p (b a) n", a=2), ACT.Copy).then_inc(sem("yT"), 1)
                sqrt_of(8 + 3 * l, 2, st[:, 0:2], std)
                if l == 0:
                    for c in range(NCH):
                        chunk_silu(hidden + 2 * c + 2)
                    hidden += 2 * NCH
            for b in range(NT):
                act.wait_ge(sem("rt_max"), NT + b + 1)
                ac(rt[:, b, 31:32], rt[:, b, 30:31], ACT.Exp).then_inc(sem("rt_exp"), 1)
            moe_silu(1, E2 * NCH, hidden)
            sqrt_of(12, 2, st[:, 0:2], std)

        @block.vector
        def _(dve):
            v = nc.vector
            fence = dve.drain

            def bc(ap, *shape):
                return ap.to_broadcast(list(shape))

            def reduce_angle(r, a, k):
                v.tensor_scalar(k, a, 1.0 / (2 * math.pi), ROUND, ALU.mult, ALU.add)
                fence()
                v.tensor_scalar(k, k, ROUND, None, ALU.subtract)
                fence()
                v.scalar_tensor_tensor(r, k, -TWO_PI[0], a, ALU.mult, ALU.add)
                fence()
                v.scalar_tensor_tensor(r, k, -TWO_PI[1], r, ALU.mult, ALU.add)
                fence()
                v.scalar_tensor_tensor(r, k, -TWO_PI[2], r, ALU.mult, ALU.add)
                fence()
                return v.tensor_scalar(r, r, PI, -PI, ALU.min, ALU.max)

            def ada_sum(a, u):
                s, _, n = PLAN[f"ada{a}"][0][u]
                dve.wait_ge(full[s], DMA3 * n)
                vectors = (0, 8) if a == 0 and u < 4 else (0,) if a == 0 else (16,)
                for k in range(4 if a == 0 else KD):
                    if k:
                        fence()
                    for i, c in enumerate(vectors):
                        acc = ring[:, s, 4096 + i * 512:4096 + (i + 1) * 512]
                        w = ring[:, s, k * 512:(k + 1) * 512]
                        if k == 0:
                            last = v.tensor_scalar(acc, w, cact[:, c:c + 1], None, ALU.mult)
                        else:
                            last = v.scalar_tensor_tensor(acc, w, cact[:, c + k:c + k + 1], acc, ALU.mult, ALU.add)
                last.then_inc(sem("ada_sum"), 1)

            def mod_in(a, u0, u1, bank):
                dve.wait_ge(used, USED[f"ada{a}"][u1 - 1])
                if a == 0 and u0 == 0:
                    both = ps[:, bank, 0:32].rearrange("p (c i) -> p c i", i=2)
                    v.tensor_copy(modc[:, :], both[:, :, 1])
                    v.tensor_copy(modn[:, 0:16], both[:, :, 0])
                    u0 = 4
                at = 16 if a == 0 else 0
                v.tensor_copy(modn[:, 4 * u0:4 * u1], ps[:, bank, at + 4 * u0:at + 4 * u1]).then_inc(sem("mod_in"), 1)

            v.memset(dn[:, :], 0.0).then_inc(sem("act_ready"), 2)
            v.memset(comb[:, :, :], 0.0)
            v.memset(slots[:, :, :], 0.0)
            dve.wait_ge(sem("cols_t"), 1)
            total = sum(k for *_, k in COLS)
            v.tensor_copy(colv[:, 0:total], ps[:, 0, 0:total]).then_inc(sem("cols"), 1)

            dve.wait_ge(sem("filter_in"), 96)
            a, k = (region(R_SQ + i * 256 + 1024, T)[0:64, :] for i in range(2))
            for i in range(2):
                dve.wait_ge(sem("filter_mm"), i + 1)
                v.tensor_scalar(a, ps[0:64, 1 + i, 0:T], fcol[:, i:i + 1], fcol[:, 2:3], ALU.add, ALU.mult)
                fence()
                reduce_angle(region(R_SQ, T)[0:64, :], a, k).then_inc(sem("filter_a"), 1)
            h3 = region(R_H3, NT, 2, 2, DBR)
            dve.wait_ge(sem("c_act"), 1)
            ada_sum(0, 0)
            for b in range(NT):
                ada_sum(0, 1 + b)
                dve.wait_ge(sem("filter_mm"), 3 + b)
                dve.wait_ge(sem("decay"), b + 1)
                v.tensor_tensor(region(R_H3, NT, 2048)[:, b, :], all_ps[:, 2048:4096], region(R_EXP, 2048), ALU.mult
                                ).then_inc(sem("filter_h3"), 1)
            fence()
            v.memset(h3[0:1, 0, :, 1, :], 0.0)
            dve.wait_ge(sem("rows_in"), 16 * N_ROWS_IN)
            for l in range(2):
                for i in range(2):
                    v.tensor_tensor_reduce(lamj, lamr[:, l, 2 * i, :], lamr[:, l, 2 * i + 1, :], 1.0, 0.0,
                                           ALU.mult, ALU.add, lamt[:, 2 * l + i:2 * l + i + 1])
                    fence()
            v.tensor_copy(posf[:, :], posi[:, :]).then_inc(sem("lam_in"), 1)
            fence()
            for b in range(NT):
                v.tensor_scalar(ang[:, 0, b, :], const("inv"), posf[:, b:b + 1], None, ALU.mult)
            fence()
            reduce_angle(ang[:, 2, :, :], ang[:, 0, :, :], ang[:, 1, :, :])
            fence()
            v.scalar_tensor_tensor(ang[:, 3, :, :], ang[:, 2, :, :], -1.0, ang[:, 2, :, :], ALU.mult, ALU.max)
            fence()
            v.tensor_scalar(ang[:, 3, :, :], ang[:, 3, :, :], -1.0, math.pi / 2, ALU.mult, ALU.add).then_inc(sem("ang_in"), 1)
            v.tensor_tensor(region(R_SQ, 4096), region(R_H3, 4096), region(R_H3, 4096), ALU.mult).then_inc(sem("filter_sq"), 1)
            pq = region(R_PQ, NT, 2, 2, DBR)
            for o in range(2):
                v.tensor_tensor(pq[:, :, o, 0, :], h3[:, :, o, 0, :], h3[:, :, o, 1, :], ALU.add)
                last = v.tensor_tensor(pq[:, :, o, 1, :], h3[:, :, o, 1, :], h3[:, :, o, 0, :], ALU.subtract)
            last.then_inc(sem("filter_pq"), 1)
            ada_sum(0, 3)
            ada_sum(0, 4)
            dve.wait_ge(sem("filter_ssum"), 1)
            v.tensor_scalar(kn[:, :], ps[:, 1, 0:8], EPS, None, ALU.add).then_inc(sem("kn_in"), 1)
            dve.wait_ge(sem("kn_sqrt"), 1)
            v.reciprocal(kn[:, :], kn[:, :])
            dve.wait_ge(sem("lam_exp"), 1)
            for l in range(2):
                v.tensor_scalar(lamt[:, 4 + l:5 + l], lamt[:, 2 * l:2 * l + 1], lamt[:, 2 * l + 1:2 * l + 2], LAM_INIT[l],
                                ALU.subtract, ALU.add)
            for u in range(5, 8):
                ada_sum(0, u)
            mod_in(0, 0, 8, 3)
            ada_sum(0, 8)
            dve.wait_ge(sem("spectra_mm"), 1)
            v.tensor_copy(region(R_KF, 4096), all_ps[:, :]).then_inc(sem("spectra_in"), 1)
            v.memset(v1[:, :, :, P:P + 1], 1.0)
            for u in range(9, NA):
                ada_sum(0, u)
            mod_in(0, 8, NA, 3)
            fence()

            def ada(a, n1, n2):
                v.tensor_tensor(mod[:, :], modn[:, :], col(f"ab{a}", 0, 48), ALU.add)
                if a == 0:
                    v.tensor_tensor(modc[:, :], modc[:, :], col("ab0", 0, 16), ALU.add)
                fence()
                if a == 0:
                    v.scalar_tensor_tensor(gac[:, :], modc[:, 8:16], 1.0, col(n1, 0, 8), ALU.add, ALU.mult)
                v.scalar_tensor_tensor(ga[:, 0:8], mod[:, 8:16], 1.0, col(n1, 0, 8), ALU.add, ALU.mult)
                v.scalar_tensor_tensor(ga[:, 8:16], mod[:, 32:40], 1.0, col(n2, 0, 8), ALU.add, ALU.mult)
                fence()

            def gate_rows(a):
                for g in range(16):
                    c = 16 + g if g < 8 else 32 + g
                    last = v.tensor_scalar(xn[:, g * P:(g + 1) * P], ident, mod[:, c:c + 1], None, ALU.mult)
                last.then_inc(sem("diag"), 1)
                dve.wait_ge(sem("gaterow_mm"), a + 1)
                v.tensor_copy(grow[:, :, :].rearrange("p a n -> p (a n)"), all_ps[:, 2048:4096]).then_inc(sem("gaterow_in"), 1)
                fence()

            def rstd(i, src):
                for b in range(NT):
                    v.tensor_tensor_reduce(xn2[:, b, :], src[:, b, :], src[:, b, :], 1.0, 0.0, ALU.mult, ALU.add, st[:, b:b + 1])
                fence()
                v.tensor_scalar(st[:, 0:2], st[:, 0:2], 1.0 / D, EPS, ALU.mult, ALU.add).then_inc(sem("ms"), 1)
                dve.wait_ge(sem("std"), i)
                v.reciprocal(st[:, 4:6], st[:, 2:4])
                fence()

            def norm(i, src, n, dst, gain, shift):
                rstd(i, src)
                for b in range(NT):
                    last = v.tensor_scalar(xn2[:, b, :], src[:, b, :], st[:, 4 + b:5 + b], None, ALU.mult)
                last.then_inc(sem("normed"), 1)
                dve.wait_ge(sem("turned"), n)
                for k in range(KD):
                    last = v.tensor_scalar(dst[:, k, :], ps[:, 4 + k // 2, (k % 2) * T:(k % 2 + 1) * T],
                                           gain[:, k:k + 1], shift[:, k:k + 1], ALU.mult, ALU.add)
                last.then_inc(sem("hT_ready"), 1)

            ada(0, "n1", "n2")
            dve.wait_ge(sem("ctx_in"), 16)
            norm(1, hT[:, :, :].rearrange("p k n -> p (k n)").rearrange("p (b d) -> p b d", b=NT), 1, hTc, gac, modc)
            dve.wait_ge(sem("x_in"), 16)
            norm(2, x, 2, hT, ga, mod)
            gate_rows(0)

            def conv(j0, count, w, wcount, bias, acc):
                acc = acc.rearrange("p (a r c) -> p a r c", a=2, c=GW)
                with dve.Fori(0, count // 2) as i:
                    blocks = (i, i + count // 2)
                    grids = [z[:, bass.ds(b + j0, 1), :].rearrange("p a (r c) -> p (a r) c", c=GW) for b in blocks]
                    for a, b in enumerate(blocks):
                        v.tensor_copy(acc[:, a], bc(colv[:, bass.ds(b + COL[bias], 1)].unsqueeze(2), P, GR, GW))
                    fence()
                    for dr in (-1, 0, 1):
                        for dc in (-1, 0, 1):
                            if dr == dc == 0:
                                continue
                            ro, co = slice(max(0, -dr), GR - max(0, dr)), slice(max(0, -dc), GW - max(0, dc))
                            ri, ci = slice(max(0, dr), GR - max(0, -dr)), slice(max(0, dc), GW - max(0, -dc))
                            tap = ((dr + 1) * 3 + dc + 1) * wcount + COL[w]
                            for a, b in enumerate(blocks):
                                v.scalar_tensor_tensor(acc[:, a, ro, co], grids[a][:, ri, ci], colv[:, bass.ds(b + tap, 1)],
                                                       acc[:, a, ro, co], ALU.mult, ALU.add)
                            fence()
                    for a, b in enumerate(blocks):
                        v.scalar_tensor_tensor(grids[a], grids[a], colv[:, bass.ds(b + 4 * wcount + COL[w], 1)], acc[:, a],
                                               ALU.mult, ALU.add)
                    fence()

            def conv_qk():
                dve.wait_ge(sem("z_in"), 6)
                conv(ZQ, 8, "mcw", 8, "mcb", region(R_VT, 2 * T))
                acc = region(R_VT, NH, T)
                for h in range(NH):
                    v.tensor_scalar(acc[:, h, :], kc[:, h, :], col("mcw", 4 * 8 + 4 + h), col("mcb", 4 + h), ALU.mult, ALU.add)
                fence()
                for tap, (o, i) in ((3, (slice(1, T), slice(0, T - 1))), (5, (slice(0, T - 1), slice(1, T)))):
                    for h in range(NH):
                        v.scalar_tensor_tensor(acc[:, h, o], kc[:, h, i], col("mcw", tap * 8 + 4 + h), acc[:, h, o], ALU.mult, ALU.add)
                    fence()
                v.tensor_copy(kc, acc).then_inc(sem("conv_qk"), 1)

            dve.wait_ge(sem("z_in"), 3)
            conv(0, 12, "hcw", 12, "hcb", xn[:, 0:2 * T])
            dve.wait_ge(sem("vo_mm"), 1)
            for i, (sb0, bank) in enumerate(((2, 6), (0, 0))):
                if i:
                    conv_qk()
                    dve.wait_ge(used, USED["in1"][6])
                for b in range(NT):
                    last = v.tensor_tensor(v1[:, sb0 + b, :, 0:P], ps[:, bank + b, :].rearrange("p (h n) -> p h n", h=NH),
                                           rowv[:, 0:DBR].rearrange("p (h n) -> p h n", h=NH), ALU.add)
                last.then_inc(sem("vo_in"), 1)
            dve.wait_ge(used, USED["in1"][7])
            for b in range(NT):
                last = v.tensor_tensor(og[:, b, :], ps[:, 2 + b, :], rowv[:, DBR:2 * DBR], ALU.add)
            last.then_inc(sem("vo_in"), 1)
            fence()
            v.memset(dn[:, 4:5], 0.0).then_inc(sem("hy_u"), 1)

            dve.wait_ge(sem("gates_mm"), 1)
            for g in range(4):
                last = v.tensor_scalar(gates[:, g % 2, g // 2, :], ps[0:NH, 4 + g, :], gb[:, g:g + 1], None, ALU.add)
            last.then_inc(sem("vo_in"), 1)

            yy = xn[:, :].rearrange("p (r n) -> p r n", r=2)
            dve.wait_ge(sem("fnet_mm"), 2)
            flat_vt = region(R_VT, 1024)
            for o in range(2):
                ada_sum(1, 2 * o)
                dve.wait_ge(sem("hy_spec"), o + 1)
                ur, us = all_ps[:, 0:1024], all_ps[:, 1024:2048]
                kr, ki = (kf[:, o, r, :] for r in range(2))
                v.tensor_tensor(yy[:, 0, :], ur, kr, ALU.mult)
                v.tensor_tensor(flat_vt, us, ki, ALU.mult)
                v.tensor_tensor(yy[:, 1, :], ur, ki, ALU.mult)
                fence()
                v.tensor_tensor(yy[:, 0, :], yy[:, 0, :], flat_vt, ALU.add)
                fence()
                v.tensor_tensor(flat_vt, us, kr, ALU.mult)
                fence()
                v.tensor_tensor(yy[:, 1, :], yy[:, 1, :], flat_vt, ALU.subtract).then_inc(sem("hy_y"), 1)
                fence()
                vt4 = region(R_VT, NBR, T)
                for c in range(NBR):
                    v.tensor_scalar(vt4[:, c, :], z[:, c, :], col("skip", o * NBR + c), None, ALU.mult)
                ada_sum(1, 2 * o + 1)
                dve.wait_ge(sem("hy_inv"), o + 1)
                fence()
                for c in range(NBR):
                    v.scalar_tensor_tensor(vt4[:, c, :], ps[:, 6 + c // 2, (c % 2) * T:(c % 2 + 1) * T],
                                           kn[:, o * NBR + c:o * NBR + c + 1], vt4[:, c, :], ALU.mult, ALU.add)
                fence()
                v.tensor_tensor(z[:, 0:4, :], vt4, z[:, 4 * (o + 1):4 * (o + 2), :], ALU.mult).then_inc(sem("hy_u"), 1)

            mod_in(1, 0, 4, 4)
            fence()
            gi, gf, gB, gm = (region(R_KF + i * 1024, 2, 512)[0:NH] for i in range(4))
            v.tensor_copy(gf, gates[:, 1, :, :]).then_inc(sem("ml_f"), 1)
            v.tensor_copy(gi, gates[:, 0, :, :])
            fence()
            v.tensor_scalar(gates[:, 1, :, :], gf, 0.0, None, ALU.min)
            dve.wait_ge(sem("ml_softplus"), 1)
            fence()
            v.tensor_tensor(gf, gates[:, 1, :, :], gm, ALU.subtract)
            fence()
            v.memset(gm, 0.0)
            fence()

            def scans(dst, src, op, second):
                v.tensor_tensor_scan(dst[:, 0, :], src[:, 0, :], second(src[:, 0, :]), 0.0, op, op)
                v.tensor_tensor_scan(dst[:, 1, 0:T][:, ::-1], src[:, 1, 0:T][:, ::-1], second(src[:, 1, 0:T][:, ::-1]), 0.0, op, op)
                fence()
                v.tensor_tensor_scan(dst[:, 1, T:2 * T][:, ::-1], src[:, 1, T:2 * T][:, ::-1],
                                     second(src[:, 1, T:2 * T][:, ::-1]), dst[:, 1, 0:1], op, op)
                fence()

            scans(gB, gf, ALU.add, lambda s: gm[:, 0, 0:s.shape[-1]])
            v.tensor_tensor(gi, gi, gB, ALU.subtract)
            fence()
            scans(gm, gi, ALU.max, lambda s: s)
            v.tensor_tensor(gf, gB, gm, ALU.add).then_inc(sem("ml_gates"), 1)

            dve.wait_ge(sem("ml_silu"), 1)
            v.tensor_scalar(z[:, ZQ:ZQ + 4, :], z[:, ZQ:ZQ + 4, :], float(P) ** -0.5, None, ALU.mult).then_inc(sem("ml_qk"), 1)
            dve.wait_ge(sem("ml_cols_mm"), 1)
            v.tensor_copy(gcol[:, :], ps[:, 0, 0:32]).then_inc(sem("ml_cols"), 1)
            dve.wait_ge(sem("ml_cols"), 2)
            fence()

            hh = region(R_VT, NT, NH, P)

            def weight_args(j):
                h, d = divmod(j, 2)
                w = xn[:, (j % 2) * 1024:(j % 2 + 1) * 1024].rearrange("p (s n) -> p s n", s=4)
                if j >= 2:
                    dve.wait_ge(sem("ml_pv"), j - 1)
                for s in range(4):
                    c = (d * 4 + s) * 4 + h
                    last = v.tensor_scalar(w[:, s, :], ps[:, 2 + 2 * d + h // 2, (h % 2) * T:(h % 2 + 1) * T], gcol[:, c:c + 1], 0.0,
                                           ALU.add, ALU.min)
                last.then_inc(sem("ml_w"), 1)

            weight_args(0)
            for j in range(8):
                h, d = divmod(j, 2)
                if j + 1 < 8:
                    weight_args(j + 1)
                w = xn[:, (j % 2) * 1024:(j % 2 + 1) * 1024]
                dve.wait_ge(sem("ml_exp"), j + 1)
                v.tensor_tensor(w[:, 512:1024], w[:, 512:1024], const(("upto", "from")[d]), ALU.mult)
                dve.wait_ge(sem("ml_s"), h + 1)
                fence()
                v.tensor_tensor(w, w, all_ps[:, 3072:4096], ALU.mult).then_inc(sem("ml_p"), 1)
                dve.wait_ge(sem("ml_pv"), j + 1)
                den = ps[:, j % 2, :].rearrange("p (b n) -> p b n", b=NT)
                v.tensor_scalar(dn[:, 4:6], den[:, :, P], -1.0, None, ALU.mult)
                fence()
                for b in range(NT):
                    o = (d * 2 + b) * 4 + h
                    v.tensor_scalar(dn[:, b:b + 1], den[:, b, P:P + 1], dn[:, 4 + b:5 + b], en[:, o:o + 1], ALU.max, ALU.max)
                fence()
                v.reciprocal(dn[:, 2:4], dn[:, 0:2])
                fence()
                for b in range(NT):
                    if d == 0:
                        last = v.tensor_scalar(hh[:, b, h, :], den[:, b, 0:P], dn[:, 2 + b:3 + b], None, ALU.mult)
                    else:
                        last = v.scalar_tensor_tensor(hh[:, b, h, :], den[:, b, 0:P], dn[:, 2 + b:3 + b], hh[:, b, h, :],
                                                      ALU.mult, ALU.add)
                last.then_inc(sem("ml_h"), 1)
            fence()
            flat = region(R_VT, 8, P)
            sqs = xn[:, 0:1024].rearrange("p (a n) -> p a n", a=8)
            v.tensor_tensor(sqs, flat, flat, ALU.mult)
            fence()
            v.tensor_reduce(st[:, 0:8], sqs, AX.X, ALU.add)
            fence()
            v.tensor_scalar(st[:, 0:8], st[:, 0:8], 1.0 / P, EPS, ALU.mult, ALU.add).then_inc(sem("ms"), 1)
            dve.wait_ge(sem("std"), 3)
            v.reciprocal(st[:, 8:16], st[:, 8:16])
            fence()
            v.tensor_tensor(flat, flat, bc(st[:, 8:16].unsqueeze(2), P, 8, P), ALU.mult)
            fence()
            v.tensor_tensor(vt, vt, bc(mlnw[:, :].unsqueeze(1), P, NT, DBR), ALU.mult)
            dve.wait_ge(sem("o_gate"), 1)
            fence()
            v.tensor_tensor(vt, vt, og, ALU.mult).then_inc(sem("ml_y"), 1)

            ada_sum(1, 4)
            for j in range(6):
                k, half = divmod(j, 2)
                mod_in(1, 4 + j, 5 + j, 4 * (j % 2) + 3)
                ada_sum(1, 5 + j)
                dve.wait_ge(used, USED["merge"][j])
                dve.wait_ge(sem("mg_sig"), j + 1)
                base = 4 * (j % 2) + 2
                proj = ps[:, base:base + 2, :].rearrange("p b (a n) -> p (b a) n", a=2)
                part = macc[:, half * 4:half * 4 + 4, :]
                if k == 0:
                    v.tensor_tensor(part, sgm[:, j % 2], proj, ALU.mult).then_inc(sem("merged"), 1)
                else:
                    v.tensor_tensor(sgm[:, j % 2], sgm[:, j % 2], proj, ALU.mult)
                    fence()
                    v.tensor_tensor(part, part, sgm[:, j % 2], ALU.add).then_inc(sem("merged"), 1)

            def out_add(stage):
                for half in range(2):
                    h = slice(half * 512, (half + 1) * 512)
                    if stage == "out1":
                        mod_in(1, 10 + half, 11 + half, 4 + half)
                        if half == 0:
                            ada_sum(1, NA - 1)
                    dve.wait_ge(used, USED[stage][half])
                    v.tensor_tensor(xn2[:, :, h], ps[:, 2 * half:2 * half + 2, :], bc(grow[:, 0, h].unsqueeze(1), P, NT, 512), ALU.mult)
                    fence()
                    v.tensor_tensor(x[:, :, h], x[:, :, h], xn2[:, :, h], ALU.add)
                fence()

            def first_of(dst, val, m, n, eq, cs):
                v.tensor_scalar(eq, val, m, None, ALU.is_equal)
                fence()
                v.tensor_tensor_scan(cs, eq, const("zero")[:, 0:n], 0.0, ALU.add, ALU.add)
                fence()
                v.scalar_tensor_tensor(dst, cs, 1.0, eq, ALU.is_equal, ALU.mult)
                fence()

            def top2(b, val, n):
                r = rt[:, b, :]
                v.tensor_reduce(r[:, 32:33], val, AX.X, ALU.max)
                fence()
                first_of(r[:, 48:48 + n], val, r[:, 32:33], n, r[:, 64:64 + n], r[:, 72:72 + n])
                v.scalar_tensor_tensor(r[:, 80:80 + n], r[:, 48:48 + n], TAKEN, val, ALU.mult, ALU.add)
                fence()
                v.tensor_reduce(r[:, 33:34], r[:, 80:80 + n], AX.X, ALU.max)
                fence()
                first_of(r[:, 56:56 + n], r[:, 80:80 + n], r[:, 33:34], n, r[:, 64:64 + n], r[:, 72:72 + n])
                v.tensor_tensor(r[:, 30:31], r[:, 33:34], r[:, 32:33], ALU.subtract).then_inc(sem("rt_max"), 1)

            def top2_weights(b, n, scale, dst):
                r = rt[:, b, :]
                v.tensor_scalar(r[:, 34:35], r[:, 31:32], 1.0, None, ALU.add)
                fence()
                v.reciprocal(r[:, 35:36], r[:, 34:35])
                fence()
                if scale is not None:
                    v.tensor_tensor(r[:, 35:36], r[:, 35:36], scale, ALU.mult)
                    fence()
                v.tensor_tensor(r[:, 36:37], r[:, 35:36], r[:, 31:32], ALU.mult)
                fence()
                v.tensor_scalar(r[:, 64:64 + n], r[:, 48:48 + n], r[:, 35:36], None, ALU.mult)
                fence()
                v.scalar_tensor_tensor(dst, r[:, 56:56 + n], r[:, 36:37], r[:, 64:64 + n], ALU.mult, ALU.add)
                fence()

            def router1():
                dve.wait_ge(sem("router_mm"), 1)
                for b in range(NT):
                    r = rt[:, b, :]
                    v.tensor_tensor(r[:, 0:20], ps[:, 3, b * 32:b * 32 + 20], rb1[:, :], ALU.add)
                    fence()
                    v.tensor_reduce(r[:, 38:39], r[:, 0:4], AX.X, ALU.max)
                    fence()
                    v.tensor_scalar(r[:, 28:29], r[:, 38:39], -1.0, None, ALU.mult)
                    first_of(r[:, 40:44], r[:, 0:4], r[:, 38:39], 4, r[:, 64:68], r[:, 72:76])
                    v.tensor_scalar(r[:, 44:48], r[:, 4:8], r[:, 40:41], None, ALU.mult)
                    for g in range(1, 4):
                        fence()
                        v.scalar_tensor_tensor(r[:, 44:48], r[:, 4 + 4 * g:8 + 4 * g], r[:, 40 + g:41 + g], r[:, 44:48],
                                               ALU.mult, ALU.add)
                    fence()
                    top2(b, r[:, 44:48], 4)
                for b in range(NT):
                    r = rt[:, b, :]
                    dve.wait_ge(sem("rt_exp"), b + 1)
                    v.reciprocal(r[:, 39:40], r[:, 29:30])
                    fence()
                    top2_weights(b, 4, r[:, 39:40], r[:, 88:92])
                    for g in range(4):
                        v.tensor_scalar(comb[:, b, 4 * g:4 * g + 4], r[:, 88:92], r[:, 40 + g:41 + g], None, ALU.mult)
                for b in range(NT):
                    last = v.tensor_copy(msk[:, b, 0:G1], rt[:, b, 40:44])
                last.then_inc(sem("masks"), 1)

            def router2():
                dve.wait_ge(sem("router_mm"), 2)
                for b in range(NT):
                    v.tensor_copy(rt[:, b, 0:E2], ps[:, 3, b * 32:b * 32 + E2])
                fence()
                for b in range(NT):
                    top2(b, rt[:, b, 0:E2], E2)
                for b in range(NT):
                    dve.wait_ge(sem("rt_exp"), NT + b + 1)
                    top2_weights(b, E2, None, comb[:, b, 0:E2])
                for b in range(NT):
                    last = v.tensor_tensor(msk[:, b, :], rt[:, b, 48:56], rt[:, b, 56:64], ALU.add)
                last.then_inc(sem("masks"), 1)

            ya = region(R_YA, NT, D)

            def chunk_act(n, cols=T):
                for hb in range(2):
                    dve.wait_ge(sem("gate_silu"), n - 1 + hb)
                    v.tensor_tensor(region(R_AT, 2, T)[:, hb, 0:cols], region(R_SG, 2, T)[:, hb, 0:cols],
                                    ps[:, hb, cols:2 * cols], ALU.mult).then_inc(sem("act_ready"), 1)

            def moe_act(name, i, jobs, experts, chunks, hidden):
                _, body, _ = PLAN[name]
                dve.wait_ge(sem("counted"), i + 1)
                count = ps[:, 3, 128:160].rearrange("p (b n) -> p b n", b=NT)[:, :, 0:jobs]
                v.tensor_reduce(rt[:, 0, 64:65], count[:, NT - 1, :], AX.X, ALU.max)
                v.tensor_tensor(slots[:, :, 0:jobs], count, msk[:, :, 0:jobs], ALU.mult)
                iota = region(R_IOTA, P)
                v.tensor_tensor_scan(iota, const("ones"), const("ones"), 0.0, ALU.mult, ALU.add)
                fence()
                v.tensor_scalar(flags[:, i:i + 1], rt[:, 0, 64:65], float(P), None, ALU.is_gt).then_inc(sem("flag"), 1)
                dve.wait_ge(sem("flag"), i + 1)
                over = dve.value_load(flags[P - 1:P, i:i + 1], min_val=0, max_val=1)
                sel, selT, ye, he = region(R_SE, NT, P), region(R_ST, T), region(R_YE, D), region(R_HE, KD, P)

                def select(j):
                    for b in range(NT):
                        last = v.tensor_scalar(sel[:, b, :], iota, slots[:, b, bass.ds(j, 1)], None, ALU.is_equal)
                    last.then_inc(sem(f"{name}_sel"), 1)

                def gathered(j):
                    dve.wait_ge(sem(f"{name}_gathered"), j + 1)
                    for k in range(KD):
                        last = v.tensor_scalar(he[:, k, :], ps[:, 2 + k // 4, (k % 4) * P:(k % 4 + 1) * P],
                                               ga[:, 8 + k:9 + k], mod[:, 24 + k:25 + k], ALU.mult, ALU.add)
                    last.then_inc(sem(f"{name}_he"), 1)
                    dve.wait_ge(sem(f"{name}_placed"), j + 1)
                    v.tensor_copy(selT, ps[:, 0, 0:T])
                    v.tensor_copy(wslot[:, 0:experts], ps[:, 0, T:T + experts]).then_inc(sem(f"{name}_selT"), 1)

                with dve.If(over > 0):
                    v.memset(ya, 0.0).then_inc(sem(f"{name}_y_read"), 1)
                    with dve.Fori(0, jobs) as j:
                        for c in range(body):
                            chunk_act(j * (2 * body) + hidden + 2 * c + 2)
                            if c % chunks == chunks - 1:
                                fence()
                                dve.wait_ge(used, j * body + START[name] + c + 1)
                                e = j * experts + c // chunks
                                for b in range(NT):
                                    last = v.scalar_tensor_tensor(ya[:, b, :], all_ps[:, 2048 + b * 1024:3072 + b * 1024],
                                                                  comb[:, b, bass.ds(e, 1)], ya[:, b, :], ALU.mult, ALU.add)
                                last.then_inc(sem(f"{name}_y_read"), 1)
                    fence()
                    ffn_add(ya).then_inc(sem("block_done"), 1)
                with dve.Else():
                    v.memset(selT, 0.0)
                    v.memset(ye, 0.0).then_inc(sem(f"{name}_zero"), 1)
                    v.memset(dn[:, :], 0.0).then_inc(sem(f"{name}_ye"), 1)
                    select(0)
                    gathered(0)
                    with dve.Fori(0, jobs) as j:
                        select(j + 1)
                        for c in range(body):
                            chunk_act(j * (2 * body) + hidden + 2 * c + 2, P)
                            if c % chunks == chunks - 1:
                                x_ = c // chunks
                                fence()
                                dve.wait_ge(used, j * body + START[name] + c + 1)
                                if x_ == 0:
                                    v.tensor_scalar(ye, all_ps[:, 1024:2048], wslot[:, 0:1], None, ALU.mult
                                                    ).then_inc(sem(f"{name}_ye"), 1)
                                else:
                                    v.scalar_tensor_tensor(ye, all_ps[:, 1024:2048], wslot[:, x_:x_ + 1], ye, ALU.mult, ALU.add
                                                           ).then_inc(sem(f"{name}_ye"), 1)
                        gathered(j + 1)
                    ffn_add(ps[:, 4:8, :].rearrange("p (b a) n -> p b (a n)", b=NT)).then_inc(sem("block_done"), 1)
                fence()

            def ffn_add(src):
                v.tensor_tensor(xn2, src, bc(grow[:, 1, :].unsqueeze(1), P, NT, D), ALU.mult)
                fence()
                return v.tensor_tensor(x[:, :, :], x[:, :, :], xn2, ALU.add)

            out_add("out1")
            norm(4, x, 3, hT, ga[:, 8:16], mod[:, 24:32])
            router1()
            moe_act("moe1", 0, G1, 4, 1, 0)
            hidden = 2 * E1
            rstd(5, x)
            dve.wait_ge(sem("late_in"), 32)
            for b in range(NT):
                v.scalar_tensor_tensor(x[:, b, :], x[:, b, :], st[:, 4 + b:5 + b], late[:, 0:D], ALU.mult, ALU.mult)
            fence()

            for l in range(2):
                ada(l + 1, f"ga{l}", f"gf{l}")
                norm(6 + 3 * l, x, 4 + 2 * l, hT, ga, mod)
                gate_rows(l + 1)
                pj = region(R_PJ, NT, D_IN)
                dve.wait_ge(sem("pj_in"), 6 * (l + 1))
                spans = ((O_QA, A_H + 1, HD, 8, 0), (O_QI, 5, HD, 8, 0), (O_QB, 16, 32, 4, 8), (O_QC, 2 * C_H, HD, 8, 0))
                for b in range(NT):
                    at, parts = R_SM + b * 1024, []
                    for off, heads, w, half, f in spans:
                        n = heads * half
                        heads_ = pj[:, b, off:off + heads * w].rearrange("p (h n) -> p h n", n=w)
                        x1, x2 = heads_[:, :, 0:half], heads_[:, :, half:2 * half]
                        c_, s_ = (bc(t[:, b, f:f + half].unsqueeze(1), P, heads, half) for t in (cosn, sinn))
                        t_ = [region(at + i * n, heads, half) for i in range(4)]
                        at += 4 * n
                        for t, a_, w_ in zip(t_, (x1, x2, x2, x1), (c_, s_, c_, s_)):
                            v.tensor_tensor(t, a_, w_, ALU.mult)
                        parts.append((x1, x2, t_))
                    fence()
                    for x1, x2, t_ in parts:
                        v.tensor_tensor(x1, t_[0], t_[1], ALU.subtract)
                        last = v.tensor_tensor(x2, t_[2], t_[3], ALU.add)
                    v.tensor_scalar(wix[:, b, :], pj[:, b, O_WI:O_WI + 4], 0.5 * 0.125, None, ALU.mult)
                last.then_inc(sem("roped"), 1)
                fence()
                dve.wait_ge(sem("fm_in"), -(-NFM // 4) * (l + 1))
                fm = region(R_FM, NFM, T)
                for i in range(2 * B_H):
                    last = v.tensor_scalar(hT[:, i, :], fm[:, FM_QB + i // 4, :], const("quarter")[:, i % 4:i % 4 + 1], None, ALU.mult)
                last.then_inc(sem("qb_masked"), 1)

                causal = const2("causal")
                sel = region(R_SEL, 2, T)
                for qb in range(NT):
                    ns = (qb + 1) * P
                    dve.wait_ge(sem("ix_in"), NT * l + qb + 1)
                    rel = region(R_SM, 4, T)
                    sc = [region(R_IX, 2, T)[:, i, 0:ns] for i in range(2)]
                    v.tensor_scalar(sc[0], rel[:, 0, 0:ns], wix[:, qb, 0:1], None, ALU.mult)
                    for h in range(1, 4):
                        fence()
                        last = v.scalar_tensor_tensor(sc[0], rel[:, PAIRS[4][h], 0:ns], wix[:, qb, h:h + 1], sc[0], ALU.mult, ALU.add)
                    last.then_inc(sem("ix_used"), 1)
                    fence()
                    v.tensor_tensor(sc[0], sc[0], causal[:, qb, 0:ns], ALU.add)
                    for i in range(TOPK // 8):
                        fence()
                        v.max(top[:, :], sc[i % 2])
                        fence()
                        v.match_replace(sc[(i + 1) % 2], top[:, :], sc[i % 2], TAKEN)
                    fence()
                    v.tensor_scalar(sc[1], sc[0], TAKEN / 1.5, MASKED, ALU.is_gt, ALU.mult)
                    fence()
                    v.tensor_tensor(sel[:, qb, 0:ns], sc[1], causal[:, qb, 0:ns], ALU.add)
                    fence()

                sm = region(R_SM, 2, 4, T)

                def mask_scores(j):
                    br, h0, n, qb = JOBS[j]
                    ns = (qb + 1) * P
                    dve.wait_ge(sem("s_mm"), len(JOBS) * l + j + 1)
                    if j >= 2:
                        dve.wait_ge(sem("pt_mm"), len(JOBS) * l + j - 1)
                    scale = float(32 if br == "B" else HD) ** -0.5
                    mask = (sel if br == "A" else causal)[:, qb, 0:ns]
                    bank = 2 * (j % 2)
                    s_ = ps[:, bank:bank + 2, :].rearrange("p b (a n) -> p (b a) n", a=2)
                    s_ = s_[:, 0:n, 0:ns] if br == "B" or n == 4 else s_[:, 0:4:2, 0:ns]
                    v.scalar_tensor_tensor(sm[:, j % 2, 0:n, 0:ns], s_, scale, bc(mask.unsqueeze(1), P, n, ns), ALU.mult, ALU.add
                                           ).then_inc(sem("masked"), 1)
                    fence()
                    v.tensor_reduce(amx[:, j % 2, 0:n], sm[:, j % 2, 0:n, 0:ns], AX.X, ALU.max)
                    fence()
                    v.tensor_scalar(amx[:, j % 2, 0:n], amx[:, j % 2, 0:n], -1.0, None, ALU.mult).then_inc(sem("row_max"), 1)

                def probs(j):
                    br, h0, n, qb = JOBS[j]
                    ns = (qb + 1) * P
                    fence()
                    dve.wait_ge(sem("exped"), len(JOBS) * l + j + 1)
                    last = v.reciprocal(ars[:, j % 2, 0:n], asum[:, j % 2, 0:n])
                    if br == "B":
                        fence()
                        for i in range(0, n, 2):
                            v.tensor_scalar(sm[:, j % 2, i + 1, 0:ns], sm[:, j % 2, i + 1, 0:ns], ars[:, j % 2, i + 1:i + 2],
                                            lamt[:, 4 + l:5 + l], ALU.mult, ALU.mult)
                        fence()
                        for i in range(0, n, 2):
                            last = v.scalar_tensor_tensor(sm[:, j % 2, i, 0:ns], sm[:, j % 2, i, 0:ns], ars[:, j % 2, i:i + 1],
                                                          sm[:, j % 2, i + 1, 0:ns], ALU.mult, ALU.subtract)
                    last.then_inc(sem("probs"), 1)

                def outputs_in(j):
                    br, h0, n, qb = JOBS[j]
                    dve.wait_ge(sem("o_mm"), len(JOBS) * l + j + 1)
                    heads = n // 2 if br == "B" else n
                    c = {"A": h0 * HD, "B": A_H * HD + h0 // 2 * HD, "C": (A_H + B_H + h0) * HD}[br]
                    dst = xn2[:, qb, c:c + heads * HD].rearrange("p (h n) -> p h n", n=HD)
                    src = ps[:, 6 + j % 2, 0:heads * HD].rearrange("p (h n) -> p h n", n=HD)
                    if br == "B":
                        last = v.tensor_copy(dst, src)
                    elif n == 2:
                        last = v.tensor_tensor(dst, src, bc(ars[:, j % 2, 0:n].unsqueeze(2), P, n, HD), ALU.mult)
                    else:
                        last = v.tensor_tensor(dst.rearrange("p (a b) n -> p b a n", a=2), src.rearrange("p (b a) n -> p b a n", b=2),
                                               bc(ars[:, j % 2, 0:4].rearrange("p (b a) -> p b a", b=2).unsqueeze(3), P, 2, 2, HD),
                                               ALU.mult)
                    last.then_inc(sem("o_in"), 1)

                mask_scores(0)
                for j in range(len(JOBS)):
                    if j + 1 < len(JOBS):
                        mask_scores(j + 1)
                    probs(j)
                    if j:
                        outputs_in(j - 1)
                outputs_in(len(JOBS) - 1)
                fence()
                yb = xn2[:, :, A_H * HD:(A_H + B_H) * HD]
                sq2 = region(R_SM, NT, B_H * HD)
                v.tensor_tensor(sq2, yb, yb, ALU.mult)
                fence()
                v.tensor_reduce(st[:, 0:8], region(R_SM, 8, HD), AX.X, ALU.add)
                fence()
                v.tensor_scalar(st[:, 0:8], st[:, 0:8], 1.0 / HD, SUB_EPS, ALU.mult, ALU.add).then_inc(sem("ms"), 1)
                dve.wait_ge(sem("std"), 7 + 3 * l)
                v.reciprocal(st[:, 8:16], st[:, 8:16])
                fence()
                for b in range(NT):
                    yb_ = yb[:, b, :].rearrange("p (h n) -> p h n", n=HD)
                    v.tensor_tensor(yb_, yb_, bc(st[:, 8 + 4 * b:12 + 4 * b].unsqueeze(2), P, B_H, HD), ALU.mult)
                fence()
                for b in range(NT):
                    yb_ = yb[:, b, :].rearrange("p (h n) -> p h n", n=HD)
                    last = v.scalar_tensor_tensor(yb_, yb_, 1.0 - LAM_INIT[l], bc(subln[:, l, :].unsqueeze(1), P, B_H, HD),
                                                  ALU.mult, ALU.mult)
                last.then_inc(sem("y_rows"), 1)

                out_add(f"out2_{l}")
                norm(8 + 3 * l, x, 5 + 2 * l, hT, ga[:, 8:16], mod[:, 24:32])
                if l == 0:
                    ada_sum(2, 0)
                    for c in range(NCH):
                        chunk_act(hidden + 2 * c + 2)
                        ada_sum(2, c + 1)
                    mod_in(2, 0, NA, 2)
                    hidden += 2 * NCH
                    ffn_add(ps[:, 4:8, :].rearrange("p (b a) n -> p b (a n)", b=NT)).then_inc(sem("block_done"), 1)
                    fence()
            router2()
            moe_act("moe2", 1, E2, 1, NCH, hidden)
            rstd(12, x)
            dve.wait_ge(sem("late_in"), 32)
            for b in range(NT):
                last = v.scalar_tensor_tensor(xn2[:, b, :], x[:, b, :], st[:, 4 + b:5 + b], late[:, D:2 * D], ALU.mult, ALU.mult)
            last.then_inc(sem("y_final"), 1)


_INS = ["x", "c", "ctx", "c_ctx", "ada_w", "ada_b", "norm1_w", "norm2_w", "w_in", "b_in", "hy_conv_w", "hy_conv_b", "hy_f_w1",
        "hy_f_b1", "hy_f_w2", "hy_f_b2", "hy_f_w3", "hy_f_freq", "hy_decay", "hy_skip", "ml_conv_w", "ml_conv_b",
        "ml_norm_w", "w_branch", "w_out", "moe_rg_w", "moe_rg_b", "moe_re_w", "moe_re_b", "moe_w_gate", "moe_w_up",
        "moe_w_down", "norm_f_w", "c_2", "positions_2", "w_in_2", "w_out_2", "diff_lambda_2", "diff_subln_2",
        "w_ada_2", "b_ada_2", "g_attn_2", "g_ffn_2", "w_ff_gate_2", "w_ff_up_2", "w_ff_down_2", "w_router_2",
        "w_exp_gate_2", "w_exp_up_2", "w_exp_down_2", "g_final_2"]


def kernel(**inputs):
    import concourse.bacc as bacc
    from concourse.bass_utils import run_bass_kernel_spmd

    nc = bacc.Bacc("TRN2", target_bir_lowering=False, num_devices=1)
    arrays, aps = {}, {}
    for name in _INS:
        a = np.ascontiguousarray(inputs[name])
        arrays[f"in_{name}"] = a
        aps[name] = nc.dram_tensor(f"in_{name}", a.shape, mybir.dt.from_np(a.dtype), kind="ExternalInput").ap()
    aps["b_in_gate"] = aps["b_in"][:, GATE0:GATE0 + 3 * D]
    arrays["in_tables"] = shape_constants()
    tables = nc.dram_tensor("in_tables", (P, NCONST), F32, kind="ExternalInput").ap()
    out = nc.dram_tensor("out_y", (1, T, D), F32, kind="ExternalOutput").ap()
    build(nc, aps, tables, out)
    got = run_bass_kernel_spmd(nc, [arrays], core_ids=[0])
    return got.results[0]["out_y"]
```

```python
import math
from contextlib import ExitStack

import concourse.bass as bass
import numpy as np
from concourse import mybir

F32 = mybir.dt.float32
I32 = mybir.dt.int32
ALU = mybir.AluOpType
ACT = mybir.ActivationFunctionType
AX = mybir.AxisListType

P = 128
T = 256
NT = T // P
D = 1024
KD = D // P
DBR = D // 2
NBR = DBR // P
NH = 4
GW, GR = 64, T // 64
ML0 = 3 * DBR + DBR
MLG0 = ML0 + 4 * DBR
GATE0 = MLG0 + 16
E1, E1H = 16, D // 4
FF = 2816
CH = 256
NCH = FF // CH
E2 = 8
A_H, B_H, C_H, HD = 6, 4, 6, 64
O_QA, O_KA, O_VA, O_QI, O_KI, O_WI = 0, 384, 448, 512, 768, 832
O_QB, O_KB, O_VB, O_QC, O_KC, O_VC, D_IN = 836, 1092, 1348, 1604, 1988, 2372, 2756
TOPK = T // 4
EPS, SUB_EPS = 1e-6, 1e-5
MASKED = -1e30
TAKEN = -3e38
ROUND = 12582912.0
TWO_PI = (6.28125, 0.0019350051879882812, 3.019916150957033e-07)
PI = 3.1415925

NS = 3
SLOT = 6144

CONST = {}
_at = 0
for _n, _w in (("ident", P), ("ones", P), ("feats", T), ("cs", NT * T), ("ss", NT * T), ("ict", NT * T),
               ("ist", NT * T), ("ccsc", 2 * P), ("cl", NT * T), ("sl", NT * T), ("causal", NT * T),
               ("upto", NT * T), ("from", NT * T), ("negsel", NH * P), ("tneg", NT), ("inv", 12), ("zero", 8), ("quarter", 4)):
    CONST[_n] = (_at, _w)
    _at += _w
NCONST = _at

COLS = [("c", "c", 0, 8), ("c_ctx", "c_ctx", 0, 8), ("c_2", "c_2", 0, 8), ("n1", "norm1_w", 0, 8), ("n2", "norm2_w", 0, 8),
        ("ga0", "g_attn_2", 0, 8), ("ga1", "g_attn_2", 8, 8), ("gf0", "g_ffn_2", 0, 8), ("gf1", "g_ffn_2", 8, 8),
        ("hcb", "hy_conv_b", 0, 12), ("mcb", "ml_conv_b", 0, 8), ("skip", "hy_skip", 0, 8),
        ("ab0", "ada_b", 0, 48), ("ab1", "b_ada_2", 0, 48), ("ab2", "b_ada_2", 48, 48),
        ("bz", "b_in", 0, 24), ("bg", "b_in_gate", 0, 24),
        ("hcw", "hy_conv_w", 0, 108), ("mcw", "ml_conv_w", 0, 72)]
COL = {}
_at = 0
for _n, _s, _r, _k in COLS:
    COL[_n] = _at
    _at += _k
NCOLB = -(-_at // P)


def shape_constants():
    blob = np.zeros((P, NCONST), np.float32)

    def put(name, a):
        o, w = CONST[name]
        blob[: a.shape[0], o:o + w] = a.reshape(a.shape[0], w)

    def rows(a):
        return a.reshape(NT, P, -1).transpose(1, 0, 2)

    put("ident", np.eye(P))
    put("ones", np.ones((P, P)))
    t = np.arange(T, dtype=np.float32) / np.float32(T)
    bands = np.linspace(1e-4, 15, 16, dtype=np.float32)
    ang = np.float32(2 * math.pi) * t[:, None] * bands[None, :]
    put("feats", np.concatenate([t[:, None], np.cos(ang), np.sin(ang)], -1).T)
    w = np.outer(np.arange(T), 2 * np.arange(T) + 1) * (math.pi / (2 * T))
    put("cs", rows(np.cos(w)))
    put("ss", rows(np.sin(w)))
    put("ict", rows(np.cos(w).T / T))
    put("ist", rows(-np.sin(w).T / T))
    f = np.outer(np.arange(P), np.arange(P)) * (2 * math.pi / P)
    put("ccsc", np.concatenate([np.cos(f), np.sin(f)], -1))
    g = np.outer(np.arange(T), np.arange(T)) * (2 * math.pi / T)
    put("cl", rows(np.cos(g) / math.sqrt(T * P)))
    put("sl", rows(-np.sin(g) / math.sqrt(T * P)))
    low = np.tril(np.ones((T, T)))
    put("causal", rows(np.where(low > 0, 0.0, MASKED)))
    put("upto", rows(low.T))
    put("from", rows(low))
    sel = np.zeros((NH, NH, P))
    for h in range(NH):
        sel[h, h] = -1.0
    put("negsel", sel)
    put("tneg", -t.reshape(NT, P).T)
    inv = [1.0 / (500000.0 ** (np.arange(0, r, 2, dtype=np.float32) / r)) for r in (16, 8)]
    put("quarter", (np.arange(P)[:, None] // 32 == np.arange(4)).astype(np.float32))
    put("inv", np.tile(np.concatenate(inv).astype(np.float32), (P, 1)))
    return blob


G1 = E1 // 4
NA = 12
STAGES = ([("ada0", 4, 0)] + 4 * [("ada0", 1, 0), ("in1", 1, 0)]
          + [("in1", 1, 0), ("ada0", 1, 0), ("in1", 2, 0), ("ada0", 1, 0), ("in1", 1, 0), ("ada0", 2, 0), ("ada1", 3, 0)]
          + 6 * [("ada1", 1, 0), ("merge", 1, 0)]
          + 2 * [("ada1", 1, 0), ("out1", 1, 0)] + [("ada1", 1, 0), ("moe1", E1, 4), ("in2_0", 6, 0), ("out2_0", 2, 0)]
          + NCH * [("ada2", 1, 0), ("ff", 1, 0)] + [("ada2", 1, 0), ("in2_1", 6, 0), ("out2_1", 2, 0), ("moe2", NCH * E2, NCH)])
TURNS = {4: ((0, 1, 2, 1), (0, 2, 1)), NCH: (tuple(c % NS for c in range(NCH)), (2, 0, 1))}


def unit_plan():
    plan, n, used, full = {}, 0, [0] * NS, [0] * NS
    for at, (name, count, body) in enumerate(STAGES):
        entries = []
        if body:
            slots = TURNS[body][0]
            per_slot = [slots.count(s) for s in range(NS)]
            for c, s in enumerate(slots):
                before = [b for b in range(c) if slots[b] == s]
                after = [b for b in range(body) if slots[b] == s]
                free = n + before[-1] + 1 if before else n - body + after[-1] + 1
                if not before:
                    free = max(free, used[s])
                assert free <= n + c
                entries.append((s, free, full[s] + 1 + len(before)))
            n += count
            for s in range(NS):
                used[s] = n - body + max(b for b in range(body) if slots[b] == s) + 1
                full[s] += count // body * per_slot[s]
            plan[name] = (entries, body, per_slot)
            continue
        ahead = STAGES[at:]
        loop = next(i for i, (_, _, b) in enumerate(ahead) if b)
        final = n + sum(k for _, k, _ in ahead[:loop])
        turn = TURNS[ahead[loop][2]][1]
        for _ in range(count):
            s = turn[(n - final) % NS]
            entries.append((s, used[s], full[s] + 1))
            n += 1
            used[s], full[s] = n, full[s] + 1
        plan[name] = (plan.get(name, ((),))[0] + tuple(entries), 0, None)
    return plan


PLAN = unit_plan()
START = {}
USED = {}
_at = 0
for _n, _k, _body in STAGES:
    if _body:
        START[_n] = _at
    USED.setdefault(_n, []).extend(range(_at + 1, _at + _k + 1))
    _at += _k

IN1_COLS = (0, DBR, 2 * DBR, ML0, ML0 + DBR, 3 * DBR, ML0 + 2 * DBR, ML0 + 3 * DBR)
IN2_COLS = tuple((c, min(512, D_IN - c)) for c in range(0, D_IN, 512))
ZQ, ZK, ZFN = 12, 16, 20

R_Z, R_KF, R_KC, R_V1, R_OG, R_VT, ARENA = 0, 6144, 10240, 11264, 13328, 14352, 15376
R_H3, R_SQ, R_PQ, R_DEC, R_W3, R_EXP, R_ROWS = 0, 4096, 8192, 8192, 10240, 12288, 14336
R_PJ, R_FM, R_SM, R_PT, R_IX, R_SEL = 0, 5512, 10376, 12424, 13448, 13960
R_SG, R_AT, R_YA, R_HE, R_SE, R_ST, R_YE, R_IOTA = 0, 512, 1024, 3072, 4096, 4352, 4608, 5632

FM_COLS = (0, 128, 256, 384, 320, 512, 640, 768, 704, 836, 964, 1092, 1220, 1604, 1732, 1860, 1988, 2116, 2244)
FM_QA, FM_KA, FM_QI, FM_KI, FM_QB, FM_KB, FM_QC, FM_KC = 0, (3, 4), 5, (7, 8), 9, 11, 13, 16
NFM = len(FM_COLS)

JOBS = [(br, h0, n, qb) for br, h0, n in (("B", 0, 4), ("B", 4, 4), ("C", 0, 4), ("C", 4, 2), ("A", 0, 4), ("A", 4, 2))
        for qb in range(NT)]
RMS = ("ctx", "x1", "x2", "final1", "a0", "f0", "a1", "f1", "final2")
TRS = ("ctx", "x1", "x2", "a0", "f0", "a1", "f1")
PAIRS, TILE = {4: (0, 2, 1, 3), 2: (0, 1)}, {4: 1, 2: 2}
LAM_INIT = [0.8 - 0.6 * math.exp(-0.3 * l) for l in range(2)]


def build(nc, A, blob_in, out):
    with ExitStack() as ctx:
        def sb(name, shape, dt=F32):
            return ctx.enter_context(nc.sbuf_tensor(name, shape, dt))

        sems = {}

        def sem(name):
            if name not in sems:
                sems[name] = ctx.enter_context(nc.semaphore(name))
            return sems[name]

        ring = sb("ring", [P, NS, SLOT])
        blob = sb("blob", [P, NCONST])
        colv = sb("colv", [P, NCOLB * P])
        x = sb("x", [P, NT, D])
        xn = sb("xn", [P, NT * D])
        hT = sb("hT", [P, KD, T])
        late = sb("late", [P, 2 * D])
        grow = sb("grow", [P, 2, D])
        arena = sb("arena", [P, ARENA])
        rowv = sb("rowv", [P, 2 * DBR])
        mlnw = sb("mlnw", [P, DBR])
        subln = sb("subln", [P, 2, HD])
        lamt = sb("lamt", [P, 8])
        rb1 = sb("rb1", [P, 20])
        wmlg = sb("wmlg", [P, KD, 16])
        rw1 = sb("rw1", [P, KD, 20])
        rw2 = sb("rw2", [P, KD, E2])
        gb = sb("gb", [NH, 4])
        fcol = sb("fcol", [64, 3])
        cact = sb("cact", [P, 24])
        mod = sb("mod", [P, 48])
        modn = sb("modn", [P, 48])
        modc = sb("modc", [P, 16])
        ga = sb("ga", [P, 16])
        gac = sb("gac", [P, 8])
        kn = sb("kn", [P, 8])
        st = sb("st", [P, 16])
        comb = sb("comb", [P, NT, E1 + 4])
        msk = sb("msk", [P, NT, E2])
        slots = sb("slots", [P, NT, E2 + 1])
        wslot = sb("wslot", [P, 4])
        flags = sb("flags", [P, 2], I32)
        rt = sb("rt", [P, NT, 96])
        gcol = sb("gcol", [P, 32])
        en = sb("en", [P, 16])
        dn = sb("dn", [P, 16])
        posi = sb("posi", [P, NT], I32)
        posf = sb("posf", [P, NT])
        ang = rt[:, :, :].rearrange("p b n -> p (b n)")[:, 0:96].rearrange("p (a b n) -> p a b n", a=4, b=NT)
        lamj = rt[:, 1, 0:32]
        cosn = sb("cosn", [P, NT, 12])
        sinn = sb("sinn", [P, NT, 12])
        amx = sb("amx", [P, 2, 4])
        asum = sb("asum", [P, 2, 4])
        ars = sb("ars", [P, 2, 8])
        top = sb("top", [P, 8])
        wix = sb("wix", [P, NT, 4])
        ps = ctx.enter_context(nc.psum_tensor("ps", [P, 8, 512], F32))

        def const(name, n=P):
            o, w = CONST[name]
            return blob[0:n, o:o + w]

        def const2(name):
            return const(name).rearrange("p (b n) -> p b n", b=NT)

        def region(off, *shape):
            n = int(np.prod(shape))
            v = arena[:, off:off + n]
            if len(shape) == 1:
                return v
            names = "abcd"[:len(shape)]
            return v.rearrange(f"p ({' '.join(names)}) -> p {' '.join(names)}", **dict(zip(names, shape)))

        def col(name, k, n=1):
            return colv[:, COL[name] + k:COL[name] + k + n]

        ident = const("ident")
        vrows = region(R_ROWS, NCOLB, P)
        fw1 = region(R_ROWS + 512, 64)[0:33]
        fw2 = region(R_ROWS + 576, 64)[0:64]
        lamr = region(R_ROWS + 640, 2, 4, 32)
        gates = late[0:NH, :].rearrange("p (i d n) -> p i d n", i=2, d=2)
        z = region(R_Z, 24, T)
        kf = region(R_KF, 2, 2, 2 * DBR)
        kc = region(R_KC, NBR, T)
        v1 = region(R_V1, 4, NH, P + 1)
        og = region(R_OG, NT, DBR)
        vt = region(R_VT, NT, DBR)
        macc = region(R_KF, KD, T)
        sgm = region(R_KF + KD * T, 2, NBR, T)
        xn2 = xn[:, :].rearrange("p (b n) -> p b n", b=NT)
        hTc = late[:, :].rearrange("p (k n) -> p k n", k=KD)
        all_ps = ps[:, :, :].rearrange("p b n -> p (b n)")
        full = [sem(f"slot{s}_full") for s in range(NS)]
        used = sem("units_used")
        DMA3 = 48

        gate_in = grow[0:16, 1, 0:512]

        N_COLS_IN = [sum(1 + (COL[n] // P != (COL[n] + k - 1) // P) for n, _, _, k in COLS[i::2]) for i in range(2)]
        N_ROWS_IN = 12

        block = ctx.enter_context(nc.Block())

        @block.sync
        def _(sp):
            def enter(entry):
                s, free, _ = entry
                if free:
                    sp.wait_ge(used, free)
                return s

            def columns(s, src, width):
                dst = ring[:, s, 0:KD * width].rearrange("p (k n) -> p k n", k=KD)
                for a, b in ((0, 3), (3, 6), (6, 8)):
                    sp.dma_start(dst[:, a:b, :], src[a * P:b * P, :].rearrange("(k p) n -> p k n", p=P)).then_inc(full[s], 16)

            def chunk(s, wg, wu, wd):
                for i, w in enumerate((wg, wu)):
                    sp.dma_start(ring[:, s, i * 2048:(i + 1) * 2048].rearrange("p (k n) -> p k n", k=KD),
                                 w.rearrange("(k p) n -> p k n", p=P)).then_inc(full[s], 16)
                sp.dma_start(ring[:, s, 4096:SLOT].rearrange("p (k n) -> p k n", k=2),
                             wd.rearrange("(k p) n -> p k n", p=P)).then_inc(full[s], 16)

            def straight(name, j):
                s = enter(PLAN[name][0][j])
                h, c = slice(j * 512, (j + 1) * 512), slice(j * CH, (j + 1) * CH)
                if name == "ada0":
                    columns(s, A["ada_w"][0, :, h], 512)
                elif name in ("ada1", "ada2"):
                    columns(s, A["w_ada_2"][int(name[3]) - 1, :, h], 512)
                elif name == "in1":
                    columns(s, A["w_in"][0, :, IN1_COLS[j]:IN1_COLS[j] + 512], 512)
                elif name == "out1":
                    columns(s, A["w_out"][0, :, h], 512)
                elif name.startswith("in2"):
                    o, w = IN2_COLS[j]
                    columns(s, A["w_in_2"][int(name[-1]), :, o:o + w], w)
                elif name.startswith("out2"):
                    columns(s, A["w_out_2"][int(name[-1]), :, h], 512)
                elif name == "ff":
                    chunk(s, A["w_ff_gate_2"][0, :, c], A["w_ff_up_2"][0, :, c], A["w_ff_down_2"][0, c, :])
                else:
                    gate_and_branch(s, j)

            def gate_and_branch(s, j):
                k, half = divmod(j, 2)
                src = A["w_in"][0, :, GATE0 + j * 512:GATE0 + (j + 1) * 512]
                dst = ring[:, s, 0:4096].rearrange("p (k n) -> p k n", k=KD)
                for a in (0, 4):
                    sp.dma_start(dst[:, a:a + 4, :],
                                 src[a * P:(a + 4) * P, :].rearrange("(k p) n -> p k n", p=P)).then_inc(full[s], 16)
                sp.dma_start(ring[:, s, 4096:SLOT].rearrange("p (k n) -> p k n", k=NBR),
                             A["w_branch"][0, k, :, half * 512:(half + 1) * 512].rearrange("(k p) n -> p k n", p=P)
                             ).then_inc(full[s], 16)

            sp.wait_ge(sem("filter_in"), 96)
            sp.wait_ge(sem("more_cols_in"), 16 * N_COLS_IN[1])
            loop1 = next(i for i, stage in enumerate(STAGES) if stage[0] == "moe1")
            done = {}
            for name, n, _ in STAGES[:loop1]:
                for j in range(done.get(name, 0), done.get(name, 0) + n):
                    straight(name, j)
                done[name] = done.get(name, 0) + n
            g1, u1, d1 = A["moe_w_gate"][0], A["moe_w_up"][0], A["moe_w_down"][0]
            entries, body, _ = PLAN["moe1"]
            with sp.Fori(0, G1) as i:
                for c, (s, free, _) in enumerate(entries):
                    sp.wait_ge(used, i * body + free)
                    e = i * body + c
                    chunk(s, *(w[bass.ds(e, 1)].rearrange("a k n -> (a k) n") for w in (g1, u1, d1)))

            for name, n, _ in STAGES[loop1 + 1:-1]:
                for j in range(done.get(name, 0), done.get(name, 0) + n):
                    straight(name, j)
                done[name] = done.get(name, 0) + n
            g2, u2, d2 = A["w_exp_gate_2"][0], A["w_exp_up_2"][0], A["w_exp_down_2"][0]
            entries, body, _ = PLAN["moe2"]
            with sp.Fori(0, E2) as e:
                for c, (s, free, _) in enumerate(entries):
                    sp.wait_ge(used, e * body + free)
                    h = slice(c * CH, (c + 1) * CH)
                    chunk(s, g2[bass.ds(e, 1), :, h].rearrange("a k n -> (a k) n"),
                          u2[bass.ds(e, 1), :, h].rearrange("a k n -> (a k) n"),
                          d2[bass.ds(e, 1), h, :].rearrange("a k n -> (a k) n"))
            for b in range(NT):
                sp.wait_ge(sem("y_final"), b + 1)
                sp.dma_start(out[0, b * P:(b + 1) * P, :], xn2[:, b, :]).then_inc(sem("stored"), 16)
            sp.wait_ge(sem("stored"), 16 * NT)

        def vectors_in(eng, vectors, done_sem):
            for name, src, r0, n in vectors:
                a = A[src]
                flat = a.rearrange(" ".join("abcd"[:a.ndim]) + " -> (" + " ".join("abcd"[:a.ndim]) + ")") if a.ndim > 1 else a
                v = flat[r0 * P:(r0 + n) * P].rearrange("(r p) -> r p", p=P)
                at, done = COL[name], 0
                while done < n:
                    b, p = divmod(at + done, P)
                    m = min(n - done, P - p)
                    eng.dma_start(vrows[p:p + m, b, :], v[done:done + m, :]).then_inc(done_sem, 16)
                    done += m

        @block.gpsimd
        def _(pool):
            pool.dma_start(blob[:, :], blob_in).then_inc(sem("consts_in"), 16)
            vectors_in(pool, COLS[0::2], sem("cols_in"))
            pool.dma_start(fw1[:, :], A["hy_f_w1"][0]).then_inc(sem("filter_in"), 16)
            pool.dma_start(fw2[:, :], A["hy_f_w2"][0]).then_inc(sem("filter_in"), 16)
            pool.dma_start(region(R_W3, 2048)[0:64, :], A["hy_f_w3"][0]).then_inc(sem("filter_in"), 16)
            for i, name in enumerate(("hy_f_b1", "hy_f_b2", "hy_f_freq")):
                pool.dma_start(fcol[:, i:i + 1], A[name][0].rearrange("(p a) -> p a", a=1), allow_slow_non_contiguous=True).then_inc(sem("filter_in"), 16)
            pool.dma_start(region(R_DEC, 2048), A["hy_decay"][0].rearrange("o d c -> (o d c)").partition_broadcast(P)
                           ).then_inc(sem("decay_in"), 16)
            pool.dma_start(hT[:, :, :].rearrange("p k n -> p (k n)").rearrange("p (b d) -> p b d", b=NT),
                           A["ctx"][0].rearrange("(b p) d -> p b d", p=P)).then_inc(sem("ctx_in"), 16)
            pool.dma_start(x[:, :, :], A["x"][0].rearrange("(b p) d -> p b d", p=P)).then_inc(sem("x_in"), 16)
            pool.dma_start(rowv[:, :], A["b_in"][0, ML0 + 2 * DBR:MLG0].partition_broadcast(P)).then_inc(sem("rows_in"), 16)
            pool.dma_start(mlnw[:, :], A["ml_norm_w"][0].partition_broadcast(P)).then_inc(sem("rows_in"), 16)
            pool.dma_start(gb[:, :], A["b_in"][0, MLG0:GATE0].rearrange("(g h) -> h g", h=NH), allow_slow_non_contiguous=True).then_inc(sem("rows_in"), 16)
            pool.dma_start(wmlg[:, :, :], A["w_in"][0, :, MLG0:GATE0].rearrange("(k p) n -> p k n", p=P)).then_inc(sem("rows_in"), 16)
            pool.dma_start(rb1[:, 0:4], A["moe_rg_b"][0].partition_broadcast(P)).then_inc(sem("rows_in"), 16)
            pool.dma_start(rb1[:, 4:20], A["moe_re_b"][0].partition_broadcast(P)).then_inc(sem("rows_in"), 16)
            pool.dma_start(rw1[:, :, 0:4], A["moe_rg_w"][0].rearrange("(k p) n -> p k n", p=P)).then_inc(sem("rows_in"), 16)
            pool.dma_start(rw1[:, :, 4:20], A["moe_re_w"][0].rearrange("(k p) n -> p k n", p=P)).then_inc(sem("rows_in"), 16)
            pool.dma_start(rw2[:, :, :], A["w_router_2"][0].rearrange("(k p) n -> p k n", p=P)).then_inc(sem("rows_in"), 16)
            pool.dma_start(subln[:, :, :].rearrange("p a b -> p (a b)"),
                           A["diff_subln_2"].rearrange("a b -> (a b)").partition_broadcast(P)).then_inc(sem("rows_in"), 16)
            pool.dma_start(lamr[:, :, :, :].rearrange("p a b c -> p (a b c)"),
                           A["diff_lambda_2"].rearrange("a b c -> (a b c)").partition_broadcast(P)).then_inc(sem("rows_in"), 16)
            pool.dma_start(posi[:, :], A["positions_2"][0].rearrange("(b p) -> p b", p=P), allow_slow_non_contiguous=True).then_inc(sem("rows_in"), 16)
            pool.wait_ge(sem("ml_gates"), 1)
            pool.dma_start(late[:, 0:D], A["norm_f_w"].partition_broadcast(P)).then_inc(sem("late_in"), 16)
            pool.dma_start(late[:, D:2 * D], A["g_final_2"].partition_broadcast(P)).then_inc(sem("late_in"), 16)


        @block.tensor
        def _(pe):
            mm = nc.tensor.matmul

            def unit(entry):
                s, _, n = entry
                pe.wait_ge(full[s], DMA3 * n)
                return s

            def w512(s, k, a=0, n=512, width=512):
                return ring[:, s, k * width + a:k * width + a + n]

            def ada(a, u, bank):
                pe.wait_ge(sem("ada_sum"), NA * a + u + 1)
                s = PLAN[f"ada{a}"][0][u][0]
                for i in range(2 if a == 0 and u < 4 else 1):
                    for m in range(4):
                        o = 64 * i + 4 * u + m
                        last = mm(ps[:, bank, o:o + 1], ring[:, s, 4096 + i * 512 + m * P:4096 + i * 512 + (m + 1) * P],
                                  const("ones")[:, 0:1], start=True, stop=True)
                last.then_inc(used, 1)

            def gate_rows(a):
                pe.wait_ge(sem("diag"), a + 1)
                for g in range(16):
                    last = mm(ps[:, 4 + g // 4, (g % 4) * P:(g % 4 + 1) * P], const("ones"), xn[:, g * P:(g + 1) * P],
                              start=True, stop=True)
                last.then_inc(sem("gaterow_mm"), 1)

            pe.wait_ge(sem("consts_in"), 16)
            pe.wait_ge(sem("cols_in"), 16 * N_COLS_IN[0])
            pe.wait_ge(sem("more_cols_in"), 16 * N_COLS_IN[1])
            total = sum(k for *_, k in COLS)
            for b in range(NCOLB):
                n = min(P, total - b * P)
                last = nc.tensor.transpose(ps[:, 0, b * P:b * P + n], vrows[0:n, b, :], ident[0:n, 0:n])
            last.then_inc(sem("cols_t"), 1)

            pe.wait_ge(sem("filter_in"), 96)
            mm(ps[0:64, 1, 0:T], fw1[:, :], const("feats", 33), start=True, stop=True).then_inc(sem("filter_mm"), 1)
            pe.wait_ge(sem("filter_h"), 1)
            mm(ps[0:64, 2, 0:T], fw2[:, :], region(R_SQ + 512, T)[0:64, :], start=True, stop=True).then_inc(sem("filter_mm"), 1)
            pe.wait_ge(sem("filter_h"), 2)
            h2 = region(R_SQ + 768, T)
            for b in range(NT):
                ada(0, b, 3)
                if b:
                    pe.wait_ge(sem("filter_h3"), b)
                for n in range(4):
                    last = mm(ps[:, 4 + n, :], h2[0:64, b * P:(b + 1) * P], region(R_W3, 2048)[0:64, n * 512:(n + 1) * 512],
                              start=True, stop=True)
                last.then_inc(sem("filter_mm"), 1)
            ada(0, 2, 3)
            pe.wait_ge(sem("filter_sq"), 1)
            sq = region(R_SQ, NT, 2, 2, DBR)
            for o in range(2):
                for c in range(NBR):
                    for i, (d, b) in enumerate((d, b) for d in range(2) for b in range(NT)):
                        last = mm(ps[:, 1, o * NBR + c:o * NBR + c + 1], sq[:, b, o, d, c * P:(c + 1) * P], const("ones")[:, 0:1],
                                  start=i == 0, stop=i == 3)
            last.then_inc(sem("filter_ssum"), 1)
            ada(0, 3, 3)
            pe.wait_ge(sem("mod_in"), 1)
            pe.wait_ge(sem("filter_pq"), 1)
            pe.wait_ge(sem("kn_in"), 1)
            pq = region(R_PQ, NT, 2, 2, DBR)
            for o in range(2):
                for ri, table in enumerate(("cs", "ss")):
                    for m in range(NT):
                        for b in range(NT):
                            last = mm(ps[:, 4 * o + 2 * ri + m, :], const2(table)[:, b, m * P:(m + 1) * P], pq[:, b, o, ri, :],
                                      start=b == 0, stop=b == NT - 1)
            last.then_inc(sem("spectra_mm"), 1)

            pe.wait_ge(sem("spectra_in"), 2)

            def turn(name):
                i = TRS.index(name)
                for b in range(NT):
                    pe.wait_ge(sem("normed"), NT * i + b + 1)
                    for k in range(KD):
                        last = nc.tensor.transpose(ps[:, 4 + k // 2, (k % 2) * T + b * P:(k % 2) * T + (b + 1) * P],
                                                   xn2[:, b, k * P:(k + 1) * P], ident)
                last.then_inc(sem("turned"), 1)

            def columns_by(s, src, bank, second=None):
                for m in range(4):
                    if m == 2 and second:
                        pe.wait_ge(*second)
                    for k in range(KD):
                        last = mm(ps[:, bank + m // 2, (m % 2) * T:(m % 2 + 1) * T], w512(s, k, m * P, P), src[:, k, :],
                                  start=k == 0, stop=k == KD - 1)
                return last

            def rows_by(s, src, bank, n=512, second=None):
                for b in range(NT):
                    if b and second:
                        pe.wait_ge(*second)
                    for k in range(KD):
                        last = mm(ps[:, bank + b, 0:n], src[:, k, b * P:(b + 1) * P], w512(s, k, 0, n, n),
                                  start=k == 0, stop=k == KD - 1)
                return last

            turn("ctx")
            pe.wait_ge(sem("hT_ready"), 2)
            turn("x1")
            pe.wait_ge(sem("hT_ready"), 4)

            entries = PLAN["in1"][0]
            for g in range(4):
                ada(0, 4 + g, 2 * g + 1)
                s = unit(entries[g])
                columns_by(s, hT, 2 * g, (sem("mod_in"), 2 + g)).then_inc(used, 1)
            s = unit(entries[4])
            pe.wait_ge(sem("z_in"), 1)
            columns_by(s, hT, 0).then_inc(sem("k_mm"), 1)
            pe.wait_ge(sem("z_in"), 2)
            columns_by(s, hTc, 2).then_inc(used, 1)
            pe.wait_ge(sem("z_in"), 3)
            ada(0, 8, 5)
            s = unit(entries[5])
            columns_by(s, hT, 4, (sem("mod_in"), 6)).then_inc(used, 1)
            s = unit(entries[6])
            pe.wait_ge(sem("z_in"), 4)
            rows_by(s, hT, 6).then_inc(sem("vo_mm"), 1)
            pe.wait_ge(sem("z_in"), 5)
            rows_by(s, hTc, 0).then_inc(used, 1)
            pe.wait_ge(sem("z_in"), 6)
            ada(0, 9, 3)
            s = unit(entries[7])
            rows_by(s, hT, 2, second=(sem("mod_in"), 7)).then_inc(used, 1)
            pe.wait_ge(sem("rows_in"), 16 * N_ROWS_IN)
            pe.wait_ge(sem("z_in"), 7)
            pe.wait_ge(sem("vo_in"), 1)
            for i, src in enumerate((hTc, hT)):
                for k in range(KD):
                    last = mm(ps[0:16, 4, i * T:(i + 1) * T], wmlg[:, k, :], src[:, k, :], start=k == 0, stop=k == KD - 1)
            last.then_inc(sem("gate_rows_mm"), 1)
            pe.wait_ge(sem("gate_rows_out"), 1)
            for g in range(4):
                last = mm(ps[0:NH, 4 + g, :], ident[0:16, g * NH:(g + 1) * NH], gate_in, start=True, stop=True)
            last.then_inc(sem("gates_mm"), 1)

            pe.wait_ge(sem("vo_in"), 3)
            for b in range(NT):
                for g in range(4):
                    last = mm(ps[:, 2 * b + g // 2, (g % 2) * T:(g % 2 + 1) * T], z[:, ZFN + g, b * P:(b + 1) * P], const("ccsc"),
                              start=True, stop=True)
            last.then_inc(sem("fnet_mm"), 1)
            pe.wait_ge(sem("fnet_in"), 1)
            pe.wait_ge(sem("vo_in"), 4)
            ab = xn[:, :].rearrange("p (b g n) -> p b g n", b=NT, g=4)
            for g in range(4):
                for i, (b, table) in enumerate((b, t) for b in range(NT) for t in range(2)):
                    last = mm(ps[:, 4 + g // 2, (g % 2) * T:(g % 2 + 1) * T], ab[:, b, g, table * P:(table + 1) * P],
                              const2(("cl", "sl")[table])[:, b, :], start=i == 0, stop=i == 3)
            last.then_inc(sem("fnet_mm"), 1)

            for o in range(2):
                pe.wait_ge(sem("hy_u"), o + 1)
                for b in range(NT):
                    for c in range(NBR):
                        last = nc.tensor.transpose(ps[:, b, c * P:(c + 1) * P], z[:, c, b * P:(b + 1) * P], ident)
                last.then_inc(sem("hy_t"), 1)
                pe.wait_ge(sem("hy_rows"), o + 1)
                for ri, table in enumerate(("cs", "ss")):
                    for m in range(NT):
                        for b in range(NT):
                            last = mm(ps[:, 2 * ri + m, :], const2(table)[:, b, m * P:(m + 1) * P], vt[:, b, :],
                                      start=b == 0, stop=b == NT - 1)
                last.then_inc(sem("hy_spec"), 1)
                if o == 0:
                    pe.wait_ge(sem("fnet_in"), 2)
                    ada(0, NA - 2, 4)
                    ada(0, NA - 1, 4)
                    pe.wait_ge(sem("mod_in"), 8)
                else:
                    ada(1, 1, 4)
                pe.wait_ge(sem("hy_y"), o + 1)
                yy = xn[:, :].rearrange("p (r m n) -> p r m n", r=2, m=NT)
                for c in range(NBR):
                    for i, (r, m) in enumerate((r, m) for r in range(2) for m in range(NT)):
                        last = mm(ps[:, 6 + c // 2, (c % 2) * T:(c % 2 + 1) * T], yy[:, r, m, c * P:(c + 1) * P],
                                  const2(("ict", "ist")[r])[:, m, :], start=i == 0, stop=i == 3)
                last.then_inc(sem("hy_inv"), 1)
                ada(1, 2 * o, 4)

            gi, gf, _, gm = (region(R_KF + i * 1024, 2, 512) for i in range(4))
            pe.wait_ge(sem("ml_gates"), 1)
            pe.wait_ge(sem("mod_in"), 9)
            for d in range(2):
                for sbk in range(4):
                    nc.tensor.transpose(ps[:, 0, (d * 4 + sbk) * 4:(d * 4 + sbk) * 4 + 4], gi[0:NH, d, sbk * P:(sbk + 1) * P], ident[0:NH, 0:NH])
                for b in range(NT):
                    o = 32 + (d * 2 + b) * 4
                    nc.tensor.transpose(ps[:, 1, o:o + 4], gf[0:NH, d, T + b * P:T + (b + 1) * P], ident[0:NH, 0:NH])
                for h in range(NH):
                    last = mm(ps[:, 2 + 2 * d + h // 2, (h % 2) * T:(h % 2 + 1) * T], const("negsel", NH)[:, h * P:(h + 1) * P],
                              gm[0:NH, d, T:2 * T], start=True, stop=True)
            last.then_inc(sem("ml_cols_mm"), 1)
            pe.wait_ge(sem("ml_qk"), 1)
            pe.wait_ge(sem("ml_cols"), 2)
            for h in range(NH):
                if h:
                    pe.wait_ge(sem("ml_p"), 2 * h)
                for sbk in range(4):
                    k_ = kc[:, h, sbk * P:(sbk + 1) * P] if sbk < 2 else z[:, ZK + h, (sbk - 2) * P:(sbk - 1) * P]
                    last = mm(ps[:, 6 + sbk // 2, (sbk % 2) * T:(sbk % 2 + 1) * T], k_, z[:, ZQ + h, :], start=True, stop=True)
                last.then_inc(sem("ml_s"), 1)
                for d in range(2):
                    j = 2 * h + d
                    pe.wait_ge(sem("ml_p"), j + 1)
                    if j >= 2:
                        pe.wait_ge(sem("ml_h"), j - 1)
                    w = xn[:, (j % 2) * 1024:(j % 2 + 1) * 1024].rearrange("p (s n) -> p s n", s=4)
                    for b in range(NT):
                        for sbk in range(4):
                            last = mm(ps[:, j % 2, b * T:b * T + P + 1], w[:, sbk, b * P:(b + 1) * P], v1[:, sbk, h, :],
                                      start=sbk == 0, stop=sbk == 3)
                    last.then_inc(sem("ml_pv"), 1)
            pe.wait_ge(sem("ml_y"), 1)
            for c in range(NH):
                for b in range(NT):
                    last = nc.tensor.transpose(ps[:, 2 + c // 2, (c % 2) * T + b * P:(c % 2) * T + (b + 1) * P],
                                               vt[:, b, c * P:(c + 1) * P], ident)
            last.then_inc(sem("ml_t"), 1)
            gate_rows(0)

            pe.wait_ge(sem("ml_yT"), 1)
            pe.wait_ge(sem("fnet_in"), 2)
            for j, entry in enumerate(PLAN["merge"][0]):
                k, base = j // 2, 4 * (j % 2)
                if j >= 2:
                    pe.wait_ge(sem("merged"), j - 1)
                if j == 1:
                    pe.wait_ge(sem("gaterow_in"), 1)
                ada(1, 3 + j, base + 3)
                s = unit(entry)
                columns_by(s, hT, base).then_inc(sem("mg_mm"), 1)
                pe.wait_ge(sem("mod_in"), 10 + j)
                y0 = (0, ZFN, ZQ)[k]
                for m in range(4):
                    for c in range(NBR):
                        last = mm(ps[:, base + 2 + m // 2, (m % 2) * T:(m % 2 + 1) * T],
                                  ring[:, s, 4096 + c * 512 + m * P:4096 + c * 512 + (m + 1) * P], z[:, y0 + c, :],
                                  start=c == 0, stop=c == NBR - 1)
                last.then_inc(used, 1)

            def out_proj(name, src):
                for half, entry in enumerate(PLAN[name][0]):
                    if name == "out1":
                        ada(1, 9 + half, 4 + half)
                    s = unit(entry)
                    rows_by(s, src, 2 * half).then_inc(used, 1)

            def chunk_mm(s, n, first, last_, read, src=hT, cols=T, base=4):
                for hb in range(2):
                    pe.wait_ge(sem("act_ready"), n - 1 + hb)
                    for i in range(2):
                        for k in range(KD):
                            o = i * 2048 + k * CH + hb * P
                            m_ = mm(ps[:, hb, i * cols:(i + 1) * cols], ring[:, s, o:o + P], src[:, k, :],
                                    start=k == 0, stop=k == KD - 1)
                    m_.then_inc(sem("gu_mm"), 1)
                if first:
                    pe.wait_ge(*read)
                for hb in range(2):
                    pe.wait_ge(sem("act_ready"), n + 1 + hb)
                    for b in range(cols // P):
                        for half in range(2):
                            o = 4096 + hb * 1024 + half * 512
                            m_ = mm(ps[:, base + 2 * b + half, :], region(R_AT, 2, T)[:, hb, b * P:(b + 1) * P],
                                    ring[:, s, o:o + 512], start=first and hb == 0, stop=last_ and hb == 1)
                m_.then_inc(used, 1)

            def moe_mm(name, i, jobs, experts, chunks, hidden):
                entries, body, per_slot = PLAN[name]
                sel, selT, ye, he = region(R_SE, NT, P), region(R_ST, T), region(R_YE, D), region(R_HE, KD, P)
                y, ready, he_in, selt_in = (sem(f"{name}_{w}") for w in ("ye", "sel", "he", "selT"))

                pe.wait_ge(sem("masks"), i + 1)
                for b in range(NT):
                    for s_ in range(b + 1):
                        last = mm(ps[:, 3, 128 + b * 16:128 + b * 16 + jobs], const2("upto")[:, s_, b * P:(b + 1) * P],
                                  msk[:, s_, 0:jobs], start=s_ == 0, stop=s_ == b)
                last.then_inc(sem("counted"), 1)
                pe.wait_ge(sem("flag"), i + 1)
                over = pe.value_load(flags[P - 1:P, i:i + 1], min_val=0, max_val=1)

                def gather(j):
                    pe.wait_ge(ready, j + 1)
                    for k in range(KD):
                        for b in range(NT):
                            mm(ps[:, 4 + k // 4, (k % 4) * P:(k % 4 + 1) * P], xn2[:, b, k * P:(k + 1) * P], sel[:, b, :],
                               start=b == 0, stop=b == NT - 1)
                    for b in range(NT):
                        last = mm(ps[:, 6, 0:experts], sel[:, b, :], comb[:, b, bass.ds(j * experts, experts)],
                                  start=b == 0, stop=b == NT - 1)
                    last.then_inc(sem(f"{name}_gathered"), 1)

                def spread(j):
                    pe.wait_ge(y, j * experts + 1)
                    pe.wait_ge(selt_in, j + 1)
                    pe.wait_ge(sem(f"{name}_weights"), j + 1)
                    for b in range(NT):
                        for half in range(2):
                            last = mm(ps[:, 4 + 2 * b + half, :], selT[:, b * P:(b + 1) * P], ye[:, half * 512:(half + 1) * 512],
                                      start=True, stop=True)
                    last.then_inc(sem(f"{name}_spread"), 1)

                with pe.If(over > 0):
                    with pe.Fori(0, jobs) as j:
                        for c, (s, _, f) in enumerate(entries):
                            pe.wait_ge(full[s], j * (DMA3 * per_slot[s]) + DMA3 * f)
                            chunk_mm(s, j * (2 * body) + hidden + 2 * c + 2, c % chunks == 0, c % chunks == chunks - 1,
                                     (sem(f"{name}_y_read"), j * experts + c // chunks + 1))
                with pe.Else():
                    gather(0)
                    with pe.Fori(0, jobs) as j:
                        pe.wait_ge(he_in, j + 1)
                        for c, (s, _, f) in enumerate(entries):
                            pe.wait_ge(full[s], j * (DMA3 * per_slot[s]) + DMA3 * f)
                            chunk_mm(s, j * (2 * body) + hidden + 2 * c + 2, c % chunks == 0, c % chunks == chunks - 1,
                                     (y, j * experts + c // chunks + 1), he, P, 2)
                            if c == 0:
                                spread(j)
                            elif c == 1:
                                pe.wait_ge(sem(f"{name}_added"), j + 1)
                                for b in range(NT):
                                    last = nc.tensor.transpose(ps[:, 7, b * P:(b + 1) * P], sel[:, b, :], ident)
                                last.then_inc(sem(f"{name}_placed"), 1)
                            elif c == 2:
                                gather(j + 1)
                    spread(jobs)
                pe.drain()

            def router(rw, n, i):
                for b in range(NT):
                    for k in range(KD):
                        last = mm(ps[:, 3, b * 32:b * 32 + n], hT[:, k, b * P:(b + 1) * P], rw[:, k, :],
                                  start=k == 0, stop=k == KD - 1)
                last.then_inc(sem("router_mm"), 1)

            pe.wait_ge(sem("merged"), 6)
            out_proj("out1", macc)
            ada(1, NA - 1, 4)
            turn("x2")
            pe.wait_ge(sem("hT_ready"), 6)
            router(rw1, 20, 0)
            moe_mm("moe1", 0, G1, 4, 1, 0)
            hidden = 2 * E1

            for l in range(2):
                pe.wait_ge(sem("block_done"), l + 1)
                turn(f"a{l}")
                pe.wait_ge(sem("hT_ready"), 8 + 4 * l)
                for j, ((c, w), entry) in enumerate(zip(IN2_COLS, PLAN[f"in2_{l}"][0])):
                    s = unit(entry)
                    if j == 2:
                        pe.wait_ge(sem("gaterow_in"), l + 2)
                    if j >= 4:
                        pe.wait_ge(sem("pj_in"), 6 * l + j - 3)
                    rows_by(s, hT, 2 * (j % 4), w).then_inc(used, 1)
                    if j == 0:
                        gate_rows(l + 1)
                pj = region(R_PJ, NT, D_IN)
                fm = region(R_FM, NFM, T)
                pe.wait_ge(sem("roped"), l + 1)
                n_t = -(-NFM // 4)
                for q in range(n_t):
                    if q >= 2:
                        pe.wait_ge(sem("fm_in"), n_t * l + q - 1)
                    for i in range(4 * q, min(NFM, 4 * q + 4)):
                        for b in range(NT):
                            last = nc.tensor.transpose(
                                ps[:, 2 * (q % 2) + (i % 4) // 2, (i % 2) * T + b * P:(i % 2) * T + (b + 1) * P],
                                pj[:, b, FM_COLS[i]:FM_COLS[i] + P], ident)
                    last.then_inc(sem("fm_mm"), 1)
                pe.wait_ge(sem("fm_in"), n_t * (l + 1))
                for qb in range(NT):
                    ns = (qb + 1) * P
                    for h in range(4):
                        p0 = 64 * (h % 2)
                        last = mm(ps[:, 4 + 2 * qb + h % 2, (h // 2) * T:(h // 2) * T + ns],
                                  fm[p0:p0 + 64, FM_QI + h // 2, qb * P:(qb + 1) * P], fm[p0:p0 + 64, FM_KI[h % 2], 0:ns],
                                  start=True, stop=True)
                    last.then_inc(sem("ix_mm"), 1)

                sm = region(R_SM, 2, 4, T)
                pt = region(R_PT, 4, NT, P)

                def scores(j):
                    br, h0, n, qb = JOBS[j]
                    ns = (qb + 1) * P
                    if j >= 2:
                        pe.wait_ge(sem("masked"), len(JOBS) * l + j - 1)
                    if j == 0:
                        pe.wait_ge(sem("qb_masked"), l + 1)
                    for k in range(n):
                        if br == "B":
                            i, tile = k, k
                            q_, k_ = hT[:, h0 + i, :], fm[:, FM_KB + h0 // 4, :]
                        else:
                            i, tile = PAIRS[n][k], TILE[n] * k
                            h = h0 + i
                            rows = slice(64 * (h % 2), 64 * (h % 2) + 64)
                            q_ = fm[rows, (FM_QA if br == "A" else FM_QC) + h // 2, :]
                            k_ = fm[rows, FM_KA[h % 2] if br == "A" else FM_KC + h // 2, :]
                        last = mm(ps[:, 2 * (j % 2) + tile // 2, (tile % 2) * T:(tile % 2) * T + ns],
                                  q_[:, qb * P:(qb + 1) * P], k_[:, 0:ns], start=True, stop=True)
                    last.then_inc(sem("s_mm"), 1)

                scores(0)
                scores(1)
                for j, (br, h0, n, qb) in enumerate(JOBS):
                    if j + 2 < len(JOBS):
                        scores(j + 2)
                    done = len(JOBS) * l + j
                    heads = n // 2 if br == "B" else n
                    pe.wait_ge(sem("probs"), done + 1)
                    if j == 0:
                        pe.wait_ge(sem("ix_in"), 2 * (l + 1))
                    for i in range(heads):
                        for sbk in range(qb + 1):
                            src = sm[:, j % 2, 2 * i if br == "B" else i, sbk * P:(sbk + 1) * P]
                            o = (i * 2 + sbk) * P
                            last = nc.tensor.transpose(ps[:, 4 + o // 512, o % 512:o % 512 + P], src, ident)
                    last.then_inc(sem("pt_mm"), 1)
                    pe.wait_ge(sem("pt_in"), done + 1)
                    if j >= 2:
                        pe.wait_ge(sem("o_in"), done - 1)
                    for i in range(heads):
                        v_ = {"A": O_VA, "B": O_VB + (h0 // 2 + i) * HD, "C": O_VC + (h0 + PAIRS[n][i]) * HD}[br]
                        for sbk in range(qb + 1):
                            last = mm(ps[:, 6 + j % 2, i * HD:(i + 1) * HD], pt[:, i, sbk, :], pj[:, sbk, v_:v_ + HD],
                                      start=sbk == 0, stop=sbk == qb)
                    last.then_inc(sem("o_mm"), 1)
                pe.wait_ge(sem("y_rows"), l + 1)
                for k in range(KD):
                    for b in range(NT):
                        last = nc.tensor.transpose(ps[:, 4 + k // 2, (k % 2) * T + b * P:(k % 2) * T + (b + 1) * P],
                                                   xn2[:, b, k * P:(k + 1) * P], ident)
                last.then_inc(sem("y_t"), 1)
                pe.wait_ge(sem("yT"), l + 1)
                out_proj(f"out2_{l}", hT)
                turn(f"f{l}")
                pe.wait_ge(sem("hT_ready"), 10 + 4 * l)
                if l == 0:
                    for c, entry in enumerate(PLAN["ff"][0]):
                        ada(2, c, 2)
                        s = unit(entry)
                        chunk_mm(s, hidden + 2 * c + 2, c == 0, c == NCH - 1, (sem("hT_ready"), 10))
                    ada(2, NA - 1, 2)
                    hidden += 2 * NCH
            router(rw2, E2, 1)
            moe_mm("moe2", 1, E2, 1, NCH, hidden)

        @block.scalar
        def _(act):
            ac = nc.scalar.activation

            def sqrt_of(i, width, src, dst):
                act.wait_ge(sem("ms"), i)
                ac(dst, src, ACT.Sqrt).then_inc(sem("std"), 1)

            vectors_in(act, COLS[1::2], sem("more_cols_in"))

            def turned(n, dst, gain, shift):
                act.wait_ge(sem("turned"), n)
                for k in range(KD // 2, KD):
                    last = ac(dst[:, k, :], ps[:, 4 + k // 2, (k % 2) * T:(k % 2 + 1) * T], ACT.Identity,
                              bias=shift[:, k:k + 1], scale=gain[:, k:k + 1])
                last.then_inc(sem("hT_ready"), 1)

            act.wait_ge(sem("cols"), 1)
            ac(cact[:, :], col("c", 0, 24), ACT.Silu).then_inc(sem("c_act"), 1)
            for i in range(2):
                act.wait_ge(sem("filter_a"), i + 1)
                ac(region(R_SQ + 512 + 256 * i, T)[0:64, :], region(R_SQ, T)[0:64, :], ACT.Sin).then_inc(sem("filter_h"), 1)
            act.wait_ge(sem("decay_in"), 16)
            ac(region(R_DEC, 2048), region(R_DEC, 2048), ACT.Abs)
            act.drain()
            for b in range(NT):
                if b:
                    act.wait_ge(sem("filter_h3"), b)
                ac(region(R_EXP, 2048), region(R_DEC, 2048), ACT.Exp, scale=const("tneg")[:, b:b + 1]).then_inc(sem("decay"), 1)
            act.wait_ge(sem("lam_in"), 1)
            ac(lamt[:, 0:4], lamt[:, 0:4], ACT.Exp).then_inc(sem("lam_exp"), 1)
            act.wait_ge(sem("ang_in"), 1)
            ac(sinn[:, :, :], ang[:, 2, :, :], ACT.Sin)
            ac(cosn[:, :, :], ang[:, 3, :, :], ACT.Sin).then_inc(sem("rope_in"), 1)
            act.wait_ge(sem("kn_in"), 1)
            ac(kn[:, :], kn[:, :], ACT.Sqrt).then_inc(sem("kn_sqrt"), 1)

            std = st[:, 2:4]
            sqrt_of(1, 2, st[:, 0:2], std)
            act.wait_ge(sem("spectra_mm"), 1)
            ac(region(R_KF + 2048, 2048), all_ps[:, 2048:4096], ACT.Copy).then_inc(sem("spectra_in"), 1)
            act.wait_ge(sem("gains"), 1)
            turned(1, hTc, gac, modc)
            sqrt_of(2, 2, st[:, 0:2], std)
            turned(2, hT, ga, mod)

            for g, (dst, b0, bank) in enumerate(((z[:, 0:4], 0, 0), (z[:, 4:8], 4, 2), (z[:, 8:12], 8, 4), (z[:, 12:16], 16, 6),
                                                 (z[:, 16:20], 20, 0), (kc, 20, 2), (z[:, 20:24], 12, 4))):
                if g == 4:
                    act.wait_ge(sem("k_mm"), 1)
                else:
                    act.wait_ge(used, USED["in1"][g if g < 4 else g - 1])
                for m in range(4):
                    last = ac(dst[:, m, :], ps[:, bank + m // 2, (m % 2) * T:(m % 2 + 1) * T], ACT.Identity, bias=col("bz", b0 + m))
                last.then_inc(sem("z_in"), 1)
            act.wait_ge(sem("vo_in"), 3)
            ac(og, og, ACT.Sigmoid).then_inc(sem("o_gate"), 1)

            act.wait_ge(sem("fnet_mm"), 1)
            ac(xn[:, :], all_ps[:, 0:2048], ACT.Copy).then_inc(sem("fnet_in"), 1)
            act.wait_ge(sem("fnet_mm"), 2)
            ac(z[:, ZFN:ZFN + 4, :], ps[:, 4:6, :].rearrange("p b (a n) -> p (b a) n", a=2), ACT.Copy).then_inc(sem("fnet_in"), 1)
            for o in range(2):
                act.wait_ge(sem("hy_t"), o + 1)
                ac(vt, ps[:, 0:2, :], ACT.Copy).then_inc(sem("hy_rows"), 1)
                if o == 0:
                    act.wait_ge(sem("conv_qk"), 1)
                    ac(z[:, ZQ:ZQ + 8, :], z[:, ZQ:ZQ + 8, :], ACT.Silu)
                    ac(kc, kc, ACT.Silu).then_inc(sem("ml_silu"), 1)

            _, gf, _, gm = (region(R_KF + i * 1024, 1024)[0:NH, :] for i in range(4))
            act.wait_ge(sem("ml_f"), 1)
            ac(gm, gf, ACT.Abs)
            act.drain()
            ac(gm, gm, ACT.Exp, scale=-1.0)
            act.drain()
            ac(gm, gm, ACT.Ln, bias=1.0).then_inc(sem("ml_softplus"), 1)
            act.wait_ge(sem("ml_cols_mm"), 1)
            ac(en[:, :], ps[:, 1, 32:48], ACT.Exp, scale=-1.0).then_inc(sem("ml_cols"), 1)
            for j in range(8):
                act.wait_ge(sem("ml_w"), j + 1)
                w = xn[:, (j % 2) * 1024:(j % 2 + 1) * 1024]
                ac(w, w, ACT.Exp).then_inc(sem("ml_exp"), 1)
            sqrt_of(3, 8, st[:, 0:8], st[:, 8:16])
            act.wait_ge(sem("ml_t"), 1)
            ac(z[:, ZQ:ZQ + 4, :], ps[:, 2:4, :].rearrange("p b (a n) -> p (b a) n", a=2), ACT.Copy).then_inc(sem("ml_yT"), 1)

            for j in range(6):
                k, half = divmod(j, 2)
                act.wait_ge(sem("mg_mm"), j + 1)
                if j >= 2:
                    act.wait_ge(sem("merged"), j - 1)
                for m in range(4):
                    last = ac(sgm[:, j % 2, m, :], ps[:, 4 * (j % 2) + m // 2, (m % 2) * T:(m % 2 + 1) * T], ACT.Sigmoid,
                              bias=col("bg", k * 8 + half * 4 + m))
                last.then_inc(sem("mg_sig"), 1)

            def chunk_silu(n, cols=T):
                for hb in range(2):
                    act.wait_ge(sem("gu_mm"), n - 1 + hb)
                    act.wait_ge(sem("act_ready"), n - 1 + hb)
                    ac(region(R_SG, 2, T)[:, hb, 0:cols], ps[:, hb, 0:cols], ACT.Silu).then_inc(sem("gate_silu"), 1)

            def moe_silu(i, units, hidden):
                act.wait_ge(sem("flag"), i + 1)
                over = act.value_load(flags[P - 1:P, i:i + 1], min_val=0, max_val=1)
                with act.If(over > 0):
                    with act.Fori(0, units) as c:
                        chunk_silu(c * 2 + hidden + 2)
                with act.Else():
                    with act.Fori(0, units) as c:
                        chunk_silu(c * 2 + hidden + 2, P)
                act.drain()

            sqrt_of(4, 2, st[:, 0:2], std)
            turned(3, hT, ga[:, 8:16], mod[:, 24:32])
            for b in range(NT):
                act.wait_ge(sem("rt_max"), b + 1)
                ac(rt[:, b, 24:28], rt[:, b, 0:4], ACT.Exp, bias=rt[:, b, 28:29], accum_out=rt[:, b, 29:30])
                ac(rt[:, b, 31:32], rt[:, b, 30:31], ACT.Exp).then_inc(sem("rt_exp"), 1)
            moe_silu(0, E1, 0)
            hidden = 2 * E1
            sqrt_of(5, 2, st[:, 0:2], std)

            for l in range(2):
                sqrt_of(6 + 3 * l, 2, st[:, 0:2], std)
                turned(4 + 2 * l, hT, ga, mod)
                for j, (c, w) in enumerate(IN2_COLS):
                    act.wait_ge(used, USED[f"in2_{l}"][j])
                    bank = 2 * (j % 4)
                    ac(region(R_PJ, NT, D_IN)[:, :, c:c + w], ps[:, bank:bank + 2, 0:w], ACT.Copy).then_inc(sem("pj_in"), 1)
                n_t = -(-NFM // 4)
                fm = region(R_FM, NFM, T)
                for q in range(n_t):
                    act.wait_ge(sem("fm_mm"), n_t * l + q + 1)
                    n = min(4, NFM - 4 * q)
                    src = ps[:, 2 * (q % 2):2 * (q % 2) + 2, :].rearrange("p b (a n) -> p (b a) n", a=2)
                    ac(fm[:, 4 * q:4 * q + n, :], src[:, 0:n, :], ACT.Copy).then_inc(sem("fm_in"), 1)
                for qb in range(NT):
                    act.wait_ge(sem("ix_mm"), NT * l + qb + 1)
                    if qb:
                        act.wait_ge(sem("ix_used"), NT * l + qb)
                    ns = (qb + 1) * P
                    src = ps[:, 4 + 2 * qb:6 + 2 * qb, :].rearrange("p b (a n) -> p (b a) n", a=2)
                    ac(region(R_SM, 4, T)[:, :, 0:ns], src[:, :, 0:ns], ACT.Relu).then_inc(sem("ix_in"), 1)
                sm = region(R_SM, 2, 4, T)
                pt = region(R_PT, 4 * NT * P)

                def exps(j):
                    _, _, n, qb = JOBS[j]
                    ns = (qb + 1) * P
                    act.wait_ge(sem("row_max"), len(JOBS) * l + j + 1)
                    for i in range(n):
                        last = ac(sm[:, j % 2, i, 0:ns], sm[:, j % 2, i, 0:ns], ACT.Exp, bias=amx[:, j % 2, i:i + 1],
                                  accum_out=asum[:, j % 2, i:i + 1])
                    last.then_inc(sem("exped"), 1)

                exps(0)
                for j, (br, h0, n, qb) in enumerate(JOBS):
                    if j + 1 < len(JOBS):
                        exps(j + 1)
                    heads = n // 2 if br == "B" else n
                    act.wait_ge(sem("pt_mm"), len(JOBS) * l + j + 1)
                    if qb:
                        ac(pt[:, 0:heads * 2 * P], all_ps[:, 2048:2048 + heads * 2 * P], ACT.Copy).then_inc(sem("pt_in"), 1)
                    else:
                        ac(pt[:, 0:heads * 2 * P].rearrange("p (h s n) -> p h s n", s=2, n=P)[:, :, 0, :],
                           all_ps[:, 2048:2048 + heads * 2 * P].rearrange("p (h s n) -> p h s n", s=2, n=P)[:, :, 0, :],
                           ACT.Copy).then_inc(sem("pt_in"), 1)
                sqrt_of(7 + 3 * l, 8, st[:, 0:8], st[:, 8:16])
                act.wait_ge(sem("y_t"), l + 1)
                ac(hT[:, :, :], ps[:, 4:8, :].rearrange("p b (a n) -> p (b a) n", a=2), ACT.Copy).then_inc(sem("yT"), 1)
                sqrt_of(8 + 3 * l, 2, st[:, 0:2], std)
                turned(5 + 2 * l, hT, ga[:, 8:16], mod[:, 24:32])
                if l == 0:
                    for c in range(NCH):
                        chunk_silu(hidden + 2 * c + 2)
                    hidden += 2 * NCH
            for b in range(NT):
                act.wait_ge(sem("rt_max"), NT + b + 1)
                ac(rt[:, b, 31:32], rt[:, b, 30:31], ACT.Exp).then_inc(sem("rt_exp"), 1)
            moe_silu(1, E2 * NCH, hidden)
            sqrt_of(12, 2, st[:, 0:2], std)

        @block.vector
        def _(dve):
            v = nc.vector
            fence = dve.drain

            def bc(ap, *shape):
                return ap.to_broadcast(list(shape))

            def reduce_angle(r, a, k):
                v.tensor_scalar(k, a, 1.0 / (2 * math.pi), ROUND, ALU.mult, ALU.add)
                fence()
                v.tensor_scalar(k, k, ROUND, None, ALU.subtract)
                fence()
                v.scalar_tensor_tensor(r, k, -TWO_PI[0], a, ALU.mult, ALU.add)
                fence()
                v.scalar_tensor_tensor(r, k, -TWO_PI[1], r, ALU.mult, ALU.add)
                fence()
                v.scalar_tensor_tensor(r, k, -TWO_PI[2], r, ALU.mult, ALU.add)
                fence()
                return v.tensor_scalar(r, r, PI, -PI, ALU.min, ALU.max)

            def ada_sum(a, u):
                s, _, n = PLAN[f"ada{a}"][0][u]
                dve.wait_ge(full[s], DMA3 * n)
                vectors = (0, 8) if a == 0 and u < 4 else (0,) if a == 0 else (16,)
                for k in range(KD):
                    if k:
                        fence()
                    for i, c in enumerate(vectors):
                        acc = ring[:, s, 4096 + i * 512:4096 + (i + 1) * 512]
                        w = ring[:, s, k * 512:(k + 1) * 512]
                        if k == 0:
                            last = v.tensor_scalar(acc, w, cact[:, c:c + 1], None, ALU.mult)
                        else:
                            last = v.scalar_tensor_tensor(acc, w, cact[:, c + k:c + k + 1], acc, ALU.mult, ALU.add)
                last.then_inc(sem("ada_sum"), 1)

            def mod_in(a, u0, u1, bank):
                dve.wait_ge(used, USED[f"ada{a}"][u1 - 1])
                if a == 0 and u0 == 0:
                    v.tensor_copy(modc[:, :], ps[:, bank, 64:80])
                v.tensor_copy(modn[:, 4 * u0:4 * u1], ps[:, bank, 4 * u0:4 * u1]).then_inc(sem("mod_in"), 1)

            v.memset(dn[:, :], 0.0).then_inc(sem("act_ready"), 2)
            v.memset(comb[:, :, :], 0.0)
            v.memset(slots[:, :, :], 0.0)
            dve.wait_ge(sem("cols_t"), 1)
            total = sum(k for *_, k in COLS)
            v.tensor_copy(colv[:, 0:total], ps[:, 0, 0:total]).then_inc(sem("cols"), 1)

            dve.wait_ge(sem("filter_in"), 96)
            a, k = (region(R_SQ + i * 256 + 1024, T)[0:64, :] for i in range(2))
            for i in range(2):
                dve.wait_ge(sem("filter_mm"), i + 1)
                v.tensor_scalar(a, ps[0:64, 1 + i, 0:T], fcol[:, i:i + 1], fcol[:, 2:3], ALU.add, ALU.mult)
                fence()
                reduce_angle(region(R_SQ, T)[0:64, :], a, k).then_inc(sem("filter_a"), 1)
            h3 = region(R_H3, NT, 2, 2, DBR)
            dve.wait_ge(sem("c_act"), 1)
            ada_sum(0, 0)
            for b in range(NT):
                ada_sum(0, 1 + b)
                dve.wait_ge(sem("filter_mm"), 3 + b)
                dve.wait_ge(sem("decay"), b + 1)
                v.tensor_tensor(region(R_H3, NT, 2048)[:, b, :], all_ps[:, 2048:4096], region(R_EXP, 2048), ALU.mult
                                ).then_inc(sem("filter_h3"), 1)
            fence()
            v.memset(h3[0:1, 0, :, 1, :], 0.0)
            dve.wait_ge(sem("rows_in"), 16 * N_ROWS_IN)
            for l in range(2):
                for i in range(2):
                    v.tensor_tensor_reduce(lamj, lamr[:, l, 2 * i, :], lamr[:, l, 2 * i + 1, :], 1.0, 0.0,
                                           ALU.mult, ALU.add, lamt[:, 2 * l + i:2 * l + i + 1])
                    fence()
            v.tensor_copy(posf[:, :], posi[:, :]).then_inc(sem("lam_in"), 1)
            fence()
            for b in range(NT):
                v.tensor_scalar(ang[:, 0, b, :], const("inv"), posf[:, b:b + 1], None, ALU.mult)
            fence()
            reduce_angle(ang[:, 2, :, :], ang[:, 0, :, :], ang[:, 1, :, :])
            fence()
            v.scalar_tensor_tensor(ang[:, 3, :, :], ang[:, 2, :, :], -1.0, ang[:, 2, :, :], ALU.mult, ALU.max)
            fence()
            v.tensor_scalar(ang[:, 3, :, :], ang[:, 3, :, :], -1.0, math.pi / 2, ALU.mult, ALU.add).then_inc(sem("ang_in"), 1)
            v.tensor_tensor(region(R_SQ, 4096), region(R_H3, 4096), region(R_H3, 4096), ALU.mult).then_inc(sem("filter_sq"), 1)
            pq = region(R_PQ, NT, 2, 2, DBR)
            for o in range(2):
                v.tensor_tensor(pq[:, :, o, 0, :], h3[:, :, o, 0, :], h3[:, :, o, 1, :], ALU.add)
                last = v.tensor_tensor(pq[:, :, o, 1, :], h3[:, :, o, 1, :], h3[:, :, o, 0, :], ALU.subtract)
            last.then_inc(sem("filter_pq"), 1)
            ada_sum(0, 3)
            dve.wait_ge(sem("filter_ssum"), 1)
            v.tensor_scalar(kn[:, :], ps[:, 1, 0:8], EPS, None, ALU.add).then_inc(sem("kn_in"), 1)
            dve.wait_ge(sem("kn_sqrt"), 1)
            v.reciprocal(kn[:, :], kn[:, :])
            dve.wait_ge(sem("lam_exp"), 1)
            for l in range(2):
                v.tensor_scalar(lamt[:, 4 + l:5 + l], lamt[:, 2 * l:2 * l + 1], lamt[:, 2 * l + 1:2 * l + 2], LAM_INIT[l],
                                ALU.subtract, ALU.add)
            mod_in(0, 0, 4, 3)
            ada_sum(0, 4)
            def rstd(i, src):
                for b in range(NT):
                    v.tensor_tensor_reduce(xn2[:, b, :], src[:, b, :], src[:, b, :], 1.0, 0.0, ALU.mult, ALU.add, st[:, b:b + 1])
                fence()
                v.tensor_scalar(st[:, 0:2], st[:, 0:2], 1.0 / D, EPS, ALU.mult, ALU.add).then_inc(sem("ms"), 1)
                dve.wait_ge(sem("std"), i)
                v.reciprocal(st[:, 4:6], st[:, 2:4])
                fence()

            def norm_rows(i, src):
                rstd(i, src)
                for b in range(NT):
                    v.tensor_scalar(xn2[:, b, :], src[:, b, :], st[:, 4 + b:5 + b], None, ALU.mult).then_inc(sem("normed"), 1)

            def norm(i, src, n, dst, gain, shift):
                norm_rows(i, src)
                norm_columns(n, dst, gain, shift)

            def norm_columns(n, dst, gain, shift):
                dve.wait_ge(sem("turned"), n)
                for k in range(KD // 2):
                    last = v.tensor_scalar(dst[:, k, :], ps[:, 4 + k // 2, (k % 2) * T:(k % 2 + 1) * T],
                                           gain[:, k:k + 1], shift[:, k:k + 1], ALU.mult, ALU.add)
                last.then_inc(sem("hT_ready"), 1)

            dve.wait_ge(sem("ctx_in"), 16)
            norm_rows(1, hT[:, :, :].rearrange("p k n -> p (k n)").rearrange("p (b d) -> p b d", b=NT))
            dve.wait_ge(sem("spectra_mm"), 1)
            v.tensor_copy(region(R_KF, 2048), all_ps[:, 0:2048]).then_inc(sem("spectra_in"), 1)
            v.memset(v1[:, :, :, P:P + 1], 1.0)

            def ada_first(a, gain):
                fence()
                v.tensor_tensor(mod[:, 0:16], modn[:, 0:16], col(f"ab{a}", 0, 16), ALU.add)
                fence()
                v.scalar_tensor_tensor(ga[:, 0:8], mod[:, 8:16], 1.0, col(gain, 0, 8), ALU.add, ALU.mult)
                fence()

            def ada_rest(a, gain):
                fence()
                v.tensor_tensor(mod[:, 16:48], modn[:, 16:48], col(f"ab{a}", 16, 32), ALU.add)
                fence()
                v.scalar_tensor_tensor(ga[:, 8:16], mod[:, 32:40], 1.0, col(gain, 0, 8), ALU.add, ALU.mult)
                fence()

            def gate_rows(a):
                for g in range(16):
                    c = 16 + g if g < 8 else 32 + g
                    last = v.tensor_scalar(xn[:, g * P:(g + 1) * P], ident, mod[:, c:c + 1], None, ALU.mult)
                last.then_inc(sem("diag"), 1)
                dve.wait_ge(sem("gaterow_mm"), a + 1)
                v.tensor_copy(grow[:, :, :].rearrange("p a n -> p (a n)"), all_ps[:, 2048:4096]).then_inc(sem("gaterow_in"), 1)
                fence()

            ada_first(0, "n1")
            v.tensor_tensor(modc[:, :], modc[:, :], col("ab0", 0, 16), ALU.add)
            fence()
            v.scalar_tensor_tensor(gac[:, :], modc[:, 8:16], 1.0, col("n1", 0, 8), ALU.add, ALU.mult).then_inc(sem("gains"), 1)
            fence()
            norm_columns(1, hTc, gac, modc)
            dve.wait_ge(sem("x_in"), 16)
            norm(2, x, 2, hT, ga, mod)
            def conv(blocks, j0, w, wcount, bias, acc):
                acc = acc.rearrange("p (a r c) -> p a r c", a=2, c=GW)
                grids = [z[:, bass.ds(b + j0, 1), :].rearrange("p a (r c) -> p (a r) c", c=GW) for b in blocks]

                def tap(b, t):
                    return colv[:, bass.ds(b + t * wcount + COL[w], 1)]

                for a, b in enumerate(blocks):
                    v.tensor_copy(acc[:, a], colv[:, bass.ds(b + COL[bias], 1)].unsqueeze(2).to_broadcast([P, GR, GW]))
                fence()
                for dr in (-1, 0, 1):
                    for dc in (-1, 0, 1):
                        if dr == dc == 0:
                            continue
                        ro, co = slice(max(0, -dr), GR - max(0, dr)), slice(max(0, -dc), GW - max(0, dc))
                        ri, ci = slice(max(0, dr), GR - max(0, -dr)), slice(max(0, dc), GW - max(0, -dc))
                        for a, b in enumerate(blocks):
                            v.scalar_tensor_tensor(acc[:, a, ro, co], grids[a][:, ri, ci], tap(b, (dr + 1) * 3 + dc + 1),
                                                     acc[:, a, ro, co], ALU.mult, ALU.add)
                        fence()
                for a, b in enumerate(blocks):
                    v.scalar_tensor_tensor(grids[a], grids[a], tap(b, 4), acc[:, a], ALU.mult, ALU.add)
                fence()

            for g in range(4):
                mod_in(0, 4 + g, 5 + g, 2 * g + 1)
                if g:
                    dve.wait_ge(sem("z_in"), (g + 1) // 2)
                    conv((2 * g - 2, 2 * g - 1), 0, "hcw", 12, "hcb", xn[:, 0:2 * T])
                ada_sum(0, 5 + g)
            dve.wait_ge(sem("z_in"), 3)
            with dve.Fori(3, 5) as i:
                conv((i * 2, i * 2 + 1), 0, "hcw", 12, "hcb", xn[:, 0:2 * T])
            mod_in(0, 8, 9, 5)
            ada_sum(0, 9)
            conv((10, 11), 0, "hcw", 12, "hcb", xn[:, 0:2 * T])
            v.memset(dn[:, 4:5], 0.0).then_inc(sem("hy_u"), 1)
            def v_in(sb0, bank):
                for b in range(NT):
                    last = v.tensor_tensor(v1[:, sb0 + b, :, 0:P], ps[:, bank + b, :].rearrange("p (h n) -> p h n", h=NH),
                                           rowv[:, 0:DBR].rearrange("p (h n) -> p h n", h=NH), ALU.add)
                last.then_inc(sem("vo_in"), 1)

            dve.wait_ge(sem("z_in"), 6)
            with dve.Fori(0, 2) as i:
                conv((i, i + 4), ZQ, "mcw", 8, "mcb", grow[:, 0, 0:2 * T])
            dve.wait_ge(sem("vo_mm"), 1)
            v_in(2, 6)
            mod_in(0, 9, 10, 3)
            conv((2, 6), ZQ, "mcw", 8, "mcb", grow[:, 0, 0:2 * T])
            dve.wait_ge(used, USED["in1"][6])
            v_in(0, 0)
            dve.wait_ge(used, USED["in1"][7])
            for b in range(NT):
                last = v.tensor_tensor(og[:, b, :], ps[:, 2 + b, :], rowv[:, DBR:2 * DBR], ALU.add)
            last.then_inc(sem("vo_in"), 1)

            dve.wait_ge(sem("gate_rows_mm"), 1)
            v.tensor_copy(gate_in, ps[0:16, 4, :]).then_inc(sem("gate_rows_out"), 1)
            conv((3, 7), ZQ, "mcw", 8, "mcb", grow[:, 0, 0:2 * T])
            dve.wait_ge(sem("gates_mm"), 1)
            for g in range(4):
                last = v.tensor_scalar(gates[:, g % 2, g // 2, :], ps[0:NH, 4 + g, :], gb[:, g:g + 1], None, ALU.add)
            last.then_inc(sem("vo_in"), 1)

            acc = grow[:, 0, :].rearrange("p (h n) -> p h n", h=NH)
            for h in range(NH):
                v.tensor_scalar(acc[:, h, :], kc[:, h, :], col("mcw", 4 * 8 + 4 + h), col("mcb", 4 + h), ALU.mult, ALU.add)
            fence()
            for tap, (o, i) in ((3, (slice(1, T), slice(0, T - 1))), (5, (slice(0, T - 1), slice(1, T)))):
                for h in range(NH):
                    v.scalar_tensor_tensor(acc[:, h, o], kc[:, h, i], col("mcw", tap * 8 + 4 + h), acc[:, h, o], ALU.mult, ALU.add)
                fence()
            v.tensor_copy(kc, acc).then_inc(sem("conv_qk"), 1)

            yy = xn[:, :].rearrange("p (r n) -> p r n", r=2)
            dve.wait_ge(sem("fnet_mm"), 2)
            flat_vt = region(R_VT, 1024)
            ada_sum(0, NA - 2)
            ada_sum(0, NA - 1)
            for o in range(2):
                if o:
                    ada_sum(1, 1)
                dve.wait_ge(sem("hy_spec"), o + 1)
                ur, us = all_ps[:, 0:1024], all_ps[:, 1024:2048]
                kr, ki = (kf[:, o, r, :] for r in range(2))
                if o == 0:
                    mod_in(0, NA - 2, NA, 4)
                v.tensor_tensor(yy[:, 0, :], ur, kr, ALU.mult)
                v.tensor_tensor(flat_vt, us, ki, ALU.mult)
                v.tensor_tensor(yy[:, 1, :], ur, ki, ALU.mult)
                fence()
                v.tensor_tensor(yy[:, 0, :], yy[:, 0, :], flat_vt, ALU.add)
                fence()
                v.tensor_tensor(flat_vt, us, kr, ALU.mult)
                fence()
                v.tensor_tensor(yy[:, 1, :], yy[:, 1, :], flat_vt, ALU.subtract).then_inc(sem("hy_y"), 1)
                fence()
                vt4 = region(R_VT, NBR, T)
                for c in range(NBR):
                    v.tensor_scalar(vt4[:, c, :], z[:, c, :], col("skip", o * NBR + c), None, ALU.mult)
                ada_sum(1, 2 * o)
                dve.wait_ge(sem("hy_inv"), o + 1)
                fence()
                for c in range(NBR):
                    v.scalar_tensor_tensor(vt4[:, c, :], ps[:, 6 + c // 2, (c % 2) * T:(c % 2 + 1) * T],
                                           kn[:, o * NBR + c:o * NBR + c + 1], vt4[:, c, :], ALU.mult, ALU.add)
                fence()
                v.tensor_tensor(z[:, 0:4, :], vt4, z[:, 4 * (o + 1):4 * (o + 2), :], ALU.mult).then_inc(sem("hy_u"), 1)

            ada_rest(0, "n2")
            mod_in(1, 0, 3, 4)
            fence()
            gi, gf, gB, gm = (region(R_KF + i * 1024, 2, 512)[0:NH] for i in range(4))
            v.tensor_copy(gf, gates[:, 1, :, :]).then_inc(sem("ml_f"), 1)
            v.tensor_copy(gi, gates[:, 0, :, :])
            fence()
            v.tensor_scalar(gates[:, 1, :, :], gf, 0.0, None, ALU.min)
            ada_sum(1, 3)
            dve.wait_ge(sem("ml_softplus"), 1)
            fence()
            v.tensor_tensor(gf, gates[:, 1, :, :], gm, ALU.subtract)
            fence()
            v.memset(gm, 0.0)
            fence()

            def scans(dst, src, op, second):
                v.tensor_tensor_scan(dst[:, 0, :], src[:, 0, :], second(src[:, 0, :]), 0.0, op, op)
                v.tensor_tensor_scan(dst[:, 1, 0:T][:, ::-1], src[:, 1, 0:T][:, ::-1], second(src[:, 1, 0:T][:, ::-1]), 0.0, op, op)
                fence()
                v.tensor_tensor_scan(dst[:, 1, T:2 * T][:, ::-1], src[:, 1, T:2 * T][:, ::-1],
                                     second(src[:, 1, T:2 * T][:, ::-1]), dst[:, 1, 0:1], op, op)
                fence()

            scans(gB, gf, ALU.add, lambda s: gm[:, 0, 0:s.shape[-1]])
            v.tensor_tensor(gi, gi, gB, ALU.subtract)
            fence()
            scans(gm, gi, ALU.max, lambda s: s)
            v.tensor_tensor(gf, gB, gm, ALU.add).then_inc(sem("ml_gates"), 1)

            dve.wait_ge(sem("ml_silu"), 1)
            v.tensor_scalar(z[:, ZQ:ZQ + 4, :], z[:, ZQ:ZQ + 4, :], float(P) ** -0.5, None, ALU.mult).then_inc(sem("ml_qk"), 1)
            dve.wait_ge(sem("ml_cols_mm"), 1)
            v.tensor_copy(gcol[:, :], ps[:, 0, 0:32]).then_inc(sem("ml_cols"), 1)
            dve.wait_ge(sem("ml_cols"), 2)
            fence()

            hh = region(R_VT, NT, NH, P)

            def weight_args(j):
                h, d = divmod(j, 2)
                w = xn[:, (j % 2) * 1024:(j % 2 + 1) * 1024].rearrange("p (s n) -> p s n", s=4)
                if j >= 2:
                    dve.wait_ge(sem("ml_pv"), j - 1)
                for s in range(4):
                    c = (d * 4 + s) * 4 + h
                    last = v.tensor_scalar(w[:, s, :], ps[:, 2 + 2 * d + h // 2, (h % 2) * T:(h % 2 + 1) * T], gcol[:, c:c + 1], 0.0,
                                           ALU.add, ALU.min)
                last.then_inc(sem("ml_w"), 1)

            def head_out(j):
                h, d = divmod(j, 2)
                dve.wait_ge(sem("ml_pv"), j + 1)
                den = ps[:, j % 2, :].rearrange("p (b n) -> p b n", b=NT)
                v.tensor_scalar(dn[:, 4:6], den[:, :, P], -1.0, None, ALU.mult)
                fence()
                for b in range(NT):
                    o = (d * 2 + b) * 4 + h
                    v.tensor_scalar(dn[:, b:b + 1], den[:, b, P:P + 1], dn[:, 4 + b:5 + b], en[:, o:o + 1], ALU.max, ALU.max)
                fence()
                v.reciprocal(dn[:, 2:4], dn[:, 0:2])
                fence()
                for b in range(NT):
                    if d == 0:
                        last = v.tensor_scalar(hh[:, b, h, :], den[:, b, 0:P], dn[:, 2 + b:3 + b], None, ALU.mult)
                    else:
                        last = v.scalar_tensor_tensor(hh[:, b, h, :], den[:, b, 0:P], dn[:, 2 + b:3 + b], hh[:, b, h, :],
                                                      ALU.mult, ALU.add)
                last.then_inc(sem("ml_h"), 1)

            weight_args(0)
            for j in range(8):
                h, d = divmod(j, 2)
                w = xn[:, (j % 2) * 1024:(j % 2 + 1) * 1024]
                dve.wait_ge(sem("ml_exp"), j + 1)
                v.tensor_tensor(w[:, 512:1024], w[:, 512:1024], const(("upto", "from")[d]), ALU.mult)
                dve.wait_ge(sem("ml_s"), h + 1)
                fence()
                v.tensor_tensor(w, w, all_ps[:, 3072:4096], ALU.mult).then_inc(sem("ml_p"), 1)
                if j + 1 < 8:
                    weight_args(j + 1)
                if j:
                    head_out(j - 1)
            head_out(7)
            fence()
            flat = region(R_VT, 8, P)
            sqs = xn[:, 0:1024].rearrange("p (a n) -> p a n", a=8)
            v.tensor_tensor(sqs, flat, flat, ALU.mult)
            fence()
            v.tensor_reduce(st[:, 0:8], sqs, AX.X, ALU.add)
            fence()
            v.tensor_scalar(st[:, 0:8], st[:, 0:8], 1.0 / P, EPS, ALU.mult, ALU.add).then_inc(sem("ms"), 1)
            dve.wait_ge(sem("std"), 3)
            v.reciprocal(st[:, 8:16], st[:, 8:16])
            fence()
            v.tensor_tensor(flat, flat, bc(st[:, 8:16].unsqueeze(2), P, 8, P), ALU.mult)
            fence()
            v.tensor_tensor(vt, vt, bc(mlnw[:, :].unsqueeze(1), P, NT, DBR), ALU.mult)
            dve.wait_ge(sem("o_gate"), 1)
            fence()
            v.tensor_tensor(vt, vt, og, ALU.mult).then_inc(sem("ml_y"), 1)
            gate_rows(0)

            for j in range(6):
                k, half = divmod(j, 2)
                mod_in(1, 3 + j, 4 + j, 4 * (j % 2) + 3)
                ada_sum(1, 4 + j)
                dve.wait_ge(used, USED["merge"][j])
                dve.wait_ge(sem("mg_sig"), j + 1)
                base = 4 * (j % 2) + 2
                proj = ps[:, base:base + 2, :].rearrange("p b (a n) -> p (b a) n", a=2)
                part = macc[:, half * 4:half * 4 + 4, :]
                if k == 0:
                    v.tensor_tensor(part, sgm[:, j % 2], proj, ALU.mult).then_inc(sem("merged"), 1)
                else:
                    v.tensor_tensor(sgm[:, j % 2], sgm[:, j % 2], proj, ALU.mult)
                    fence()
                    v.tensor_tensor(part, part, sgm[:, j % 2], ALU.add).then_inc(sem("merged"), 1)

            def out_add(stage):
                for half in range(2):
                    h = slice(half * 512, (half + 1) * 512)
                    if stage == "out1":
                        mod_in(1, 9 + half, 10 + half, 4 + half)
                        ada_sum(1, 10 + half)
                    dve.wait_ge(used, USED[stage][half])
                    v.tensor_tensor(xn2[:, :, h], ps[:, 2 * half:2 * half + 2, :], bc(grow[:, 0, h].unsqueeze(1), P, NT, 512), ALU.mult)
                    fence()
                    v.tensor_tensor(x[:, :, h], x[:, :, h], xn2[:, :, h], ALU.add)
                fence()

            def first_of(dst, val, m, n, eq, cs):
                v.tensor_scalar(eq, val, m, None, ALU.is_equal)
                fence()
                v.tensor_tensor_scan(cs, eq, const("zero")[:, 0:n], 0.0, ALU.add, ALU.add)
                fence()
                v.scalar_tensor_tensor(dst, cs, 1.0, eq, ALU.is_equal, ALU.mult)
                fence()

            def top2(b, val, n):
                r = rt[:, b, :]
                v.tensor_reduce(r[:, 32:33], val, AX.X, ALU.max)
                fence()
                first_of(r[:, 48:48 + n], val, r[:, 32:33], n, r[:, 64:64 + n], r[:, 72:72 + n])
                v.scalar_tensor_tensor(r[:, 80:80 + n], r[:, 48:48 + n], TAKEN, val, ALU.mult, ALU.add)
                fence()
                v.tensor_reduce(r[:, 33:34], r[:, 80:80 + n], AX.X, ALU.max)
                fence()
                first_of(r[:, 56:56 + n], r[:, 80:80 + n], r[:, 33:34], n, r[:, 64:64 + n], r[:, 72:72 + n])
                v.tensor_tensor(r[:, 30:31], r[:, 33:34], r[:, 32:33], ALU.subtract).then_inc(sem("rt_max"), 1)

            def top2_weights(b, n, scale, dst):
                r = rt[:, b, :]
                v.tensor_scalar(r[:, 34:35], r[:, 31:32], 1.0, None, ALU.add)
                fence()
                v.reciprocal(r[:, 35:36], r[:, 34:35])
                fence()
                if scale is not None:
                    v.tensor_tensor(r[:, 35:36], r[:, 35:36], scale, ALU.mult)
                    fence()
                v.tensor_tensor(r[:, 36:37], r[:, 35:36], r[:, 31:32], ALU.mult)
                fence()
                v.tensor_scalar(r[:, 64:64 + n], r[:, 48:48 + n], r[:, 35:36], None, ALU.mult)
                fence()
                v.scalar_tensor_tensor(dst, r[:, 56:56 + n], r[:, 36:37], r[:, 64:64 + n], ALU.mult, ALU.add)
                fence()

            def router1():
                dve.wait_ge(sem("router_mm"), 1)
                for b in range(NT):
                    r = rt[:, b, :]
                    v.tensor_tensor(r[:, 0:20], ps[:, 3, b * 32:b * 32 + 20], rb1[:, :], ALU.add)
                    fence()
                    v.tensor_reduce(r[:, 38:39], r[:, 0:4], AX.X, ALU.max)
                    fence()
                    v.tensor_scalar(r[:, 28:29], r[:, 38:39], -1.0, None, ALU.mult)
                    first_of(r[:, 40:44], r[:, 0:4], r[:, 38:39], 4, r[:, 64:68], r[:, 72:76])
                    v.tensor_scalar(r[:, 44:48], r[:, 4:8], r[:, 40:41], None, ALU.mult)
                    for g in range(1, 4):
                        fence()
                        v.scalar_tensor_tensor(r[:, 44:48], r[:, 4 + 4 * g:8 + 4 * g], r[:, 40 + g:41 + g], r[:, 44:48],
                                               ALU.mult, ALU.add)
                    fence()
                    top2(b, r[:, 44:48], 4)
                for b in range(NT):
                    last = v.tensor_copy(msk[:, b, 0:G1], rt[:, b, 40:44])
                last.then_inc(sem("masks"), 1)
                for b in range(NT):
                    r = rt[:, b, :]
                    dve.wait_ge(sem("rt_exp"), b + 1)
                    v.reciprocal(r[:, 39:40], r[:, 29:30])
                    fence()
                    top2_weights(b, 4, r[:, 39:40], r[:, 88:92])
                    for g in range(4):
                        v.tensor_scalar(comb[:, b, 4 * g:4 * g + 4], r[:, 88:92], r[:, 40 + g:41 + g], None, ALU.mult)

            def router2():
                dve.wait_ge(sem("router_mm"), 2)
                for b in range(NT):
                    v.tensor_copy(rt[:, b, 0:E2], ps[:, 3, b * 32:b * 32 + E2])
                fence()
                for b in range(NT):
                    top2(b, rt[:, b, 0:E2], E2)
                fence()
                for b in range(NT):
                    last = v.tensor_tensor(msk[:, b, :], rt[:, b, 48:56], rt[:, b, 56:64], ALU.add)
                last.then_inc(sem("masks"), 1)
                for b in range(NT):
                    dve.wait_ge(sem("rt_exp"), NT + b + 1)
                    top2_weights(b, E2, None, comb[:, b, 0:E2])

            ya = region(R_YA, NT, D)

            def chunk_act(n, cols=T):
                for hb in range(2):
                    dve.wait_ge(sem("gate_silu"), n - 1 + hb)
                    v.tensor_tensor(region(R_AT, 2, T)[:, hb, 0:cols], region(R_SG, 2, T)[:, hb, 0:cols],
                                    ps[:, hb, cols:2 * cols], ALU.mult).then_inc(sem("act_ready"), 1)

            def moe_act(name, i, jobs, experts, chunks, hidden):
                _, body, _ = PLAN[name]
                dve.wait_ge(sem("counted"), i + 1)
                count = ps[:, 3, 128:160].rearrange("p (b n) -> p b n", b=NT)[:, :, 0:jobs]
                v.tensor_reduce(rt[:, 0, 64:65], count[:, NT - 1, :], AX.X, ALU.max)
                v.tensor_tensor(slots[:, :, 0:jobs], count, msk[:, :, 0:jobs], ALU.mult)
                iota = region(R_IOTA, P)
                v.tensor_tensor_scan(iota, const("ones"), const("ones"), 0.0, ALU.mult, ALU.add)
                fence()
                v.tensor_scalar(flags[:, i:i + 1], rt[:, 0, 64:65], float(P), None, ALU.is_gt).then_inc(sem("flag"), 1)
                dve.wait_ge(sem("flag"), i + 1)
                over = dve.value_load(flags[P - 1:P, i:i + 1], min_val=0, max_val=1)
                sel, selT, ye, he = region(R_SE, NT, P), region(R_ST, T), region(R_YE, D), region(R_HE, KD, P)

                def select(j):
                    for b in range(NT):
                        last = v.tensor_scalar(sel[:, b, :], iota, slots[:, b, bass.ds(j, 1)], None, ALU.is_equal)
                    last.then_inc(sem(f"{name}_sel"), 1)

                def he_in(j):
                    dve.wait_ge(sem(f"{name}_gathered"), j + 1)
                    for k in range(KD):
                        last = v.tensor_scalar(he[:, k, :], ps[:, 4 + k // 4, (k % 4) * P:(k % 4 + 1) * P],
                                               ga[:, 8 + k:9 + k], mod[:, 24 + k:25 + k], ALU.mult, ALU.add)
                    last.then_inc(sem(f"{name}_he"), 1)

                def weights_in():
                    v.tensor_copy(wslot[:, 0:experts], ps[:, 6, 0:experts]).then_inc(sem(f"{name}_weights"), 1)

                def add(j):
                    dve.wait_ge(sem(f"{name}_spread"), j + 1)
                    v.tensor_tensor(ya, ya, ps[:, 4:8, :].rearrange("p (b a) n -> p b (a n)", b=NT), ALU.add
                                    ).then_inc(sem(f"{name}_added"), 1)

                with dve.If(over > 0):
                    v.memset(ya, 0.0).then_inc(sem(f"{name}_y_read"), 1)
                    with dve.Fori(0, jobs) as j:
                        for c in range(body):
                            chunk_act(j * (2 * body) + hidden + 2 * c + 2)
                            if c % chunks == chunks - 1:
                                fence()
                                dve.wait_ge(used, j * body + START[name] + c + 1)
                                e = j * experts + c // chunks
                                for b in range(NT):
                                    last = v.scalar_tensor_tensor(ya[:, b, :], all_ps[:, 2048 + b * 1024:3072 + b * 1024],
                                                                  comb[:, b, bass.ds(e, 1)], ya[:, b, :], ALU.mult, ALU.add)
                                last.then_inc(sem(f"{name}_y_read"), 1)
                    fence()
                    ffn_add(ya).then_inc(sem("block_done"), 1)
                with dve.Else():
                    v.memset(ya, 0.0)
                    v.memset(selT, 0.0).then_inc(sem(f"{name}_selT"), 1)
                    v.memset(ye, 0.0).then_inc(sem(f"{name}_ye"), 1)
                    select(0)
                    he_in(0)
                    weights_in()
                    with dve.Fori(0, jobs) as j:
                        for c in range(body):
                            chunk_act(j * (2 * body) + hidden + 2 * c + 2, P)
                            if c == body - 1:
                                he_in(j + 1)
                            if c % chunks == chunks - 1:
                                x_ = c // chunks
                                fence()
                                if c == 0:
                                    dve.wait_ge(sem(f"{name}_spread"), j + 1)
                                dve.wait_ge(used, j * body + START[name] + c + 1)
                                if x_ == 0:
                                    v.tensor_scalar(ye, all_ps[:, 1024:2048], wslot[:, 0:1], None, ALU.mult
                                                    ).then_inc(sem(f"{name}_ye"), 1)
                                else:
                                    v.scalar_tensor_tensor(ye, all_ps[:, 1024:2048], wslot[:, x_:x_ + 1], ye, ALU.mult, ALU.add
                                                           ).then_inc(sem(f"{name}_ye"), 1)
                            if c == 0:
                                add(j)
                            elif c == 1:
                                dve.wait_ge(sem(f"{name}_placed"), j + 1)
                                v.tensor_copy(selT, ps[:, 7, 0:T]).then_inc(sem(f"{name}_selT"), 1)
                                select(j + 1)
                        fence()
                        weights_in()
                    ffn_add(ya)
                    fence()
                    dve.wait_ge(sem(f"{name}_spread"), jobs + 1)
                    ffn_add(ps[:, 4:8, :].rearrange("p (b a) n -> p b (a n)", b=NT)).then_inc(sem("block_done"), 1)
                fence()

            def ffn_add(src):
                v.tensor_tensor(xn2, src, bc(grow[:, 1, :].unsqueeze(1), P, NT, D), ALU.mult)
                fence()
                return v.tensor_tensor(x[:, :, :], x[:, :, :], xn2, ALU.add)

            out_add("out1")
            mod_in(1, NA - 1, NA, 4)
            norm(4, x, 3, hT, ga[:, 8:16], mod[:, 24:32])
            router1()
            moe_act("moe1", 0, G1, 4, 1, 0)
            hidden = 2 * E1
            rstd(5, x)
            dve.wait_ge(sem("late_in"), 32)
            for b in range(NT):
                v.scalar_tensor_tensor(x[:, b, :], x[:, b, :], st[:, 4 + b:5 + b], late[:, 0:D], ALU.mult, ALU.mult)
            fence()

            for l in range(2):
                ada_first(l + 1, f"ga{l}")
                ada_rest(l + 1, f"gf{l}")
                norm(6 + 3 * l, x, 4 + 2 * l, hT, ga, mod)
                gate_rows(l + 1)
                pj = region(R_PJ, NT, D_IN)
                spans = ((O_QA, A_H + 1, HD, 8, 0), (O_QI, 5, HD, 8, 0), (O_QB, 16, 32, 4, 8), (O_QC, 2 * C_H, HD, 8, 0))
                at = [R_SM + b * 1024 for b in range(NT)]
                for off, heads, w, half, f in spans:
                    end = off + heads * w
                    dve.wait_ge(sem("pj_in"), 6 * l + next(j for j, (c, n) in enumerate(IN2_COLS) if c + n >= end) + 1)
                    n, parts = heads * half, []
                    for b in range(NT):
                        heads_ = pj[:, b, off:end].rearrange("p (h n) -> p h n", n=w)
                        x1, x2 = heads_[:, :, 0:half], heads_[:, :, half:2 * half]
                        c_, s_ = (bc(t[:, b, f:f + half].unsqueeze(1), P, heads, half) for t in (cosn, sinn))
                        t_ = [region(at[b] + i * n, heads, half) for i in range(4)]
                        at[b] += 4 * n
                        for t, a_, w_ in zip(t_, (x1, x2, x2, x1), (c_, s_, c_, s_)):
                            v.tensor_tensor(t, a_, w_, ALU.mult)
                        parts.append((x1, x2, t_))
                    fence()
                    for x1, x2, t_ in parts:
                        v.tensor_tensor(x1, t_[0], t_[1], ALU.subtract)
                        last = v.tensor_tensor(x2, t_[2], t_[3], ALU.add)
                dve.wait_ge(sem("pj_in"), 6 * (l + 1))
                for b in range(NT):
                    last = v.tensor_scalar(wix[:, b, :], pj[:, b, O_WI:O_WI + 4], 0.5 * 0.125, None, ALU.mult)
                last.then_inc(sem("roped"), 1)
                fence()
                dve.wait_ge(sem("fm_in"), -(-NFM // 4) * (l + 1))
                fm = region(R_FM, NFM, T)
                for i in range(2 * B_H):
                    last = v.tensor_scalar(hT[:, i, :], fm[:, FM_QB + i // 4, :], const("quarter")[:, i % 4:i % 4 + 1], None, ALU.mult)
                last.then_inc(sem("qb_masked"), 1)

                causal = const2("causal")
                sel = region(R_SEL, 2, T)
                rel = region(R_SM, 4, T)
                buf = (region(R_SM + 4 * T, 2, T), region(R_IX, 2, T))
                sc = [[buf[qb][:, i, 0:(qb + 1) * P] for i in range(2)] for qb in range(NT)]
                tops = (top[:, :], rt[:, 0, 0:8])
                for qb in range(NT):
                    ns = (qb + 1) * P
                    dve.wait_ge(sem("ix_in"), NT * l + qb + 1)
                    v.tensor_scalar(sc[qb][0], rel[:, 0, 0:ns], wix[:, qb, 0:1], None, ALU.mult)
                    for h in range(1, 4):
                        fence()
                        last = v.scalar_tensor_tensor(sc[qb][0], rel[:, PAIRS[4][h], 0:ns], wix[:, qb, h:h + 1], sc[qb][0],
                                                      ALU.mult, ALU.add)
                    last.then_inc(sem("ix_used"), 1)
                    fence()
                    v.tensor_tensor(sc[qb][0], sc[qb][0], causal[:, qb, 0:ns], ALU.add)
                for i in range(TOPK // 8):
                    fence()
                    for qb in range(NT):
                        v.max(tops[qb], sc[qb][i % 2])
                    fence()
                    for qb in range(NT):
                        v.match_replace(sc[qb][(i + 1) % 2], tops[qb], sc[qb][i % 2], TAKEN)
                fence()
                for qb in range(NT):
                    v.tensor_scalar(sc[qb][1], sc[qb][0], TAKEN / 1.5, MASKED, ALU.is_gt, ALU.mult)
                fence()
                for qb in range(NT):
                    ns = (qb + 1) * P
                    v.tensor_tensor(sel[:, qb, 0:ns], sc[qb][1], causal[:, qb, 0:ns], ALU.add)
                fence()

                sm = region(R_SM, 2, 4, T)

                def mask_scores(j):
                    br, h0, n, qb = JOBS[j]
                    ns = (qb + 1) * P
                    dve.wait_ge(sem("s_mm"), len(JOBS) * l + j + 1)
                    if j >= 2:
                        dve.wait_ge(sem("pt_mm"), len(JOBS) * l + j - 1)
                    scale = float(32 if br == "B" else HD) ** -0.5
                    mask = (sel if br == "A" else causal)[:, qb, 0:ns]
                    bank = 2 * (j % 2)
                    s_ = ps[:, bank:bank + 2, :].rearrange("p b (a n) -> p (b a) n", a=2)
                    s_ = s_[:, 0:n, 0:ns] if br == "B" or n == 4 else s_[:, 0:4:2, 0:ns]
                    v.scalar_tensor_tensor(sm[:, j % 2, 0:n, 0:ns], s_, scale, bc(mask.unsqueeze(1), P, n, ns), ALU.mult, ALU.add
                                           ).then_inc(sem("masked"), 1)
                    fence()
                    v.tensor_reduce(amx[:, j % 2, 0:n], sm[:, j % 2, 0:n, 0:ns], AX.X, ALU.max)
                    fence()
                    v.tensor_scalar(amx[:, j % 2, 0:n], amx[:, j % 2, 0:n], -1.0, None, ALU.mult).then_inc(sem("row_max"), 1)

                def probs(j):
                    br, h0, n, qb = JOBS[j]
                    ns = (qb + 1) * P
                    fence()
                    dve.wait_ge(sem("exped"), len(JOBS) * l + j + 1)
                    last = v.reciprocal(ars[:, j % 2, 0:n], asum[:, j % 2, 0:n])
                    if br == "B":
                        fence()
                        for i in range(0, n, 2):
                            v.tensor_scalar(sm[:, j % 2, i + 1, 0:ns], sm[:, j % 2, i + 1, 0:ns], ars[:, j % 2, i + 1:i + 2],
                                            lamt[:, 4 + l:5 + l], ALU.mult, ALU.mult)
                        fence()
                        for i in range(0, n, 2):
                            last = v.scalar_tensor_tensor(sm[:, j % 2, i, 0:ns], sm[:, j % 2, i, 0:ns], ars[:, j % 2, i:i + 1],
                                                          sm[:, j % 2, i + 1, 0:ns], ALU.mult, ALU.subtract)
                    last.then_inc(sem("probs"), 1)

                def outputs_in(j):
                    br, h0, n, qb = JOBS[j]
                    dve.wait_ge(sem("o_mm"), len(JOBS) * l + j + 1)
                    heads = n // 2 if br == "B" else n
                    c = {"A": h0 * HD, "B": A_H * HD + h0 // 2 * HD, "C": (A_H + B_H + h0) * HD}[br]
                    dst = xn2[:, qb, c:c + heads * HD].rearrange("p (h n) -> p h n", n=HD)
                    src = ps[:, 6 + j % 2, 0:heads * HD].rearrange("p (h n) -> p h n", n=HD)
                    if br == "B":
                        last = v.tensor_copy(dst, src)
                    elif n == 2:
                        last = v.tensor_tensor(dst, src, bc(ars[:, j % 2, 0:n].unsqueeze(2), P, n, HD), ALU.mult)
                    else:
                        last = v.tensor_tensor(dst.rearrange("p (a b) n -> p b a n", a=2), src.rearrange("p (b a) n -> p b a n", b=2),
                                               bc(ars[:, j % 2, 0:4].rearrange("p (b a) -> p b a", b=2).unsqueeze(3), P, 2, 2, HD),
                                               ALU.mult)
                    last.then_inc(sem("o_in"), 1)

                mask_scores(0)
                for j in range(len(JOBS)):
                    if j + 1 < len(JOBS):
                        mask_scores(j + 1)
                    probs(j)
                    if j:
                        outputs_in(j - 1)
                outputs_in(len(JOBS) - 1)
                fence()
                yb = xn2[:, :, A_H * HD:(A_H + B_H) * HD]
                sq2 = region(R_SM, NT, B_H * HD)
                v.tensor_tensor(sq2, yb, yb, ALU.mult)
                fence()
                v.tensor_reduce(st[:, 0:8], region(R_SM, 8, HD), AX.X, ALU.add)
                fence()
                v.tensor_scalar(st[:, 0:8], st[:, 0:8], 1.0 / HD, SUB_EPS, ALU.mult, ALU.add).then_inc(sem("ms"), 1)
                dve.wait_ge(sem("std"), 7 + 3 * l)
                v.reciprocal(st[:, 8:16], st[:, 8:16])
                fence()
                for b in range(NT):
                    yb_ = yb[:, b, :].rearrange("p (h n) -> p h n", n=HD)
                    v.tensor_tensor(yb_, yb_, bc(st[:, 8 + 4 * b:12 + 4 * b].unsqueeze(2), P, B_H, HD), ALU.mult)
                fence()
                for b in range(NT):
                    yb_ = yb[:, b, :].rearrange("p (h n) -> p h n", n=HD)
                    last = v.scalar_tensor_tensor(yb_, yb_, 1.0 - LAM_INIT[l], bc(subln[:, l, :].unsqueeze(1), P, B_H, HD),
                                                  ALU.mult, ALU.mult)
                last.then_inc(sem("y_rows"), 1)

                if l == 0:
                    ada_sum(2, 0)
                out_add(f"out2_{l}")
                norm(8 + 3 * l, x, 5 + 2 * l, hT, ga[:, 8:16], mod[:, 24:32])
                if l == 0:
                    for c in range(NCH):
                        chunk_act(hidden + 2 * c + 2)
                        ada_sum(2, c + 1)
                    mod_in(2, 0, NA, 2)
                    hidden += 2 * NCH
                    ffn_add(ps[:, 4:8, :].rearrange("p (b a) n -> p b (a n)", b=NT)).then_inc(sem("block_done"), 1)
                    fence()
            router2()
            moe_act("moe2", 1, E2, 1, NCH, hidden)
            rstd(12, x)
            dve.wait_ge(sem("late_in"), 32)
            for b in range(NT):
                v.scalar_tensor_tensor(xn2[:, b, :], x[:, b, :], st[:, 4 + b:5 + b], late[:, D:2 * D], ALU.mult, ALU.mult
                                       ).then_inc(sem("y_final"), 1)


_INS = ["x", "c", "ctx", "c_ctx", "ada_w", "ada_b", "norm1_w", "norm2_w", "w_in", "b_in", "hy_conv_w", "hy_conv_b", "hy_f_w1",
        "hy_f_b1", "hy_f_w2", "hy_f_b2", "hy_f_w3", "hy_f_freq", "hy_decay", "hy_skip", "ml_conv_w", "ml_conv_b",
        "ml_norm_w", "w_branch", "w_out", "moe_rg_w", "moe_rg_b", "moe_re_w", "moe_re_b", "moe_w_gate", "moe_w_up",
        "moe_w_down", "norm_f_w", "c_2", "positions_2", "w_in_2", "w_out_2", "diff_lambda_2", "diff_subln_2",
        "w_ada_2", "b_ada_2", "g_attn_2", "g_ffn_2", "w_ff_gate_2", "w_ff_up_2", "w_ff_down_2", "w_router_2",
        "w_exp_gate_2", "w_exp_up_2", "w_exp_down_2", "g_final_2"]


def kernel(**inputs):
    import concourse.bacc as bacc
    from concourse.bass_utils import run_bass_kernel_spmd

    nc = bacc.Bacc("TRN2", target_bir_lowering=False, num_devices=1)
    arrays, aps = {}, {}
    for name in _INS:
        a = np.ascontiguousarray(inputs[name])
        arrays[f"in_{name}"] = a
        aps[name] = nc.dram_tensor(f"in_{name}", a.shape, mybir.dt.from_np(a.dtype), kind="ExternalInput").ap()
    aps["b_in_gate"] = aps["b_in"][:, GATE0:GATE0 + 3 * D]
    arrays["in_tables"] = shape_constants()
    tables = nc.dram_tensor("in_tables", (P, NCONST), F32, kind="ExternalInput").ap()
    out = nc.dram_tensor("out_y", (1, T, D), F32, kind="ExternalOutput").ap()
    build(nc, aps, tables, out)
    got = run_bass_kernel_spmd(nc, [arrays], core_ids=[0])
    return got.results[0]["out_y"]
```
